# Optimizing a Trainium2 kernel written in Bass

```python
import math
import jax, jax.numpy as jnp
from jax import lax
import numpy as np

D_MODEL = 1024
BATCH = 1
SEQ = 256
DEPTH = 2

N_HEADS = 16
HEAD_DIM = D_MODEL // N_HEADS
NSA_KV_HEADS = 4
NSA_GROUP = N_HEADS // NSA_KV_HEADS
CMP_BLOCK = 32
CMP_STRIDE = 16
CMP_HIDDEN = 256
SEL_BLOCK = 64
SEL_TOPK = 16
WINDOW = 512
NSA_QBLOCK = 64
FOX_QBLOCK = 128
D_FF = int(round(8 * D_MODEL / 3 / 256)) * 256
N_BUCKETS = 32
MAX_DISTANCE = 128
N_A_LAYERS = DEPTH // 2
N_B_LAYERS = DEPTH - N_A_LAYERS
HD = N_HEADS * HEAD_DIM
KVD = NSA_KV_HEADS * HEAD_DIM
NSA_IN = HD + 6 * KVD + 3 * N_HEADS
EPS = 1e-6
NEG_INF = -1e30
SEL_FORCE = 1e4

kernel_name = 'yoco_nsa_fox_macaron_trunk'

def rms_norm(x, g):
    xf = x.astype(jnp.float32)
    y = xf * lax.rsqrt(jnp.mean(xf * xf, axis=-1, keepdims=True) + EPS)
    return (y * g.astype(jnp.float32)).astype(x.dtype)

def swiglu(h, w_in, w_out):
    a, b = jnp.split(h @ w_in, 2, axis=-1)
    return (jax.nn.silu(a) * b) @ w_out

def t5_bucket(dist):
    dist = jnp.maximum(dist, 0)
    max_exact = N_BUCKETS // 2
    scaled = jnp.log(jnp.maximum(dist, 1).astype(jnp.float32) / max_exact) / math.log(MAX_DISTANCE / max_exact)
    large = jnp.minimum(max_exact + (scaled * (N_BUCKETS - max_exact)).astype(jnp.int32), N_BUCKETS - 1)
    return jnp.where(dist < max_exact, dist, large).astype(jnp.int32)

def masked_softmax(logits, mask):
    p = jax.nn.softmax(jnp.where(mask, logits, NEG_INF), axis=-1)
    return jnp.where(mask, p, 0.0)

def compress_blocks(x_kv, pos, w1, w2):
    B, T, G, dh = x_kv.shape
    n_cmp = (T - CMP_BLOCK) // CMP_STRIDE + 1
    idx = np.arange(n_cmp)[:, None] * CMP_STRIDE + np.arange(CMP_BLOCK)[None, :]
    blocks = x_kv[:, idx] + pos[None, None, :, None, :]
    flat = jnp.moveaxis(blocks, 3, 2).reshape(B, n_cmp, G, CMP_BLOCK * dh)
    return jax.nn.silu(flat @ w1) @ w2

def nsa_mixer(h, w_in, cmp_pos, cmp_w1, cmp_w2, rel_bias, w_out):
    B, T, _ = h.shape
    G, R, dh, QB = NSA_KV_HEADS, NSA_GROUP, HEAD_DIM, NSA_QBLOCK
    scale = dh ** -0.5
    q, kc, vc, ks, vs, kw, vw, gl = jnp.split(h @ w_in, [HD + i * KVD for i in range(7)], axis=-1)
    q = q.reshape(B, T, G, R, dh)
    gl = gl.reshape(B, T, G, R, 3)
    kc, vc, ks, vs, kw, vw = (a.reshape(B, T, G, dh) for a in (kc, vc, ks, vs, kw, vw))

    k_cmp = compress_blocks(kc, cmp_pos[0], cmp_w1[0], cmp_w2[0])
    v_cmp = compress_blocks(vc, cmp_pos[1], cmp_w1[1], cmp_w2[1])
    n_cmp = k_cmp.shape[1]
    cmp_start = np.arange(n_cmp) * CMP_STRIDE
    cmp_end = jnp.asarray(cmp_start + CMP_BLOCK - 1)

    n_sel = T // SEL_BLOCK
    k_sel = min(SEL_TOPK, n_sel)
    sel_start = np.arange(n_sel) * SEL_BLOCK
    overlap = jnp.asarray(((cmp_start[:, None] < sel_start[None, :] + SEL_BLOCK)
                           & (cmp_start[:, None] + CMP_BLOCK > sel_start[None, :])).astype(np.float32))
    ks_blk = ks.reshape(B, n_sel, SEL_BLOCK, G, dh).transpose(0, 3, 1, 2, 4)
    vs_blk = vs.reshape(B, n_sel, SEL_BLOCK, G, dh).transpose(0, 3, 1, 2, 4)

    kw_pad = jnp.pad(kw, ((0, 0), (WINDOW, 0), (0, 0), (0, 0)))
    vw_pad = jnp.pad(vw, ((0, 0), (WINDOW, 0), (0, 0), (0, 0)))
    L_win = WINDOW + QB

    tbl_group = rel_bias.reshape(N_BUCKETS, G, R)
    gather_blocks = jax.vmap(jax.vmap(lambda blk, ix: blk[ix]))
    group_bias = jax.vmap(lambda tb, bk: tb[bk], in_axes=(1, 1), out_axes=1)
    blk_id = jnp.arange(n_sel)
    within = jnp.arange(SEL_BLOCK)

    def head_bias(bucket):
        return jnp.moveaxis(rel_bias[bucket], -1, 0).reshape(G, R, *bucket.shape)

    def chunk(i):
        t0 = i * QB
        tpos = t0 + jnp.arange(QB)
        qc = lax.dynamic_slice_in_dim(q, t0, QB, axis=1)
        gc = jax.nn.sigmoid(lax.dynamic_slice_in_dim(gl, t0, QB, axis=1).astype(jnp.float32))
        dist_c = tpos[:, None] - cmp_end[None, :]
        s_c = jnp.einsum('bqgrd,bngd->bgrqn', qc, k_cmp).astype(jnp.float32) * scale + head_bias(t5_bucket(dist_c))
        p_c = masked_softmax(s_c, dist_c >= 0)
        o_c = jnp.einsum('bgrqn,bngd->bqgrd', p_c.astype(v_cmp.dtype), v_cmp)
        imp = jnp.einsum('bgrqn,ns->bgqs', p_c, overlap)
        cur = (tpos // SEL_BLOCK)[:, None]
        forced = (blk_id == 0) | (blk_id == cur) | (blk_id == cur - 1)
        score = jnp.where(blk_id > cur, -SEL_FORCE, imp + jnp.where(forced, SEL_FORCE, 0.0))
        _, sel = lax.top_k(score, k_sel)
        k_g = gather_blocks(ks_blk, sel).reshape(B, G, QB, k_sel * SEL_BLOCK, dh)
        v_g = gather_blocks(vs_blk, sel).reshape(B, G, QB, k_sel * SEL_BLOCK, dh)
        spos = (sel[..., None] * SEL_BLOCK + within).reshape(B, G, QB, k_sel * SEL_BLOCK)
        dist_s = tpos[:, None] - spos
        bias_s = jnp.moveaxis(group_bias(tbl_group, t5_bucket(dist_s)), -1, 2)
        s_s = jnp.einsum('bqgrd,bgqld->bgrql', qc, k_g).astype(jnp.float32) * scale + bias_s
        p_s = masked_softmax(s_s, (dist_s >= 0)[:, :, None])
        o_s = jnp.einsum('bgrql,bgqld->bqgrd', p_s.astype(v_g.dtype), v_g)
        k_w = lax.dynamic_slice_in_dim(kw_pad, t0, L_win, axis=1)
        v_w = lax.dynamic_slice_in_dim(vw_pad, t0, L_win, axis=1)
        kpos = t0 - WINDOW + jnp.arange(L_win)
        dist_w = tpos[:, None] - kpos[None, :]
        mask_w = (dist_w >= 0) & (dist_w < WINDOW) & (kpos >= 0)[None, :]
        s_w = jnp.einsum('bqgrd,blgd->bgrql', qc, k_w).astype(jnp.float32) * scale + head_bias(t5_bucket(dist_w))
        p_w = masked_softmax(s_w, mask_w)
        o_w = jnp.einsum('bgrql,blgd->bqgrd', p_w.astype(v_w.dtype), v_w)
        gc = gc.astype(o_c.dtype)
        o = gc[..., 0:1] * o_c + gc[..., 1:2] * o_s + gc[..., 2:3] * o_w
        return o.reshape(B, QB, HD)

    out = lax.map(chunk, jnp.arange(T // QB))
    return jnp.moveaxis(out, 0, 1).reshape(B, T, HD) @ w_out

def shared_kv(x, g, w_kvf, b_f):
    B, T, _ = x.shape
    k, v, fl = jnp.split(rms_norm(x, g) @ w_kvf, [HD, 2 * HD], axis=-1)
    log_f = jax.nn.log_sigmoid(fl.astype(jnp.float32) + b_f.astype(jnp.float32))
    c = jnp.cumsum(log_f, axis=1)
    return (k.reshape(B, T, N_HEADS, HEAD_DIM), v.reshape(B, T, N_HEADS, HEAD_DIM), c)

def fox_mixer(h, w_q, k, v, c_cum, w_out):
    B, T, _ = h.shape
    QB = FOX_QBLOCK
    scale = HEAD_DIM ** -0.5
    q = (h @ w_q).reshape(B, T, N_HEADS, HEAD_DIM)
    cT = jnp.transpose(c_cum, (0, 2, 1))
    kpos = jnp.arange(T)

    def chunk(i):
        t0 = i * QB
        tpos = t0 + jnp.arange(QB)
        qc = lax.dynamic_slice_in_dim(q, t0, QB, axis=1)
        cq = lax.dynamic_slice_in_dim(cT, t0, QB, axis=2)
        s = jnp.einsum('bqhd,bkhd->bhqk', qc, k).astype(jnp.float32) * scale + cq[..., None] - cT[:, :, None, :]
        p = masked_softmax(s, kpos[None, :] <= tpos[:, None])
        o = jnp.einsum('bhqk,bkhd->bqhd', p.astype(v.dtype), v)
        return o.reshape(B, QB, HD)

    out = lax.map(chunk, jnp.arange(T // QB))
    return jnp.moveaxis(out, 0, 1).reshape(B, T, HD) @ w_out

def setup_inputs(seed: int = 0) -> dict:
    key = jax.random.key(seed)
    ks = jax.random.split(key, 17)
    nrm = jax.random.normal
    f32 = jnp.float32
    x = nrm(ks[0], (BATCH, SEQ, D_MODEL), f32)
    norm_g = 1.0 + 0.05 * nrm(ks[1], (DEPTH, 3, D_MODEL), f32)
    ffn_w_in = nrm(ks[2], (DEPTH, 2, D_MODEL, 2 * D_FF), f32) * D_MODEL ** -0.5
    ffn_w_out = nrm(ks[3], (DEPTH, 2, D_FF, D_MODEL), f32) * D_FF ** -0.5
    nsa_w_in = nrm(ks[4], (N_A_LAYERS, D_MODEL, NSA_IN), f32) * D_MODEL ** -0.5
    nsa_cmp_pos = 0.5 * nrm(ks[5], (N_A_LAYERS, 2, CMP_BLOCK, HEAD_DIM), f32)
    nsa_cmp_w1 = nrm(ks[6], (N_A_LAYERS, 2, CMP_BLOCK * HEAD_DIM, CMP_HIDDEN), f32) * (CMP_BLOCK * HEAD_DIM) ** -0.5
    nsa_cmp_w2 = nrm(ks[7], (N_A_LAYERS, 2, CMP_HIDDEN, HEAD_DIM), f32) * CMP_HIDDEN ** -0.5
    nsa_w_out = nrm(ks[8], (N_A_LAYERS, HD, D_MODEL), f32) * HD ** -0.5
    rel_bias = 0.5 * nrm(ks[9], (N_BUCKETS, N_HEADS), f32)
    kv_norm_g = 1.0 + 0.05 * nrm(ks[10], (D_MODEL,), f32)
    fox_w_kvf = jnp.concatenate([nrm(ks[11], (D_MODEL, 2 * HD), f32) * D_MODEL ** -0.5,
                                 0.1 * nrm(ks[12], (D_MODEL, N_HEADS), f32) * D_MODEL ** -0.5], axis=1)
    fox_b_f = 4.0 + 0.5 * nrm(ks[13], (N_HEADS,), f32)
    fox_w_q = nrm(ks[14], (N_B_LAYERS, D_MODEL, HD), f32) * D_MODEL ** -0.5
    fox_w_out = nrm(ks[15], (N_B_LAYERS, HD, D_MODEL), f32) * HD ** -0.5
    final_g = 1.0 + 0.05 * nrm(ks[16], (D_MODEL,), f32)
    return {'x': x, 'norm_g': norm_g, 'ffn_w_in': ffn_w_in, 'ffn_w_out': ffn_w_out,
            'nsa_w_in': nsa_w_in, 'nsa_cmp_pos': nsa_cmp_pos, 'nsa_cmp_w1': nsa_cmp_w1,
            'nsa_cmp_w2': nsa_cmp_w2, 'nsa_w_out': nsa_w_out, 'rel_bias': rel_bias,
            'kv_norm_g': kv_norm_g, 'fox_w_kvf': fox_w_kvf, 'fox_b_f': fox_b_f,
            'fox_w_q': fox_w_q, 'fox_w_out': fox_w_out, 'final_g': final_g}

def reference(x, norm_g, ffn_w_in, ffn_w_out, nsa_w_in, nsa_cmp_pos, nsa_cmp_w1, nsa_cmp_w2,
              nsa_w_out, rel_bias, kv_norm_g, fox_w_kvf, fox_b_f, fox_w_q, fox_w_out, final_g):
    k_sh = v_sh = c_sh = None
    for l in range(DEPTH):
        if l == N_A_LAYERS:
            k_sh, v_sh, c_sh = shared_kv(x, kv_norm_g, fox_w_kvf, fox_b_f)
        x = x + 0.5 * swiglu(rms_norm(x, norm_g[l, 0]), ffn_w_in[l, 0], ffn_w_out[l, 0])
        h = rms_norm(x, norm_g[l, 1])
        if l < N_A_LAYERS:
            x = x + nsa_mixer(h, nsa_w_in[l], nsa_cmp_pos[l], nsa_cmp_w1[l], nsa_cmp_w2[l], rel_bias, nsa_w_out[l])
        else:
            j = l - N_A_LAYERS
            x = x + fox_mixer(h, fox_w_q[j], k_sh, v_sh, c_sh, fox_w_out[j])
        x = x + 0.5 * swiglu(rms_norm(x, norm_g[l, 2]), ffn_w_in[l, 1], ffn_w_out[l, 1])
    return rms_norm(x, final_g)


_drawn_inputs = setup_inputs


def setup_inputs(seed=0):
    import zlib

    import numpy as np

    out = dict(_drawn_inputs(seed))
    spreads = {}
    factors = {'kv_norm_g': 4.158}
    for name, (base, spread) in spreads.items():
        noise = np.random.default_rng([zlib.crc32(name.encode()), seed]).standard_normal(out[name].shape)
        drawn = base * np.exp(spread * noise) if base else spread * noise
        out[name] = __import__('jax').numpy.asarray(drawn.astype(out[name].dtype))
    for name, factor in factors.items():
        out[name] = (out[name] * factor).astype(out[name].dtype)
    return out
```

```python
import math
from contextlib import ExitStack

import numpy as np
import concourse.bass as bass
from concourse import mybir

F32 = mybir.dt.float32
F32R = mybir.dt.float32r
BF16 = mybir.dt.bfloat16
ALU = mybir.AluOpType
ACT = mybir.ActivationFunctionType
AX = mybir.AxisListType

P = 128
SEQ, D = 256, 1024
NT = SEQ // P
KT = D // P
H, DH = 16, 64
G = 4
KVD = G * DH
DFF = 2816
FC = 256
NJ = DFF // FC
CMP_BLOCK, CMP_STRIDE, CMP_HIDDEN = 32, 16, 256
NCMP = (SEQ - CMP_BLOCK) // CMP_STRIDE + 1
GN = G * NCMP
HN = 8 * NCMP
NB, MAXD = 32, 128
NG = 3 * H
EPS = 1e-6
NEG = -1e30
SCALE = DH ** -0.5
CW = 512
UNIT = 4 * CW
RING = 3

FFN_UNITS = 3 * NJ
U_FFN0 = 0
U_NSA = U_FFN0 + FFN_UNITS
U_CMP = U_NSA + 10
U_NSA_OUT = U_CMP + 4
U_FFN1 = U_NSA_OUT + 4
U_KV = U_FFN1 + FFN_UNITS
U_FFN2 = U_KV + 8
U_FOXQ = U_FFN2 + FFN_UNITS
U_FOX_OUT = U_FOXQ + 4
U_FFN3 = U_FOX_OUT + 4
U_END = U_FFN3 + FFN_UNITS
U_FFN = [U_FFN0, U_FFN1, U_FFN2, U_FFN3]

TURNS = ["ffn0", "nsa", "nsa_o", "ffn1", "kv", "ffn2", "fox", "fox_o", "ffn3"]
PIECES = {t: 4 if t.endswith("_o") else KT for t in TURNS}
PIECE0 = {t: sum(PIECES[s] for s in TURNS[:i]) for i, t in enumerate(TURNS)}
GAIN = {"ffn0": 0, "nsa": 1, "ffn1": 2, "ffn2": 3, "fox": 4, "ffn3": 5, "kv": 6}
NORMS = ["ffn0", "nsa", "ffn1", "kv", "fox", "ffn3", "final"]
ADDS = ["ffn0", "nsa", "ffn1", "ffn2", "fox", "ffn3"]


def bucket_starts():
    dist = np.arange(SEQ)
    exact = NB // 2
    scaled = np.log(np.maximum(dist, 1).astype(np.float32) / np.float32(exact)).astype(np.float32)
    scaled = scaled / np.float32(math.log(MAXD / exact))
    large = np.minimum(exact + (scaled * np.float32(NB - exact)).astype(np.int32), NB - 1)
    bucket = np.where(dist < exact, dist, large)
    return [int(np.argmax(bucket == b)) for b in range(NB)] + [SEQ]


def yoco_trunk(nc, x, norm_g, ffn_w_in, ffn_w_out, nsa_w_in, nsa_cmp_pos, nsa_cmp_w1, nsa_cmp_w2,
               nsa_w_out, rel_bias, kv_norm_g, fox_w_kvf, fox_b_f, fox_w_q, fox_w_out, final_g, out):
    ctx = ExitStack()
    with ctx:
        def sb(name, shape, dt=F32):
            return ctx.enter_context(nc.sbuf_tensor(name, shape, dt))

        def ps(name):
            return ctx.enter_context(nc.psum_tensor(name, [P, 512], F32))

        def sem(name):
            return ctx.enter_context(nc.semaphore(name))

        raw = [sb(f"raw{s}", [P, UNIT]) for s in range(RING)]
        whi = [sb(f"whi{s}", [P, UNIT], F32R) for s in range(RING)]
        wlo = [sb(f"wlo{s}", [P, UNIT], F32R) for s in range(RING)]
        xs = sb("xs", [P, NT, D])
        xn = sb("xn", [P, NT, D])
        thi = sb("thi", [P, KT, SEQ], F32R)
        tlo = sb("tlo", [P, KT, SEQ], F32R)
        ghi = sb("ghi", [P, 2, SEQ], F32R)
        glo = sb("glo", [P, 2, SEQ], F32R)
        sa = sb("sa", [P, NT, FC])
        gg = sb("gg", [P, NT, FC])
        qT = sb("qT", [P, H // 2, SEQ])
        nat = sb("nat", [P, 5120])
        kblk = sb("kblk", [P, 2, 8, SEQ])
        bias = sb("bias", [P, H, SEQ])
        work = sb("work", [P, 3072])
        fhi = sb("fhi", [P, 16, GN], F32R)
        flo = sb("flo", [P, 16, GN], F32R)
        low = sb("low", [P, 2048])
        gate_w = sb("gate_w", [P, KT, NG])
        fl_w = sb("fl_w", [P, KT, H])
        w2k = sb("w2k", [P, 2, 2, DH])
        w2v = sb("w2v", [P, 2, DH])
        ident = sb("ident", [P, P])
        cmask = sb("cmask", [P, P])
        gains = sb("gains", [P, 56])
        posT = sb("posT", [P, 32])
        tbT = sb("tbT", [H, NB])
        cmask01 = sb("cmask01", [P, NT, NCMP])
        blkmask = sb("blkmask", [HN, 8])
        kcb = sb("kcb", [P, G, 2, NCMP])
        zeros = sb("zeros", [32, P], BF16)
        epst = sb("epst", [P, 1])
        ss = sb("ss", [P, 2 * NT])
        rstd = sb("rstd", [P, NT])
        mx = sb("mx", [P, 4, 4])
        nmx = sb("nmx", [P, 4, 4])
        lsum = sb("lsum", [P, 4, 4])
        linv = sb("linv", [P, 4])
        lw = sb("lw", [P, 4])
        gate = sb("gate", [P, NT, NG])
        cmx = sb("cmx", [P, NT * H])
        csum = sb("csum", [P, NT * H])
        cw = sb("cw", [P, NT * H])
        cq = sb("cq", [P, NT, H])
        fl = sb("fl", [P, NT, H])
        bf = sb("bf", [H, 1])
        rel_s = sb("rel_s", [NB, H])

        kd = nat[:, 0:4096].rearrange("p (t k g u d) -> p t k g u d", t=NT, k=4, g=G, u=2)
        vd = nat[:, 4096:5120].rearrange("p (t a n) -> p t a n", t=NT, a=2)
        kf = nat[:, 0:2048].rearrange("p (t n) -> p t n", t=NT)
        vf = nat[:, 2048:4096].rearrange("p (t n) -> p t n", t=NT)
        k2 = work[:, 0:1024].rearrange("p (x g m) -> p x g m", x=2, g=G)
        fsum = work[:, 1024:1024 + 2 * 16 * GN].rearrange("p (x c) -> p x c", x=2)
        hidk = work[:, 0:2 * GN].rearrange("p (c n) -> p c n", c=2)
        hidv = work[:, 256:256 + 4 * HN].rearrange("p (c g r n) -> p c g r n", c=2, g=G, r=4)
        hidv2 = work[:, 256:256 + 4 * HN].rearrange("p (c n) -> p c n", c=2)
        probs = work[:, 0:1536].rearrange("p (b n) -> p b n", b=2)
        pT = work[:, 1536:3072].rearrange("p (b h n) -> p b h n", b=2, h=2)
        vblk = low[0:HN, 0:1024].rearrange("p (e h d) -> p e h d", e=2, h=8)
        pcT = low[0:HN, 1024:1536].rearrange("p (c n) -> p c n", c=4)
        biasc = low[:, 1536:1536 + NT * H * NCMP].rearrange("p (t h n) -> p t h n", t=NT, h=H)
        decay0 = low[:, :].rearrange("p (h n) -> p h n", h=H)
        pc = sa[:, :, :].rearrange("p t n -> p (t n)")[:, 0:NT * H * NCMP]
        pc4 = pc.rearrange("p (t h n) -> p t h n", t=NT, h=H)
        otmp = gg[:, :, :].rearrange("p b (t h d) -> p b t h d", t=2, h=2)
        gwhi = ghi[:, :, :].rearrange("p a n -> p (a n)")
        gwlo = glo[:, :, :].rearrange("p a n -> p (a n)")
        onat = xn[:, :, :].rearrange("p t (h d) -> p t h d", h=H)
        rows = low[0:H, 0:512]
        rfl = rows[:, 0:SEQ]
        raux = rows[:, SEQ:2 * SEQ]
        finalb = work[:, 0:D]
        fexp = work[0:H, 0:SEQ]
        flog = work[0:H, SEQ:2 * SEQ]
        fcor = work[0:H, 2 * SEQ:3 * SEQ]
        frec = work[0:H, 3 * SEQ:4 * SEQ]

        acc = [ps(f"acc{i}") for i in range(4)]
        inb = [ps(f"inb{i}") for i in range(2)]
        tb = [ps(f"tb{i}") for i in range(2)]
        tbanks = [tb[0], tb[1], acc[2], acc[3]]

        s_raw = [sem(f"raw_loaded{s}") for s in range(RING)]
        s_hi = sem("unit_hi")
        s_lo = sem("unit_lo")
        s_used = sem("unit_used")
        s_x = sem("x_loaded")
        s_small = sem("small_loaded")
        s_small2 = sem("small_loaded_later")
        s_const = sem("consts")
        s_setup_t = sem("setup_turned")
        s_setup = sem("setup_copied")
        s_rows = sem("bias_rows")
        s_rows_out = sem("bias_rows_stored")
        s_bias = sem("bias_loaded")
        s_biasc = sem("biasc_ready")
        s_sumsq = sem("sumsq")
        s_rms = sem("rms")
        s_rstd = sem("rstd_ready")
        s_xn = sem("xn_ready")
        s_tt = sem("turned")
        s_thi = sem("turned_hi")
        s_tlo = sem("turned_lo")
        s_silu = sem("silu_done")
        s_g = sem("hidden_ready")
        s_gt = sem("hidden_turned")
        s_ghi = sem("hidden_hi")
        s_glo = sem("hidden_lo")
        s_acc0 = sem("ffn_tile0_done")
        s_xadd = sem("x_added")
        s_nat_a = sem("chunk_copied_act")
        s_nat_d = sem("chunk_copied_dve")
        s_rt = sem("round_turned")
        s_ra = sem("round_copied_act")
        s_rd = sem("round_copied_dve")
        s_tailw = sem("small_split")
        s_tail = sem("tail_done")
        s_gate = sem("gate_ready")
        s_fsum = sem("windows_summed")
        s_fhi = sem("windows_hi")
        s_flo = sem("windows_lo")
        s_hid = sem("cmp_hidden")
        s_cmp2 = sem("cmp_out")
        s_kcb = sem("cmp_kv_ready")
        s_sc = sem("cmp_scores")
        s_csh = sem("cmp_shifted")
        s_cexp = sem("cmp_exp")
        s_cp = sem("cmp_probs")
        s_cpt = sem("cmp_probs_turned")
        s_cpc = sem("cmp_probs_copied")
        s_co = sem("cmp_values")
        s_cog = sem("cmp_gated")
        s_qk = sem("scores")
        s_max = sem("max_done")
        s_nmax = sem("negmax_ready")
        s_exp = sem("probs_ready")
        s_pt = sem("probs_turned")
        s_pta = sem("pT_act")
        s_ptd = sem("pT_dve")
        s_pv = sem("values_done")
        s_on = sem("o_gated")
        s_oadd = sem("o_added")
        s_flc = sem("fl_copied")
        s_flt = sem("fl_turned")
        s_fa = sem("fl_abs_ready")
        s_fexp = sem("fl_exp_act")
        s_flog = sem("fl_log")
        s_neg = sem("neg_c_ready")
        s_cst = sem("neg_c_stored")
        s_cb = sem("neg_c_loaded")
        s_ct = sem("c_turned")
        s_cq = sem("c_by_query")
        s_fg = sem("final_gain")
        s_y = sem("y_ready")
        s_out = sem("out_stored")
        s_step = sem("dve_step")
        s_pstep = sem("pool_step")

        scratch_b = nc.dram_tensor("bias_rows_dram", [P, H, 512], F32).ap()
        scratch_c = nc.dram_tensor("neg_c_dram", [H, SEQ], F32).ap()

        block = ctx.enter_context(nc.Block())

        def first(turn):
            return PIECE0[turn]

        @block.sync
        def _(sp):
            def load(u, halves, number=None):
                if number is not None or u >= RING:
                    sp.wait_ge(s_lo, (u if number is None else number) - RING + 1)
                for dst, src in halves:
                    sp.dma_start(dst, src).then_inc(s_raw[u % RING], 16)

            def ffn_in(f, j, half, u):
                w = ffn_w_in[f // 2, f % 2][half * 512:(half + 1) * 512, :]
                w = w.rearrange("(k p) n -> p k n", p=P)
                r = raw[u % RING][:, :].rearrange("p (k n) -> p k n", k=4)
                return [(r[:, :, 0:FC], w[:, :, bass.ds(j * FC, FC)]),
                        (r[:, :, FC:2 * FC], w[:, :, bass.ds(j * FC + DFF, FC)])]

            def ffn_out(f, j, u):
                w = ffn_w_out[f // 2, f % 2]
                r = raw[u % RING][:, :].rearrange("p (k n) -> p k n", k=2)
                return [(r[:, k, :], w[bass.ds(j * FC + k * P, P), :]) for k in range(2)]

            def ffn(f):
                b = U_FFN[f]
                for i in range(2):
                    load(b + i, ffn_in(f, 0, i, b + i))
                with sp.Fori(1, NJ) as j:
                    for i in range(3):
                        u = b + 2 + i
                        halves = ffn_in(f, j, i, u) if i < 2 else ffn_out(f, j - 1, u)
                        load(u, halves, 3 * (j - 1) + max(u, RING))
                u = b + FFN_UNITS - 1
                load(u, ffn_out(f, NJ - 1, u))

            def matrix(w, b, chunks):
                for c, col in enumerate(chunks):
                    for i in range(2):
                        u = b + 2 * c + i
                        wr = w[i * 512:(i + 1) * 512, col:col + CW].rearrange("(k p) n -> p k n", p=P)
                        r = raw[u % RING][:, :].rearrange("p (k n) -> p k n", k=4)
                        load(u, [(r[:, 0:2], wr[:, 0:2]), (r[:, 2:4], wr[:, 2:4])])

            for t in range(NT):
                sp.dma_start(xs[:, t, :], x[0, t * P:(t + 1) * P, :]).then_inc(s_x, 16)
            ffn(0)
            matrix(nsa_w_in[0], U_NSA, [D, D + 2 * KVD, D + 4 * KVD, 0, CW])
            for xk in range(2):
                for i in range(2):
                    u = U_CMP + 2 * xk + i
                    wr = nsa_cmp_w1[0, xk, i * 1024:(i + 1) * 1024, :].rearrange("(k p) n -> p k n", p=P)
                    r = raw[u % RING][:, :].rearrange("p (k n) -> p k n", k=8)
                    load(u, [(r[:, 0:4], wr[:, 0:4]), (r[:, 4:8], wr[:, 4:8])])
            matrix(nsa_w_out[0], U_NSA_OUT, [0, CW])
            ffn(1)
            matrix(fox_w_kvf, U_KV, [0, CW, 2 * CW, 3 * CW])
            ffn(2)
            matrix(fox_w_q[0], U_FOXQ, [0, CW])
            matrix(fox_w_out[0], U_FOX_OUT, [0, CW])
            ffn(3)
            for t in range(NT):
                sp.wait_ge(s_y, t + 1)
                sp.dma_start(out[0, t * P:(t + 1) * P, :], xn[:, t, :]).then_inc(s_out, 16)
            sp.wait_ge(s_out, 16 * NT)

        @block.tensor
        def _(pe):
            def turn(name):
                i = TURNS.index(name)
                for q in range(4):
                    for t in range(NT):
                        if q == 0 and not name.endswith("_o") and name != "ffn2":
                            pe.wait_ge(s_xn, NT * NORMS.index(name) + t + 1)
                        for k in range(2):
                            mm = pe.transpose(tbanks[q][:, k * SEQ + t * P:k * SEQ + (t + 1) * P],
                                              xn[:, t, (2 * q + k) * P:(2 * q + k + 1) * P], ident[:, :])
                    mm.then_inc(s_tt, 1)

            def three(o, lh, ll, rh, rl, start, stop):
                pe.matmul(o, lh, rh, start=start, stop=False, skip_group_check=True)
                pe.matmul(o, lh, rl, start=False, stop=False, skip_group_check=True)
                return pe.matmul(o, ll, rh, start=False, stop=stop, skip_group_check=True)

            def unit_in(slot, half, banks, need, turn_name=None):
                pe.wait_ge(s_lo, need)
                for k in range(4):
                    kk = 4 * half + k
                    if turn_name:
                        n = kk + 1 if PIECES[turn_name] == KT else kk // 2 + 1
                        pe.wait_ge(s_tlo, first(turn_name) + n)
                    for t in range(NT):
                        tok = slice(t * P, (t + 1) * P)
                        mm = three(banks[t][:, :], thi[:, kk, tok], tlo[:, kk, tok],
                                   whi[slot][:, k * CW:(k + 1) * CW], wlo[slot][:, k * CW:(k + 1) * CW],
                                   kk == 0, kk == KT - 1)
                mm.then_inc(s_used, 1)

            def chunk(b, c, banks, turn_name=None):
                for half in range(2):
                    u = b + 2 * c + half
                    unit_in(u % RING, half, banks, u + 1, turn_name)

            def hidden_out(slot, need, done, last=False):
                pe.wait_ge(s_lo, need)
                pe.wait_ge(s_glo, done)
                for t in range(NT):
                    tok = slice(t * P, (t + 1) * P)
                    for k in range(2):
                        for n in range(2):
                            col = slice(k * D + n * CW, k * D + (n + 1) * CW)
                            mm = three(acc[2 * t + n][:, :], ghi[:, k, tok], glo[:, k, tok],
                                       whi[slot][:, col], wlo[slot][:, col], False, last and k == 1)
                    if last and t == 0:
                        mm.then_inc(s_acc0, 1)
                mm.then_inc(s_used, 1)

            def hidden_turn(need):
                pe.wait_ge(s_g, need)
                for k in range(2):
                    for t in range(NT):
                        mm = pe.transpose(tb[0][:, k * SEQ + t * P:k * SEQ + (t + 1) * P],
                                          gg[:, t, k * P:(k + 1) * P], ident[:, :])
                mm.then_inc(s_gt, 1)

            def ffn(f):
                b, n0 = U_FFN[f], NJ * f
                turn(f"ffn{f}")
                chunk(b, 0, inb, f"ffn{f}")
                for a in acc:
                    pe.matmul(a[:, :], zeros[:, :], zeros[:, :].unsqueeze(1).broadcast_to([32, 4, P]), start=True, stop=False,
                              skip_group_check=True)
                hidden_turn(2 * (n0 + 1))
                with pe.Fori(1, NJ) as j:
                    for half in range(2):
                        u = b + 2 + half
                        unit_in(u % RING, half, inb, 3 * (j - 1) + u + 1)
                    hidden_out((b + 4) % RING, 3 * (j - 1) + b + 5, j + n0)
                    hidden_turn(2 * j + 2 * n0 + 2)
                u = b + FFN_UNITS - 1
                hidden_out(u % RING, u + 1, n0 + NJ, True)

            def tail(banks, cols):
                for t in range(NT):
                    tok = slice(t * P, (t + 1) * P)
                    for k in range(KT):
                        mm = three(banks[t][:, 0:cols], thi[:, k, tok], tlo[:, k, tok],
                                   gwhi[:, k * cols:(k + 1) * cols], gwlo[:, k * cols:(k + 1) * cols],
                                   k == 0, k == KT - 1)
                mm.then_inc(s_tail, 1)

            def round_(r, parts):
                if r % 12 >= 2:
                    prev = r - 2
                    pe.wait_ge(s_ra, prev + 1)
                    pe.wait_ge(s_rd, prev + 1)
                for k, src in enumerate(parts):
                    for t in range(NT):
                        mm = pe.transpose(tb[r % 2][:, k * SEQ + t * P:k * SEQ + (t + 1) * P],
                                          src(t), ident[:, :])
                mm.then_inc(s_rt, 1)

            def q_round(r, i):
                round_(r, [lambda t, p=p: xn[:, t, p * P:(p + 1) * P] for p in (2 * i, 2 * i + 1)])

            def scores(n, kidx, p):
                s1, s0 = acc[2 * (n % 2)], acc[2 * (n % 2) + 1]
                pe.matmul(s1[:, :], qT[:, p, P:2 * P], kblk[:, :, kidx, :], start=True,
                          stop=True).then_inc(s_qk, 1)
                pe.matmul(s0[:, 0:2 * P], qT[:, p, 0:P], kblk[:, :, kidx, 0:P], start=True,
                          stop=True).then_inc(s_qk, 1)

            def turn_probs(n, n_first):
                pe.wait_ge(s_exp, 4 * n + 4)
                if n > n_first:
                    pe.wait_ge(s_pta, n)
                    pe.wait_ge(s_ptd, n)
                for h in range(2):
                    parts = [h * P, 2 * P + h * SEQ, 2 * P + h * SEQ + P]
                    for i, c in enumerate(parts):
                        mm = pe.transpose(tb[h][:, i * P:(i + 1) * P], probs[:, n % 2, c:c + P],
                                          ident[:, :])
                    mm.then_inc(s_pt, 1)

            def values(n, n_first, v):
                pe.wait_ge(s_pta, n + 1)
                pe.wait_ge(s_ptd, n + 1)
                if n >= n_first + 2:
                    pe.wait_ge(s_on, n - 1)
                for h in range(2):
                    o = inb[n % 2]
                    mm = pe.matmul(o[:, h * DH:(h + 1) * DH], pT[:, n % 2, h, 0:P], v(0, h),
                                   start=True, stop=True)
                    for k in range(2):
                        mm = pe.matmul(o[:, P + h * DH:P + (h + 1) * DH],
                                       pT[:, n % 2, h, (1 + k) * P:(2 + k) * P], v(k, h),
                                       start=k == 0, stop=k == 1)
                mm.then_inc(s_pv, 1)

            def items(n0, kidx, v, count):
                for i in range(count + 1):
                    if i + 1 < count:
                        scores(n0 + i + 1, kidx(i + 1), (i + 1) % 8)
                    if i < count:
                        turn_probs(n0 + i, n0)
                    if i >= 1:
                        values(n0 + i - 1, n0, v(i - 1))

            def project_out(b, name):
                turn(name)
                chunk(b, 0, acc[0:2], name)
                chunk(b, 1, acc[2:4], name)

            pe.wait_ge(s_const, 1)
            pe.wait_ge(s_small, 16 * 4)
            pe.transpose(tb[0][:, 0:56], work[0:56, 0:P], ident[0:56, 0:56])
            pe.transpose(tb[0][:, 64:96], work[0:32, P:2 * P], ident[0:32, 0:32])
            pe.transpose(tb[0][0:H, 96:128], rel_s[:, :], ident[0:NB, 0:NB]).then_inc(s_setup_t, 1)
            pe.wait_ge(s_setup, 1)
            pe.wait_ge(s_const, 2)
            ffn(0)

            turn("nsa")
            chunk(U_NSA, 0, inb, "nsa")
            pe.wait_ge(s_tailw, 2)
            tail(acc[2:4], NG)
            chunk(U_NSA, 1, acc[0:2])
            pe.wait_ge(s_nat_a, 1)
            pe.wait_ge(s_nat_d, 1)
            for r in range(4):
                kind, g0 = r // 2, 2 * (r % 2)
                round_(r, [lambda t, g=g: kd[:, t, kind, g].rearrange("p u d -> p (u d)")
                           for g in (g0, g0 + 1)])
            chunk(U_NSA, 2, inb)
            pe.wait_ge(s_nat_a, 2)
            pe.wait_ge(s_nat_d, 2)
            for r in range(2):
                round_(4 + r, [lambda t, g=g: kd[:, t, 2, g].rearrange("p u d -> p (u d)")
                               for g in (2 * r, 2 * r + 1)])
            chunk(U_NSA, 3, acc[0:2])
            pe.wait_ge(s_nat_a, 3)
            pe.wait_ge(s_nat_d, 3)
            for r in range(2):
                round_(6 + r, [lambda t, g=g: kd[:, t, 3, g].rearrange("p u d -> p (u d)")
                               for g in (2 * r, 2 * r + 1)])
            pe.wait_ge(s_gate, 1)
            chunk(U_NSA, 4, acc[2:4])

            def compress(xk):
                pe.wait_ge(s_flo, xk + 1)
                for i in range(2):
                    u = U_CMP + 2 * xk + i
                    pe.wait_ge(s_lo, u + 1)
                    for k in range(8):
                        c = 8 * i + k
                        for hh in range(2):
                            col = slice(k * CMP_HIDDEN + hh * P, k * CMP_HIDDEN + (hh + 1) * P)
                            w_hi, w_lo = whi[u % RING][:, col], wlo[u % RING][:, col]
                            o = (inb if xk == 0 else acc[0:2])[hh][:, 0:GN]
                            pe.matmul(o, w_hi, fhi[:, c, :], start=c == 0, stop=False, skip_group_check=True)
                            pe.matmul(o, w_hi, flo[:, c, :], start=False, stop=False, skip_group_check=True)
                            mm = pe.matmul(o, w_lo, fhi[:, c, :], start=False, stop=c == 15,
                                           skip_group_check=True)
                    mm.then_inc(s_used, 1)

            compress(0)
            pe.wait_ge(s_nat_a, 5)
            pe.wait_ge(s_nat_d, 5)
            for r in range(4):
                q_round(8 + r, r)
            compress(1)
            pe.wait_ge(s_hid, 4)
            pe.wait_ge(s_ra, 12)
            pe.wait_ge(s_rd, 12)
            for c in range(2):
                pe.matmul(tb[0][:, 0:GN], w2k[:, c].rearrange("p u d -> p (u d)"), hidk[:, c, :],
                          start=c == 0, stop=c == 1)
            for e in range(2):
                for c in range(2):
                    mm = pe.matmul(tb[0][0:HN, 64 + e * DH:64 + (e + 1) * DH],
                                   hidv2[:, c, e * HN:(e + 1) * HN], w2v[:, c, :],
                                   start=c == 0, stop=c == 1)
            mm.then_inc(s_cmp2, 1)
            pe.wait_ge(s_kcb, 1)
            for t in range(NT):
                for p in range(H // 2):
                    c0 = t * H * NCMP + 2 * p * NCMP
                    mm = pe.matmul(inb[0][:, c0:c0 + 2 * NCMP], qT[:, p, t * P:(t + 1) * P],
                                   kcb[:, p // 2].rearrange("p u n -> p (u n)"), start=True, stop=True)
            mm.then_inc(s_sc, 1)
            pe.wait_ge(s_cp, 1)
            for t in range(NT):
                for e in range(2):
                    c0 = (t * H + 8 * e) * NCMP
                    mm = pe.transpose(tb[1][0:HN, (2 * t + e) * P:(2 * t + e + 1) * P],
                                      pc[:, c0:c0 + HN], ident[:, :])
            mm.then_inc(s_cpt, 1)
            pe.wait_ge(s_cpc, 1)
            for t in range(NT):
                for e in range(2):
                    pe.matmul(acc[2 * t + e][:, :], pcT[:, 2 * t + e, :],
                              vblk[:, e].rearrange("p h d -> p (h d)"), start=True,
                              stop=True).then_inc(s_co, 1)
            pe.wait_ge(s_cog, 4)
            scores(0, 0, 0)
            items(0, lambda i: i // 2, lambda i: (lambda k, h: vd[:, k, i // 8, (i % 8 // 2) * DH:
                                                              (i % 8 // 2 + 1) * DH]), 16)
            pe.wait_ge(s_oadd, 16)
            project_out(U_NSA_OUT, "nsa_o")
            ffn(1)

            turn("kv")
            for k in range(KT):
                pe.wait_ge(s_tlo, first("kv") + k + 1)
            pe.wait_ge(s_tailw, 4)
            tail(acc[2:4], H)
            chunk(U_KV, 0, acc[0:2])
            pe.wait_ge(s_flc, 1)
            for t in range(NT):
                mm = pe.transpose(tb[0][0:H, t * P:(t + 1) * P], fl[:, t, :], ident[:, :])
            mm.then_inc(s_flt, 1)
            chunk(U_KV, 1, inb)
            pe.wait_ge(s_nat_a, 6)
            pe.wait_ge(s_nat_d, 6)
            pe.wait_ge(s_fa, 1)
            for i in range(2):
                round_(12 + i, [lambda t, p=p: kf[:, t, p * P:(p + 1) * P] for p in (2 * i, 2 * i + 1)])
            chunk(U_KV, 2, acc[0:2])
            pe.wait_ge(s_nat_a, 7)
            pe.wait_ge(s_nat_d, 7)
            for i in range(2, 4):
                round_(12 + i, [lambda t, p=p: kf[:, t, p * P:(p + 1) * P] for p in (2 * i, 2 * i + 1)])
            pe.wait_ge(s_neg, 1)
            for t in range(NT):
                mm = pe.transpose(acc[2][:, t * H:(t + 1) * H], rfl[:, t * P:(t + 1) * P],
                                  ident[0:H, 0:H])
            mm.then_inc(s_ct, 1)
            chunk(U_KV, 3, inb)
            pe.wait_ge(s_ra, 16)
            pe.wait_ge(s_rd, 16)
            pe.wait_ge(s_nat_a, 9)
            pe.wait_ge(s_nat_d, 9)
            pe.wait_ge(s_cq, 1)
            ffn(2)

            turn("fox")
            chunk(U_FOXQ, 0, acc[0:2], "fox")
            chunk(U_FOXQ, 1, inb)
            for i in range(4):
                if i % 2 == 0:
                    pe.wait_ge(s_nat_a, 10 + i // 2)
                    pe.wait_ge(s_nat_d, 10 + i // 2)
                q_round(16 + i, i)
            pe.wait_ge(s_ra, 20)
            pe.wait_ge(s_rd, 20)
            scores(16, 0, 0)
            items(16, lambda i: i, lambda i: (lambda k, h: vf[:, k, (2 * i + h) * DH:(2 * i + h + 1) * DH]), 8)
            pe.wait_ge(s_on, 24)
            project_out(U_FOX_OUT, "fox_o")
            ffn(3)

        @block.scalar
        def _(act):
            def hi(u):
                if u >= U_END:
                    return
                act.wait_ge(s_raw[u % RING], 32 * (u // RING + 1))
                if u >= RING:
                    act.wait_ge(s_used, u - RING + 1)
                act.copy(whi[u % RING][:, :], raw[u % RING][:, :]).then_inc(s_hi, 1)

            def hi_loop(u, j):
                act.wait_ge(s_raw[u % RING], 32 * (j - 1) + 32 * (u // RING + 1))
                act.wait_ge(s_used, 3 * (j - 1) + u - RING + 1)
                act.copy(whi[u % RING][:, :], raw[u % RING][:, :]).then_inc(s_hi, 1)

            def norm(name):
                i = NORMS.index(name)
                for t in range(NT):
                    if i == 0:
                        act.wait_ge(s_x, 16 * NT)
                    else:
                        a = {"nsa": "ffn0", "ffn1": "nsa", "kv": "ffn1", "fox": "ffn2", "ffn3": "fox",
                             "final": "ffn3"}[name]
                        n = 4 * ADDS.index(a)
                        act.wait_ge(s_xadd, n + (2 * t + 2 if a.startswith("ffn") else 3 + t))
                    act.activation(xn[:, t, :], xs[:, t, :], ACT.Square,
                                   accum_out=ss[:, t:t + 1]).then_inc(s_sumsq, 1)
                    act.wait_ge(s_sumsq, NT * i + t + 1)
                    act.activation(ss[:, NT + t:NT + t + 1], ss[:, t:t + 1], ACT.Sqrt, bias=epst[:, :],
                                   scale=1.0 / D).then_inc(s_rms, 1)

            def turned(name):
                i = TURNS.index(name)
                for q in range(4):
                    act.wait_ge(s_tt, 4 * i + q + 1)
                    if name.endswith("_o"):
                        act.copy(thi[:, 2 * q:2 * q + 2, :].rearrange("p k n -> p (k n)"),
                                 tbanks[q][:, :]).then_inc(s_thi, 1)
                        continue
                    for k in range(2):
                        kk = 2 * q + k
                        act.mul(thi[:, kk, :], tbanks[q][:, k * SEQ:(k + 1) * SEQ],
                                gains[:, GAIN[name] * KT + kk:GAIN[name] * KT + kk + 1]).then_inc(s_thi, 1)

            def silu(used):
                act.wait_ge(s_used, used)
                for t in range(NT):
                    act.activation(sa[:, t, :], inb[t][:, 0:FC], ACT.Silu).then_inc(s_silu, 1)

            def hidden_hi(n):
                act.wait_ge(s_gt, n)
                act.copy(ghi[:, :, :].rearrange("p k n -> p (k n)"), tb[0][:, :]).then_inc(s_ghi, 1)

            def ffn(f):
                b, n0 = U_FFN[f], NJ * f
                turned(f"ffn{f}")
                hi(b + 2)
                hi(b + 3)
                silu(b + 2)
                hi(b + 4)
                last = NJ if b + FFN_UNITS < U_END else NJ - 1
                with act.Fori(1, last) as j:
                    hidden_hi(j + n0)
                    hi_loop(b + 5, j)
                    silu(3 * (j - 1) + b + 4)
                    hi_loop(b + 6, j)
                    hi_loop(b + 7, j)
                if last < NJ:
                    hidden_hi(last + n0)
                    hi(b + 5 + 3 * (last - 1))
                    silu(3 * (last - 1) + b + 4)
                hidden_hi(n0 + NJ)

            def chunk_q(bank, c, used):
                act.wait_ge(s_used, used)
                act.mul(xn[:, 0, c * CW:(c + 1) * CW], bank[:, :], SCALE).then_inc(s_nat_a, 1)

            def lower(r, dst):
                act.wait_ge(s_rt, r + 1)
                act.copy(dst, tb[r % 2][0:DH, :]).then_inc(s_ra, 1)

            def q_half(r, i):
                act.wait_ge(s_rt, r + 1)
                act.copy(qT[:, 2 * i, :], tb[r % 2][:, 0:SEQ]).then_inc(s_ra, 1)

            def exps(n):
                act.wait_ge(s_nmax, n + 1)
                for i in range(4):
                    t, h = divmod(i, 2)
                    c0, w = (h * P, P) if t == 0 else (2 * P + h * SEQ, SEQ)
                    act.activation(probs[:, n % 2, c0:c0 + w], probs[:, n % 2, c0:c0 + w], ACT.Exp,
                                   bias=nmx[:, n % 4, i:i + 1],
                                   accum_out=lsum[:, n % 4, i:i + 1]).then_inc(s_exp, 1)

            def pt_copy(n):
                act.wait_ge(s_pt, 2 * n + 1)
                act.copy(pT[:, n % 2, 0, :], tb[0][:, 0:3 * P]).then_inc(s_pta, 1)

            def items(n0, count):
                exps(n0)
                for i in range(count):
                    pt_copy(n0 + i)
                    if i + 1 < count:
                        exps(n0 + i + 1)

            act.dma_start(work[0:48, 0:P], norm_g.rearrange("l n (k p) -> (l n k) p", p=P)).then_inc(s_small, 16)
            act.dma_start(work[48:56, 0:P], kv_norm_g.rearrange("(k p) -> k p", p=P)).then_inc(s_small, 16)
            act.dma_start(work[0:32, P:2 * P],
                          nsa_cmp_pos.rearrange("l x (t c) d -> (l x t) (c d)", c=2)).then_inc(s_small, 16)
            act.dma_start(rel_s[:, :], rel_bias).then_inc(s_small, 16)
            act.wait_ge(s_const, 2)
            norm("ffn0")
            hi(0)
            hi(1)
            act.wait_ge(s_setup, 1)
            ffn(0)

            norm("nsa")
            turned("nsa")
            hi(U_NSA + 2)
            act.wait_ge(s_small2, 16 * 6)
            act.copy(gwhi[:, 0:KT * NG], gate_w[:, :, :].rearrange("p k n -> p (k n)")).then_inc(s_tailw, 1)
            hi(U_NSA + 3)
            hi(U_NSA + 4)
            act.wait_ge(s_used, U_NSA + 2)
            act.copy(kd[:, 0, 0:2].rearrange("p k g u d -> p (k g) u d"),
                     inb[0][:, :].rearrange("p (g d) -> p g d", d=DH).unsqueeze(2)
                     .broadcast_to([P, 8, 2, DH])).then_inc(s_nat_a, 1)
            act.wait_ge(s_tail, 1)
            for t in range(NT):
                mm = act.activation(gate[:, t, :], acc[2 + t][:, 0:NG], ACT.Sigmoid)
            mm.then_inc(s_gate, 1)
            hi(U_NSA + 5)
            hi(U_NSA + 6)

            def kv_copy(bank, kind, a, used):
                act.wait_ge(s_used, used)
                act.copy(kd[:, 0, kind], bank[:, 0:KVD].rearrange("p (g d) -> p g d", d=DH).unsqueeze(2)
                         .broadcast_to([P, G, 2, DH]))
                act.copy(vd[:, 0, a, :], bank[:, KVD:2 * KVD]).then_inc(s_nat_a, 1)

            kv_copy(acc[0], 2, 0, U_NSA + 4)
            for r in range(4):
                act.wait_ge(s_rt, r + 1)
                act.copy(k2[0:DH, r // 2, 2 * (r % 2):2 * (r % 2) + 2, :],
                         tb[r % 2][0:DH, :].rearrange("p (g m s) -> p g m s", g=2, s=2)[:, :, :, 0]
                         ).then_inc(s_ra, 1)
            hi(U_NSA + 7)
            hi(U_NSA + 8)
            kv_copy(inb[0], 3, 1, U_NSA + 6)
            for r in range(2):
                lower(4 + r, kblk[0:DH, 0, 2 * r:2 * r + 2, :])
            act.wait_ge(s_fsum, 1)
            act.copy(fhi[:, :, :].rearrange("p t n -> p (t n)"), fsum[:, 0, :]).then_inc(s_fhi, 1)
            hi(U_NSA + 9)
            hi(U_NSA + 10)
            chunk_q(acc[0], 0, U_NSA + 8)
            for r in range(2):
                lower(6 + r, kblk[0:DH, 0, 4 + 2 * r:6 + 2 * r, :])
            hi(U_NSA + 11)
            hi(U_NSA + 12)
            chunk_q(acc[2], 1, U_NSA + 10)
            hi(U_NSA + 13)
            hi(U_NSA + 14)
            act.wait_ge(s_fsum, 2)
            act.copy(fhi[:, :, :].rearrange("p t n -> p (t n)"), fsum[:, 1, :]).then_inc(s_fhi, 1)
            for r in range(4):
                q_half(8 + r, r)
            for c in range(2):
                act.activation(hidk[:, c, :], inb[c][:, 0:GN], ACT.Silu).then_inc(s_hid, 1)
            hi(U_NSA + 15)
            hi(U_NSA + 16)
            for c in range(2):
                act.activation(hidv[:, c], acc[c][:, 0:GN].rearrange("p (g n) -> p g n", g=G).unsqueeze(2)
                               .broadcast_to([P, G, 4, NCMP]), ACT.Silu).then_inc(s_hid, 1)
            act.wait_ge(s_csh, 1)
            act.activation(pc, pc, ACT.Exp).then_inc(s_cexp, 1)
            act.wait_ge(s_cpt, 1)
            act.copy(pcT.rearrange("p c n -> p (c n)"), tb[1][0:HN, :]).then_inc(s_cpc, 1)
            items(0, 16)
            turned("nsa_o")
            for i in range(3):
                hi(U_NSA_OUT + 3 + i)
            norm("ffn1")
            ffn(1)

            norm("kv")
            turned("kv")
            hi(U_KV + 2)
            act.copy(gwhi[:, 0:KT * H], fl_w[:, :, :].rearrange("p k n -> p (k n)")).then_inc(s_tailw, 1)
            hi(U_KV + 3)
            hi(U_KV + 4)
            act.wait_ge(s_used, U_KV + 2)
            act.copy(kf[:, 0, 0:CW], acc[0][:, :]).then_inc(s_nat_a, 1)
            act.wait_ge(s_fa, 1)
            act.activation(fexp, raux, ACT.Exp).then_inc(s_fexp, 1)
            act.wait_ge(s_fexp, 1)
            act.activation(flog, fexp, ACT.Ln, bias=1.0).then_inc(s_flog, 1)
            hi(U_KV + 5)
            hi(U_KV + 6)
            act.wait_ge(s_used, U_KV + 4)
            act.copy(kf[:, 0, CW:2 * CW], inb[0][:, :]).then_inc(s_nat_a, 1)
            for i in range(2):
                lower(12 + i, kblk[0:DH, 0, 2 * i:2 * i + 2, :])
            hi(U_KV + 7)
            hi(U_KV + 8)
            act.wait_ge(s_used, U_KV + 6)
            act.copy(vf[:, 0, 0:CW], acc[0][:, :]).then_inc(s_nat_a, 1)
            for i in range(2, 4):
                lower(12 + i, kblk[0:DH, 0, 2 * i:2 * i + 2, :])
            hi(U_KV + 9)
            act.wait_ge(s_used, U_KV + 8)
            act.copy(vf[:, 0, CW:2 * CW], inb[0][:, :]).then_inc(s_nat_a, 1)
            ffn(2)

            norm("fox")
            turned("fox")
            hi(U_FOXQ + 2)
            hi(U_FOXQ + 3)
            hi(U_FOXQ + 4)
            chunk_q(acc[0], 0, U_FOXQ + 2)
            hi(U_FOXQ + 5)
            hi(U_FOXQ + 6)
            chunk_q(inb[0], 1, U_FOXQ + 4)
            for i in range(4):
                q_half(16 + i, i)
            items(16, 8)
            turned("fox_o")
            for i in range(3):
                hi(U_FOX_OUT + 3 + i)
            norm("ffn3")
            ffn(3)
            norm("final")

        @block.vector
        def _(dve):
            steps = [0]

            def step(ins):
                steps[0] += 1
                ins.then_inc(s_step, 1)
                dve.wait_ge(s_step, steps[0])

            def lo(u):
                dve.wait_ge(s_hi, u + 1)
                dve.tensor_tensor(wlo[u % RING][:, :], raw[u % RING][:, :],
                                  whi[u % RING][:, :].bitcast(F32), ALU.subtract).then_inc(s_lo, 1)

            def lo_loop(u, j):
                dve.wait_ge(s_hi, 3 * (j - 1) + u + 1)
                dve.tensor_tensor(wlo[u % RING][:, :], raw[u % RING][:, :],
                                  whi[u % RING][:, :].bitcast(F32), ALU.subtract).then_inc(s_lo, 1)

            def norm(name):
                i = NORMS.index(name)
                for t in range(NT):
                    dve.wait_ge(s_rms, NT * i + t + 1)
                    dve.reciprocal(rstd[:, t:t + 1], ss[:, NT + t:NT + t + 1]).then_inc(s_rstd, 1)
                    dve.wait_ge(s_rstd, NT * i + t + 1)
                    if name == "final":
                        if t == 0:
                            dve.wait_ge(s_fg, 16)
                        dve.scalar_tensor_tensor(out=xn[:, t, :], in0=xs[:, t, :], scalar=rstd[:, t:t + 1],
                                                 in1=finalb, op0=ALU.mult, op1=ALU.mult).then_inc(s_y, 1)
                    else:
                        dve.tensor_scalar(xn[:, t, :], xs[:, t, :], rstd[:, t:t + 1], None,
                                          ALU.mult).then_inc(s_xn, 1)

            def turned(name):
                n = PIECE0[name]
                for q in range(4):
                    if name.endswith("_o"):
                        dve.wait_ge(s_thi, n + q + 1)
                        dve.tensor_tensor(tlo[:, 2 * q:2 * q + 2, :].rearrange("p k n -> p (k n)"),
                                          tbanks[q][:, :],
                                          thi[:, 2 * q:2 * q + 2, :].rearrange("p k n -> p (k n)").bitcast(F32),
                                          ALU.subtract).then_inc(s_tlo, 1)
                        continue
                    dve.wait_ge(s_thi, n + 2 * q + 2)
                    for k in range(2):
                        kk = 2 * q + k
                        dve.scalar_tensor_tensor(
                            out=tlo[:, kk, :], in0=tbanks[q][:, k * SEQ:(k + 1) * SEQ],
                            scalar=gains[:, GAIN[name] * KT + kk:GAIN[name] * KT + kk + 1],
                            in1=thi[:, kk, :].bitcast(F32), op0=ALU.mult, op1=ALU.subtract).then_inc(s_tlo, 1)

            def hidden(n):
                for t in range(NT):
                    dve.wait_ge(s_silu, n + t + 1)
                    dve.tensor_tensor(gg[:, t, :], sa[:, t, :], inb[t][:, FC:2 * FC],
                                      ALU.mult).then_inc(s_g, 1)

            def hidden_lo(n):
                dve.wait_ge(s_ghi, n)
                dve.tensor_tensor(glo[:, :, :].rearrange("p k n -> p (k n)"), tb[0][:, :],
                                  ghi[:, :, :].rearrange("p k n -> p (k n)").bitcast(F32),
                                  ALU.subtract).then_inc(s_glo, 1)

            def ffn(f):
                b, n0 = U_FFN[f], NJ * f
                turned(f"ffn{f}")
                lo(b + 2)
                lo(b + 3)
                hidden(2 * n0)
                lo(b + 4)
                last = NJ if b + FFN_UNITS < U_END else NJ - 1
                with dve.Fori(1, last) as j:
                    hidden_lo(j + n0)
                    lo_loop(b + 5, j)
                    hidden(2 * j + 2 * n0)
                    lo_loop(b + 6, j)
                    lo_loop(b + 7, j)
                if last < NJ:
                    hidden_lo(last + n0)
                    lo(b + 5 + 3 * (last - 1))
                    hidden(2 * last + 2 * n0)
                hidden_lo(n0 + NJ)
                for t in range(NT):
                    if t == 0:
                        dve.wait_ge(s_acc0, f + 1)
                    else:
                        dve.wait_ge(s_used, b + FFN_UNITS)
                    for n in range(2):
                        xc = xs[:, t, n * CW:(n + 1) * CW]
                        dve.scalar_tensor_tensor(out=xc, in0=acc[2 * t + n][:, :], scalar=0.5, in1=xc,
                                                 op0=ALU.mult, op1=ALU.add).then_inc(s_xadd, 1)

            def x_add(b):
                for c in range(2):
                    dve.wait_ge(s_used, b + 2 * c + 2)
                    for t in range(NT):
                        xc = xs[:, t, c * CW:(c + 1) * CW]
                        dve.tensor_tensor(xc, acc[2 * c + t][:, :], xc, ALU.add).then_inc(s_xadd, 1)
                    if c == 0:
                        lo(b + 3)
                        lo(b + 4)
                lo(b + 5)

            def chunk_q(bank, c, used):
                dve.wait_ge(s_used, used)
                dve.tensor_scalar(xn[:, 1, c * CW:(c + 1) * CW], bank[:, :], SCALE, None,
                                  ALU.mult).then_inc(s_nat_d, 1)

            def upper(r, dst):
                dve.wait_ge(s_rt, r + 1)
                dve.tensor_copy(dst, tb[r % 2][DH:P, :]).then_inc(s_rd, 1)

            def q_half(r, i):
                dve.wait_ge(s_rt, r + 1)
                dve.wait_ge(s_ra, r + 1)
                dve.tensor_copy(qT[:, 2 * i + 1, :], tb[r % 2][:, SEQ:2 * SEQ]).then_inc(s_rd, 1)

            def add_max(n, p, table0):
                for i in (2, 3, 0, 1):
                    t, h = divmod(i, 2)
                    if h == 0:
                        dve.wait_ge(s_qk, 2 * n + (1 if t else 2))
                    if t:
                        dst = probs[:, n % 2, 2 * P + h * SEQ:2 * P + (h + 1) * SEQ]
                        src = acc[2 * (n % 2)][:, h * SEQ:(h + 1) * SEQ]
                        tab = bias[:, 2 * p + h, :]
                    else:
                        dst = probs[:, n % 2, h * P:(h + 1) * P]
                        src = acc[2 * (n % 2) + 1][:, h * P:(h + 1) * P]
                        tab = table0(2 * p + h)
                    dve.tensor_tensor_reduce(dst, src, tab, 1.0, -3e38, ALU.add, ALU.max,
                                             mx[:, n % 4, i:i + 1]).then_inc(s_max, 1)
                dve.wait_ge(s_max, 4 * n + 4)
                dve.tensor_scalar(nmx[:, n % 4, :], mx[:, n % 4, :], -1.0, None, ALU.mult).then_inc(s_nmax, 1)

            def pt_copy(n):
                dve.wait_ge(s_pt, 2 * n + 2)
                dve.tensor_copy(pT[:, n % 2, 1, :], tb[1][:, 0:3 * P]).then_inc(s_ptd, 1)

            def output(n, p, branch):
                if n:
                    dve.wait_ge(s_on, n)
                dve.wait_ge(s_pv, n + 1)
                step(dve.reciprocal(linv[:, :], lsum[:, n % 4, :]))
                o = inb[n % 2][:, 0:2 * P].rearrange("p (t h d) -> p t h d", t=2, h=2)
                if branch is None:
                    w, dst = linv, onat[:, :, 2 * p:2 * p + 2, :]
                else:
                    g = gate[:, :, :].rearrange("p t (h c) -> p t h c", c=3)[:, :, 2 * p:2 * p + 2, branch]
                    step(dve.tensor_tensor(lw[:, :].rearrange("p (t h) -> p t h", t=2),
                                           linv[:, :].rearrange("p (t h) -> p t h", t=2), g, ALU.mult))
                    w, dst = lw, otmp[:, n % 2]
                    if n >= 2:
                        dve.wait_ge(s_oadd, n - 1)
                dve.tensor_tensor(dst, o, w[:, :].rearrange("p (t h) -> p t h", t=2).unsqueeze(3)
                                  .broadcast_to([P, 2, 2, DH]), ALU.mult).then_inc(s_on, 1)

            def items(n0, count, pair, table0, branch):
                add_max(n0, 0, table0)
                for i in range(count + 1):
                    if i + 1 < count:
                        add_max(n0 + i + 1, pair(i + 1), table0)
                    if i < count:
                        pt_copy(n0 + i)
                    if i >= 1:
                        output(n0 + i - 1, pair(i - 1), branch(i - 1))

            dve.wait_ge(s_setup_t, 1)
            dve.tensor_copy(gains[:, :], tb[0][:, 0:56])
            dve.tensor_copy(posT[:, :], tb[0][:, 64:96])
            dve.tensor_copy(tbT[:, :], tb[0][0:H, 96:128]).then_inc(s_setup, 1)
            dve.wait_ge(s_setup, 1)
            norm("ffn0")
            lo(0)
            lo(1)
            ffn(0)

            norm("nsa")
            turned("nsa")
            lo(U_NSA + 2)
            dve.wait_ge(s_tailw, 1)
            dve.tensor_tensor(gwlo[:, 0:KT * NG], gate_w[:, :, :].rearrange("p k n -> p (k n)"),
                              gwhi[:, 0:KT * NG].bitcast(F32), ALU.subtract).then_inc(s_tailw, 1)
            lo(U_NSA + 3)
            lo(U_NSA + 4)
            dve.wait_ge(s_used, U_NSA + 2)
            dve.tensor_copy(kd[:, 1, 0:2].rearrange("p k g u d -> p (k g) u d"),
                            inb[1][:, :].rearrange("p (g d) -> p g d", d=DH).unsqueeze(2)
                            .broadcast_to([P, 8, 2, DH])).then_inc(s_nat_d, 1)
            lo(U_NSA + 5)
            lo(U_NSA + 6)

            def kv_copy(bank, kind, a, used):
                dve.wait_ge(s_used, used)
                dve.tensor_copy(kd[:, 1, kind], bank[:, 0:KVD].rearrange("p (g d) -> p g d", d=DH)
                                .unsqueeze(2).broadcast_to([P, G, 2, DH]))
                dve.tensor_copy(vd[:, 1, a, :], bank[:, KVD:2 * KVD]).then_inc(s_nat_d, 1)

            kv_copy(acc[1], 2, 0, U_NSA + 4)
            for r in range(4):
                dve.wait_ge(s_rt, r + 1)
                dve.tensor_copy(k2[DH:P, r // 2, 2 * (r % 2):2 * (r % 2) + 2, :],
                                tb[r % 2][DH:P, :].rearrange("p (g m s) -> p g m s", g=2, s=2)[:, :, :, 1]
                                ).then_inc(s_rd, 1)
            dve.wait_ge(s_ra, 4)
            dve.wait_ge(s_rd, 4)
            for xk in range(2):
                for th in range(2):
                    tok = k2[:, xk].rearrange("p g (n t) -> p t g n", t=8)[:, :, :, th:th + NCMP]
                    pos = posT[:, 16 * xk + 8 * th:16 * xk + 8 * th + 8].unsqueeze(2).unsqueeze(3)
                    ins = dve.tensor_tensor(
                        fsum[:, xk, th * 8 * GN:(th + 1) * 8 * GN].rearrange("p (t g n) -> p t g n", t=8, g=G),
                        tok, pos.broadcast_to([P, 8, G, NCMP]), ALU.add)
                ins.then_inc(s_fsum, 1)
            lo(U_NSA + 7)
            lo(U_NSA + 8)
            kv_copy(inb[1], 3, 1, U_NSA + 6)
            for r in range(2):
                upper(4 + r, kblk[DH:P, 1, 2 * r:2 * r + 2, :])

            def window_lo(xk):
                dve.wait_ge(s_fhi, xk + 1)
                dve.wait_ge(s_fsum, xk + 1)
                dve.tensor_tensor(flo[:, :, :].rearrange("p t n -> p (t n)"), fsum[:, xk, :],
                                  fhi[:, :, :].rearrange("p t n -> p (t n)").bitcast(F32),
                                  ALU.subtract).then_inc(s_flo, 1)

            window_lo(0)
            lo(U_NSA + 9)
            lo(U_NSA + 10)
            chunk_q(acc[1], 0, U_NSA + 8)
            for r in range(2):
                upper(6 + r, kblk[DH:P, 1, 4 + 2 * r:6 + 2 * r, :])
            lo(U_NSA + 11)
            lo(U_NSA + 12)
            chunk_q(acc[3], 1, U_NSA + 10)
            lo(U_NSA + 13)
            lo(U_NSA + 14)
            window_lo(1)
            for r in range(4):
                q_half(8 + r, r)
            lo(U_NSA + 15)
            lo(U_NSA + 16)
            dve.wait_ge(s_biasc, 1)
            dve.wait_ge(s_cmp2, 1)
            for u in range(2):
                dve.tensor_copy(kcb[u * DH:(u + 1) * DH, :, u, :],
                                tb[0][u * DH:(u + 1) * DH, 0:GN].rearrange("p (g n) -> p g n", g=G))
            for e in range(2):
                v = tb[0][0:HN, 64 + e * DH:64 + (e + 1) * DH].unsqueeze(1).broadcast_to([HN, 8, DH])
                ins = dve.tensor_tensor(vblk[:, e], v, blkmask[:, :].unsqueeze(2).broadcast_to([HN, 8, DH]),
                                        ALU.mult)
            ins.then_inc(s_kcb, 1)
            dve.wait_ge(s_sc, 1)
            step(dve.tensor_tensor(pc, inb[0][:, 0:NT * H * NCMP],
                                   biasc.rearrange("p t h n -> p (t h n)"), ALU.add))
            pcr = pc.rearrange("p (r n) -> p r n", n=NCMP)
            step(dve.tensor_reduce(cmx[:, :], pcr, AX.X, ALU.max))
            dve.tensor_tensor(pcr, pcr, cmx[:, :].unsqueeze(2).broadcast_to([P, NT * H, NCMP]),
                              ALU.subtract).then_inc(s_csh, 1)
            dve.wait_ge(s_cexp, 1)
            step(dve.tensor_reduce(csum[:, :], pcr, AX.X, ALU.add))
            for t in range(NT):
                ins = dve.tensor_tensor(pc4[:, t], pc4[:, t],
                                        cmask01[:, t, :].unsqueeze(1).broadcast_to([P, H, NCMP]), ALU.mult)
            ins.then_inc(s_cp, 1)
            step(dve.reciprocal(cw[:, :], csum[:, :]))
            dve.wait_ge(s_gate, 1)
            step(dve.tensor_tensor(cw[:, :].rearrange("p (t h) -> p t h", t=NT),
                                   cw[:, :].rearrange("p (t h) -> p t h", t=NT),
                                   gate[:, :, :].rearrange("p t (h c) -> p t h c", c=3)[:, :, :, 0], ALU.mult))
            for t in range(NT):
                for e in range(2):
                    dve.wait_ge(s_co, 2 * t + e + 1)
                    w = cw[:, t * H + 8 * e:t * H + 8 * e + 8].unsqueeze(2).broadcast_to([P, 8, DH])
                    dve.tensor_tensor(onat[:, t, 8 * e:8 * e + 8, :],
                                      acc[2 * t + e][:, :].rearrange("p (h d) -> p h d", h=8), w,
                                      ALU.mult).then_inc(s_cog, 1)
            items(0, 16, lambda i: i % 8, lambda h: bias[:, h, P:2 * P], lambda i: 1 + i // 8)
            turned("nsa_o")
            x_add(U_NSA_OUT)
            norm("ffn1")
            ffn(1)

            norm("kv")
            turned("kv")
            lo(U_KV + 2)
            dve.wait_ge(s_tailw, 3)
            dve.tensor_tensor(gwlo[:, 0:KT * H], fl_w[:, :, :].rearrange("p k n -> p (k n)"),
                              gwhi[:, 0:KT * H].bitcast(F32), ALU.subtract).then_inc(s_tailw, 1)
            dve.wait_ge(s_tail, 2)
            for t in range(NT):
                ins = dve.tensor_copy(fl[:, t, :], acc[2 + t][:, 0:H])
            ins.then_inc(s_flc, 1)
            lo(U_KV + 3)
            lo(U_KV + 4)
            dve.wait_ge(s_used, U_KV + 2)
            dve.tensor_copy(kf[:, 1, 0:CW], acc[1][:, :]).then_inc(s_nat_d, 1)
            dve.wait_ge(s_flt, 1)
            step(dve.tensor_scalar(rfl, tb[0][0:H, 0:SEQ], bf[:, :], None, ALU.add))
            dve.scalar_tensor_tensor(out=raux, in0=rfl, scalar=-1.0, in1=rfl, op0=ALU.mult,
                                     op1=ALU.min).then_inc(s_fa, 1)
            lo(U_KV + 5)
            dve.wait_ge(s_flog, 1)
            step(dve.tensor_scalar(fcor, fexp, 1.0, None, ALU.add))
            step(dve.reciprocal(frec, fcor))
            step(dve.tensor_scalar(fcor, fcor, -1.0, None, ALU.add))
            step(dve.tensor_tensor(fcor, fexp, fcor, ALU.subtract))
            step(dve.tensor_tensor(fcor, fcor, frec, ALU.mult))
            step(dve.tensor_tensor(flog, flog, fcor, ALU.add))
            step(dve.tensor_scalar(rfl, rfl, 0.0, None, ALU.min))
            step(dve.tensor_tensor(flog, rfl, flog, ALU.subtract))
            step(dve.memset(fcor, 1.0))
            step(dve.tensor_tensor_scan(rfl, fcor, flog, 0.0, ALU.mult, ALU.add))
            dve.tensor_scalar(raux, rfl, -1.0, None, ALU.mult).then_inc(s_neg, 1)
            lo(U_KV + 6)
            dve.wait_ge(s_used, U_KV + 4)
            dve.tensor_copy(kf[:, 1, CW:2 * CW], inb[1][:, :]).then_inc(s_nat_d, 1)
            for i in range(2):
                upper(12 + i, kblk[DH:P, 1, 2 * i:2 * i + 2, :])
            lo(U_KV + 7)
            lo(U_KV + 8)
            dve.wait_ge(s_used, U_KV + 6)
            dve.tensor_copy(vf[:, 1, 0:CW], acc[1][:, :]).then_inc(s_nat_d, 1)
            for i in range(2, 4):
                upper(12 + i, kblk[DH:P, 1, 2 * i:2 * i + 2, :])
            dve.wait_ge(s_ct, 1)
            dve.tensor_copy(cq[:, :, :].rearrange("p t h -> p (t h)"), acc[2][:, 0:NT * H]).then_inc(s_cq, 1)
            lo(U_KV + 9)
            dve.wait_ge(s_used, U_KV + 8)
            dve.tensor_copy(vf[:, 1, CW:2 * CW], inb[1][:, :]).then_inc(s_nat_d, 1)
            dve.wait_ge(s_cb, 16)
            dve.wait_ge(s_cq, 1)
            cmask_h = cmask[:, :].unsqueeze(1).broadcast_to([P, H, P])
            step(dve.tensor_tensor(decay0, bias[:, :, 0:P], cmask_h, ALU.add))
            step(dve.tensor_tensor(decay0, decay0, cq[:, 0, :].unsqueeze(2).broadcast_to([P, H, P]), ALU.add))
            step(dve.tensor_tensor(bias[:, :, :], bias[:, :, :],
                                   cq[:, 1, :].unsqueeze(2).broadcast_to([P, H, SEQ]), ALU.add))
            step(dve.tensor_tensor(bias[:, :, P:SEQ], bias[:, :, P:SEQ], cmask_h, ALU.add))
            ffn(2)

            norm("fox")
            turned("fox")
            lo(U_FOXQ + 2)
            lo(U_FOXQ + 3)
            lo(U_FOXQ + 4)
            chunk_q(acc[1], 0, U_FOXQ + 2)
            lo(U_FOXQ + 5)
            lo(U_FOXQ + 6)
            chunk_q(inb[1], 1, U_FOXQ + 4)
            for i in range(4):
                q_half(16 + i, i)
            items(16, 8, lambda i: i, lambda h: decay0[:, h, :], lambda i: None)
            turned("fox_o")
            x_add(U_FOX_OUT)
            norm("ffn3")
            ffn(3)
            norm("final")

        @block.gpsimd
        def _(pool):
            steps = [0]

            def step(ins):
                steps[0] += 1
                ins.then_inc(s_pstep, 1)
                pool.wait_ge(s_pstep, steps[0])

            step(pool.memset(ident[:, :], 0.0))
            pool.affine_select(out=ident[:, :], in_=ident[:, :], compare_op=ALU.not_equal, fill=1.0, base=0,
                               pattern=[[-1, P]], channel_multiplier=1).then_inc(s_const, 1)
            pool.memset(epst[:, :], EPS)
            pool.memset(zeros[:, :], 0.0)
            step(pool.memset(cmask[:, :], 0.0))
            pool.affine_select(out=cmask[:, :], in_=cmask[:, :], compare_op=ALU.is_ge, fill=NEG, base=0,
                               pattern=[[-1, P]], channel_multiplier=1)
            step(pool.memset(cmask01[:, :, :], 1.0))
            for t in range(NT):
                pool.affine_select(out=cmask01[:, t, :], in_=cmask01[:, t, :], compare_op=ALU.is_ge, fill=0.0,
                                   base=t * P - (CMP_BLOCK - 1), pattern=[[-CMP_STRIDE, NCMP]],
                                   channel_multiplier=1)
            step(pool.memset(blkmask[:, :], 1.0))
            step(pool.affine_select(out=blkmask[:, :], in_=blkmask[:, :], compare_op=ALU.is_ge, fill=0.0,
                                    base=0, pattern=[[-NCMP, 8]], channel_multiplier=1))
            pool.affine_select(out=blkmask[:, :], in_=blkmask[:, :], compare_op=ALU.is_ge, fill=0.0,
                               base=NCMP - 1, pattern=[[NCMP, 8]], channel_multiplier=-1)
            pool.memset(kcb[:, :, :, :], 0.0)
            pool.memset(kblk[:, :, :, :], 0.0).then_inc(s_const, 1)
            small = [(gate_w[:, :, :], nsa_w_in[0, :, D + 6 * KVD:].rearrange("(k p) n -> p k n", p=P)),
                     (fl_w[:, :, :], fox_w_kvf[:, 2 * D:].rearrange("(k p) n -> p k n", p=P)),
                     (w2k[:, :, 0, :], nsa_cmp_w2[0, 0].rearrange("(c p) d -> p c d", p=P)),
                     (w2k[:, :, 1, :], nsa_cmp_w2[0, 0].rearrange("(c p) d -> p c d", p=P)),
                     (w2v[:, :, :], nsa_cmp_w2[0, 1].rearrange("(c p) d -> p c d", p=P)),
                     (bf[:, :], fox_b_f.rearrange("(h a) -> h a", a=1))]
            for dst, src in small:
                pool.dma_start(dst, src).then_inc(s_small2, 16)
            pool.wait_ge(s_setup, 1)
            starts = bucket_starts()
            for b in range(NB):
                near, far = starts[b], starts[b + 1] - 1
                pool.tensor_copy(rows[:, SEQ - 1 - far:SEQ - near],
                                 tbT[:, b:b + 1].broadcast_to([H, far - near + 1]))
            pool.memset(rows[:, SEQ:2 * SEQ], NEG).then_inc(s_rows, 1)
            pool.wait_ge(s_rows, 1)
            pool.dma_start(scratch_b.rearrange("p h m -> h p m"),
                           rows.unsqueeze(1).broadcast_to([H, P, 512])).then_inc(s_rows_out, 16)
            pool.wait_ge(s_rows_out, 16)
            pool.dma_start(bias[:, :, :], bass.AP(tensor=scratch_b.tensor, offset=P - 1,
                                                  ap=[[H * 512 - 1, P], [512, H], [1, SEQ]])).then_inc(s_bias, 16)
            step(pool.memset(biasc, NEG))
            pool.wait_ge(s_bias, 16)
            end = CMP_BLOCK - 1
            pool.tensor_copy(biasc[:, 1], bias[:, :, end:end + (NCMP - 1) * CMP_STRIDE + 1:CMP_STRIDE])
            pool.tensor_copy(biasc[:, 0, :, 0:7],
                             bias[:, :, P + end:P + end + 6 * CMP_STRIDE + 1:CMP_STRIDE]).then_inc(s_biasc, 1)
            for n in range(16):
                pool.wait_ge(s_on, n + 1)
                if n >= 8:
                    pool.wait_ge(s_oadd, n - 7)
                o = onat[:, :, 2 * (n % 8):2 * (n % 8) + 2, :]
                pool.tensor_tensor(o, o, otmp[:, n % 2], ALU.add).then_inc(s_oadd, 1)
            pool.wait_ge(s_neg, 1)
            pool.dma_start(scratch_c, raux).then_inc(s_cst, 16)
            pool.wait_ge(s_cst, 16)
            pool.dma_start(bias[:, :, :].rearrange("p h n -> p (h n)"),
                           bass.AP(tensor=scratch_c.tensor, offset=0, ap=[[0, P], [1, H * SEQ]])
                           ).then_inc(s_cb, 16)
            pool.wait_ge(s_on, 24)
            pool.dma_start(finalb, final_g.partition_broadcast(P)).then_inc(s_fg, 16)


_INS = ["x", "norm_g", "ffn_w_in", "ffn_w_out", "nsa_w_in", "nsa_cmp_pos", "nsa_cmp_w1", "nsa_cmp_w2",
        "nsa_w_out", "rel_bias", "kv_norm_g", "fox_w_kvf", "fox_b_f", "fox_w_q", "fox_w_out", "final_g"]


def kernel(**inputs):
    import concourse.bacc as bacc
    from concourse.bass_utils import run_bass_kernel_spmd

    nc = bacc.Bacc("TRN2", target_bir_lowering=False, num_devices=1)
    arrays, args = {}, []
    for name in _INS:
        a = np.ascontiguousarray(inputs[name])
        arrays[f"in_{name}"] = a
        args.append(nc.dram_tensor(f"in_{name}", a.shape, mybir.dt.from_np(a.dtype), kind="ExternalInput").ap())
    out = nc.dram_tensor("out", (1, SEQ, D), F32, kind="ExternalOutput").ap()
    yoco_trunk(nc, *args, out)
    r = run_bass_kernel_spmd(nc, [arrays], core_ids=[0])
    return r.results[0]["out"]
```

```python
import math
from contextlib import ExitStack

import numpy as np
import concourse.bass as bass
from concourse import mybir

F32 = mybir.dt.float32
F32R = mybir.dt.float32r
BF16 = mybir.dt.bfloat16
ALU = mybir.AluOpType
ACT = mybir.ActivationFunctionType
AX = mybir.AxisListType

P = 128
SEQ, D = 256, 1024
NT = SEQ // P
KT = D // P
H, DH = 16, 64
G = 4
KVD = G * DH
DFF = 2816
FC = 256
NJ = DFF // FC
CMP_BLOCK, CMP_STRIDE, CMP_HIDDEN = 32, 16, 256
NCMP = (SEQ - CMP_BLOCK) // CMP_STRIDE + 1
GN = G * NCMP
HN = 8 * NCMP
NB, MAXD = 32, 128
NG = 3 * H
EPS = 1e-6
NEG = -1e30
SCALE = DH ** -0.5
CW = 512
UNIT = 4 * CW
RING = 3

FFN_UNITS = 3 * NJ
U_FFN0 = 0
U_NSA = U_FFN0 + FFN_UNITS
U_CMP = U_NSA + 10
U_NSA_OUT = U_CMP + 4
U_FFN1 = U_NSA_OUT + 4
U_KV = U_FFN1 + FFN_UNITS
U_FFN2 = U_KV + 8
U_FOXQ = U_FFN2 + FFN_UNITS
U_FOX_OUT = U_FOXQ + 4
U_FFN3 = U_FOX_OUT + 4
U_END = U_FFN3 + FFN_UNITS
U_FFN = [U_FFN0, U_FFN1, U_FFN2, U_FFN3]

TURNS = ["ffn0", "nsa", "ffn1", "kv", "ffn2", "fox", "ffn3"]
GAIN = {"ffn0": 0, "nsa": 1, "ffn1": 2, "ffn2": 3, "fox": 4, "ffn3": 5, "kv": 6}
NORMS = ["ffn0", "nsa", "ffn1", "kv", "fox", "ffn3", "final"]
ADDS = ["ffn0", "nsa", "ffn1", "ffn2", "fox", "ffn3"]
TILE0 = ["ffn0", "nsa", "ffn1", "kv", "ffn2", "fox", "ffn3"]
ADD_BEFORE = {"nsa": "ffn0", "ffn1": "nsa", "kv": "ffn1", "fox": "ffn2", "ffn3": "fox", "final": "ffn3"}


def added(name, t, half):
    before = ADD_BEFORE[name]
    return 4 * ADDS.index(before) + (2 * t + half if before.startswith("ffn") else 2 * half + t) + 1


CMP_PIECES = [(0, 0), (1, 0), (0, 1), (1, 1)]


def bucket_starts():
    dist = np.arange(SEQ)
    exact = NB // 2
    scaled = np.log(np.maximum(dist, 1).astype(np.float32) / np.float32(exact)).astype(np.float32)
    scaled = scaled / np.float32(math.log(MAXD / exact))
    large = np.minimum(exact + (scaled * np.float32(NB - exact)).astype(np.int32), NB - 1)
    bucket = np.where(dist < exact, dist, large)
    return [int(np.argmax(bucket == b)) for b in range(NB)] + [SEQ]


def yoco_trunk(nc, x, norm_g, ffn_w_in, ffn_w_out, nsa_w_in, nsa_cmp_pos, nsa_cmp_w1, nsa_cmp_w2,
               nsa_w_out, rel_bias, kv_norm_g, fox_w_kvf, fox_b_f, fox_w_q, fox_w_out, final_g, out):
    ctx = ExitStack()
    with ctx:
        def sb(name, shape, dt=F32):
            return ctx.enter_context(nc.sbuf_tensor(name, shape, dt))

        def ps(name):
            return ctx.enter_context(nc.psum_tensor(name, [P, 512], F32))

        def sem(name):
            return ctx.enter_context(nc.semaphore(name))

        raw = [sb(f"raw{s}", [P, UNIT]) for s in range(RING)]
        whi = [sb(f"whi{s}", [P, UNIT], F32R) for s in range(RING)]
        wlo = [sb(f"wlo{s}", [P, UNIT], F32R) for s in range(RING)]
        xs = sb("xs", [P, NT, D])
        xn = sb("xn", [P, NT, D])
        thi = sb("thi", [P, KT, SEQ], F32R)
        tlo = sb("tlo", [P, KT, SEQ], F32R)
        ghi = sb("ghi", [P, 2, SEQ], F32R)
        glo = sb("glo", [P, 2, SEQ], F32R)
        sa = sb("sa", [P, NT, FC])
        gg = sb("gg", [P, NT, FC])
        qT = sb("qT", [P, H // 2, SEQ])
        nat = sb("nat", [P, 5120])
        kblk = sb("kblk", [P, 2, 8, SEQ])
        bias = sb("bias", [P, H, SEQ])
        work = sb("work", [P, 3072])
        fhi = sb("fhi", [P, 16, GN], F32R)
        flo = sb("flo", [P, 16, GN], F32R)
        low = sb("low", [P, 2048])
        gate_w = sb("gate_w", [P, KT, NG])
        fl_w = sb("fl_w", [P, KT, H])
        w2k = sb("w2k", [P, 2, 2, DH])
        w2v = sb("w2v", [P, 2, DH])
        ident = sb("ident", [P, P])
        cmask = sb("cmask", [P, P])
        gains = sb("gains", [P, 56])
        posT = sb("posT", [P, 32])
        tbT = sb("tbT", [H, NB])
        cmask01 = sb("cmask01", [P, NT, NCMP])
        blkmask = sb("blkmask", [HN, 8])
        kcb = sb("kcb", [P, G, 2, NCMP])
        zeros = sb("zeros", [32, P], BF16)
        epst = sb("epst", [P, 1])
        ss = sb("ss", [P, 2 * NT])
        rstd = sb("rstd", [P, NT])
        rstd_q = sb("rstd_q", [P, 1])
        mx = sb("mx", [P, 4, 4])
        nmx = sb("nmx", [P, 4, 4])
        lsum = sb("lsum", [P, 4, 4])
        linv = sb("linv", [P, 4])
        lw = sb("lw", [P, 4])
        gate = sb("gate", [P, NT, NG])
        cmx = sb("cmx", [P, NT * H])
        csum = sb("csum", [P, NT * H])
        cw = sb("cw", [P, NT * H])
        cq = sb("cq", [P, NT, H])
        fl = sb("fl", [P, NT, H])
        bf = sb("bf", [H, 1])
        rel_s = sb("rel_s", [NB, H])

        kd = nat[:, 0:4096].rearrange("p (t k g u d) -> p t k g u d", t=NT, k=4, g=G, u=2)
        vd = nat[:, 4096:5120].rearrange("p (t a n) -> p t a n", t=NT, a=2)
        kf = nat[:, 0:2048].rearrange("p (t n) -> p t n", t=NT)
        vf = nat[:, 2048:4096].rearrange("p (t n) -> p t n", t=NT)
        k2 = work[:, 0:1024].rearrange("p (x g m) -> p x g m", x=2, g=G)
        fsum = work[:, 1024:1024 + 2 * 16 * GN].rearrange("p (x c) -> p x c", x=2)
        hidk = work[:, 2304:2304 + 2 * GN].rearrange("p (c n) -> p c n", c=2)
        hidv = work[:, 2432:2432 + 4 * HN].rearrange("p (c g r n) -> p c g r n", c=2, g=G, r=4)
        hidv2 = work[:, 2432:2432 + 4 * HN].rearrange("p (c n) -> p c n", c=2)
        probs = work[:, 0:1536].rearrange("p (b n) -> p b n", b=2)
        pT = work[:, 1536:3072].rearrange("p (b h n) -> p b h n", b=2, h=2)
        vblk = low[0:HN, 0:1024].rearrange("p (e h d) -> p e h d", e=2, h=8)
        pcT = low[0:HN, 1024:1536].rearrange("p (c n) -> p c n", c=4)
        biasc = low[:, 1536:1536 + NT * H * NCMP].rearrange("p (t h n) -> p t h n", t=NT, h=H)
        decay0 = low[:, :].rearrange("p (h n) -> p h n", h=H)
        pc = sa[:, :, :].rearrange("p t n -> p (t n)")[:, 0:NT * H * NCMP]
        pc4 = pc.rearrange("p (t h n) -> p t h n", t=NT, h=H)
        ctmp = low[:, 1536:2048].rearrange("p (h d) -> p h d", h=8)
        tflat_hi = thi[:, :, :].rearrange("p k n -> p (k n)")[:, 0:16 * GN]
        tflat_lo = tlo[:, :, :].rearrange("p k n -> p (k n)")[:, 0:16 * GN]
        win_hi = [fhi[:, :, :].rearrange("p t n -> p (t n)"), tflat_hi]
        win_lo = [flo[:, :, :].rearrange("p t n -> p (t n)"), tflat_lo]
        otmp = gg[:, :, :].rearrange("p b (t h d) -> p b t h d", t=2, h=2)
        ghi_last = fhi[:, :, :].rearrange("p t n -> p (t n)")[:, 0:2 * SEQ].rearrange("p (k n) -> p k n", k=2)
        glo_last = flo[:, :, :].rearrange("p t n -> p (t n)")[:, 0:2 * SEQ].rearrange("p (k n) -> p k n", k=2)
        gwhi = ghi[:, :, :].rearrange("p a n -> p (a n)")
        gwlo = glo[:, :, :].rearrange("p a n -> p (a n)")
        onat = xn[:, :, :].rearrange("p t (h d) -> p t h d", h=H)
        rows = low[0:H, 0:512]
        rfl = rows[:, 0:SEQ]
        raux = rows[:, SEQ:2 * SEQ]
        finalb = work[:, 0:D]
        fexp = work[0:H, 0:SEQ]
        flog = work[0:H, SEQ:2 * SEQ]
        fcor = work[0:H, 2 * SEQ:3 * SEQ]
        frec = work[0:H, 3 * SEQ:4 * SEQ]

        acc = [ps(f"acc{i}") for i in range(4)]
        inb = [ps(f"inb{i}") for i in range(2)]
        tb = [ps(f"tb{i}") for i in range(2)]
        tbanks = [tb[0], tb[1], acc[2], acc[3]]

        s_raw = [sem(f"raw_loaded{s}") for s in range(RING)]
        s_hi = sem("unit_hi")
        s_lo = sem("unit_lo")
        s_used = sem("unit_used")
        s_x = [sem(f"x_loaded{t}") for t in range(NT)]
        s_small = [sem(f"small_loaded{i}") for i in range(4)]
        s_small2 = sem("small_loaded_later")
        s_const = sem("consts")
        s_setup_t = sem("setup_turned")
        s_setup = sem("setup_copied")
        s_rows = sem("bias_rows")
        s_rows_out = sem("bias_rows_stored")
        s_bias = sem("bias_loaded")
        s_biasc = sem("biasc_ready")
        s_sumsq = sem("sumsq")
        s_rms = sem("rms")
        s_rstd = sem("rstd_ready")
        s_tt = sem("turned")
        s_thi = sem("turned_hi")
        s_tlo = sem("turned_lo")
        s_silu = sem("silu_done")
        s_g = sem("hidden_ready")
        s_gt = sem("hidden_turned")
        s_ghi = sem("hidden_hi")
        s_glo = sem("hidden_lo")
        s_in0 = sem("last_hidden_tile0")
        s_tile0 = sem("tile0_done")
        s_ot = sem("o_turned")
        s_ohi = sem("o_hi")
        s_olo = sem("o_lo")
        s_xadd = sem("x_added")
        s_nat_a = sem("chunk_copied_act")
        s_nat_d = sem("chunk_copied_dve")
        s_rt = sem("round_turned")
        s_ra = sem("round_copied_act")
        s_rd = sem("round_copied_dve")
        s_tailw = sem("small_split")
        s_tail = sem("tail_done")
        s_gate = sem("gate_ready")
        s_fsum = sem("windows_summed")
        s_fhi = sem("windows_hi")
        s_flo = sem("windows_lo")
        s_hid = sem("cmp_hidden")
        s_cmp2 = sem("cmp_out")
        s_kcb = sem("cmp_kv_ready")
        s_sc = sem("cmp_scores")
        s_csh = sem("cmp_shifted")
        s_cexp = sem("cmp_exp")
        s_cp = sem("cmp_probs")
        s_cpt = sem("cmp_probs_turned")
        s_cpc = sem("cmp_probs_copied")
        s_co = sem("cmp_values")
        s_cog = sem("cmp_gated")
        s_qk = sem("scores")
        s_max = sem("max_done")
        s_nmax = sem("negmax_ready")
        s_exp = sem("probs_ready")
        s_pt = sem("probs_turned")
        s_pta = sem("pT_act")
        s_ptd = sem("pT_dve")
        s_pv = sem("values_done")
        s_on = sem("o_gated")
        s_cadd = sem("cmp_added")
        s_oadd = sem("o_added")
        s_flc = sem("fl_copied")
        s_flt = sem("fl_turned")
        s_fa = sem("fl_abs_ready")
        s_fexp = sem("fl_exp_act")
        s_flog = sem("fl_log")
        s_neg = sem("neg_c_ready")
        s_cst = sem("neg_c_stored")
        s_cb = sem("neg_c_loaded")
        s_ct = sem("c_turned")
        s_cq = sem("c_by_query")
        s_decay = sem("decay_ready")
        s_fg = sem("final_gain")
        s_y = sem("y_ready")
        s_out = sem("out_stored")
        s_step = sem("dve_step")
        s_pstep = sem("pool_step")

        scratch_b = nc.dram_tensor("bias_rows_dram", [P, H, 512], F32).ap()
        scratch_c = nc.dram_tensor("neg_c_dram", [H, SEQ], F32).ap()

        block = ctx.enter_context(nc.Block())

        @block.sync
        def _(sp):
            def load(u, halves, number=None):
                if number is not None or u >= RING:
                    sp.wait_ge(s_lo, (u if number is None else number) - RING + 1)
                for dst, src in halves:
                    sp.dma_start(dst, src).then_inc(s_raw[u % RING], 16)

            def ffn_in(f, j, half, u):
                w = ffn_w_in[f // 2, f % 2][half * 512:(half + 1) * 512, :]
                w = w.rearrange("(k p) n -> p k n", p=P)
                r = raw[u % RING][:, :].rearrange("p (k n) -> p k n", k=4)
                return [(r[:, :, 0:FC], w[:, :, bass.ds(j * FC, FC)]),
                        (r[:, :, FC:2 * FC], w[:, :, bass.ds(j * FC + DFF, FC)])]

            def ffn_out(f, j, u):
                w = ffn_w_out[f // 2, f % 2]
                r = raw[u % RING][:, :].rearrange("p (k n) -> p k n", k=2)
                return [(r[:, k, :], w[bass.ds(j * FC + k * P, P), :]) for k in range(2)]

            def ffn(f):
                b = U_FFN[f]
                for i in range(2):
                    load(b + i, ffn_in(f, 0, i, b + i))
                with sp.Fori(1, NJ) as j:
                    for i in range(3):
                        u = b + 2 + i
                        halves = ffn_in(f, j, i, u) if i < 2 else ffn_out(f, j - 1, u)
                        load(u, halves, 3 * (j - 1) + max(u, RING))
                u = b + FFN_UNITS - 1
                load(u, ffn_out(f, NJ - 1, u))

            def matrix(w, b, chunks):
                for c, col in enumerate(chunks):
                    for i in range(2):
                        u = b + 2 * c + i
                        wr = w[i * 512:(i + 1) * 512, col:col + CW].rearrange("(k p) n -> p k n", p=P)
                        r = raw[u % RING][:, :].rearrange("p (k n) -> p k n", k=4)
                        load(u, [(r[:, 0:2], wr[:, 0:2]), (r[:, 2:4], wr[:, 2:4])])

            for t in range(NT):
                sp.dma_start(xs[:, t, :], x[0, t * P:(t + 1) * P, :]).then_inc(s_x[t], 16)
            ffn(0)
            matrix(nsa_w_in[0], U_NSA, [D, D + 2 * KVD, D + 4 * KVD, 0, CW])
            for xk in range(2):
                for i in range(2):
                    u = U_CMP + 2 * xk + i
                    wr = nsa_cmp_w1[0, xk, i * 1024:(i + 1) * 1024, :].rearrange("(k p) n -> p k n", p=P)
                    r = raw[u % RING][:, :].rearrange("p (k n) -> p k n", k=8)
                    load(u, [(r[:, 0:4], wr[:, 0:4]), (r[:, 4:8], wr[:, 4:8])])
            matrix(nsa_w_out[0], U_NSA_OUT, [0, CW])
            ffn(1)
            matrix(fox_w_kvf, U_KV, [0, CW, 2 * CW, 3 * CW])
            ffn(2)
            matrix(fox_w_q[0], U_FOXQ, [0, CW])
            matrix(fox_w_out[0], U_FOX_OUT, [0, CW])
            ffn(3)
            for t in range(NT):
                sp.wait_ge(s_y, t + 1)
                sp.dma_start(out[0, t * P:(t + 1) * P, :], xn[:, t, :]).then_inc(s_out, 16)
            sp.wait_ge(s_out, 16 * NT)

        @block.tensor
        def _(pe):
            def turn(name, t):
                for e in range(2):
                    if name == "ffn0":
                        pe.wait_ge(s_x[t], 16)
                    elif name != "ffn2":
                        pe.wait_ge(s_xadd, added(name, t, e))
                    for k in range(4):
                        mm = pe.transpose(tbanks[2 * t + e][:, k * P:(k + 1) * P],
                                          xs[:, t, (4 * e + k) * P:(4 * e + k + 1) * P], ident[:, :])
                    mm.then_inc(s_tt, 1)

            def three(o, lh, ll, rh, rl, start, stop):
                pe.matmul(o, lh, rh, start=start, stop=False, skip_group_check=True)
                pe.matmul(o, lh, rl, start=False, stop=False, skip_group_check=True)
                return pe.matmul(o, ll, rh, start=False, stop=stop, skip_group_check=True)

            def rows4(slot, half, t, o):
                tok = slice(t * P, (t + 1) * P)
                for k in range(4):
                    kk = 4 * half + k
                    mm = three(o, thi[:, kk, tok], tlo[:, kk, tok], whi[slot][:, k * CW:(k + 1) * CW],
                               wlo[slot][:, k * CW:(k + 1) * CW], kk == 0, kk == KT - 1)
                return mm

            def unit_in(slot, half, banks, need):
                pe.wait_ge(s_lo, need)
                for t in range(NT):
                    mm = rows4(slot, half, t, banks[t][:, :])
                mm.then_inc(s_used, 1)

            def unit(b, c, half, banks):
                u = b + 2 * c + half
                unit_in(u % RING, half, banks, u + 1)

            def first_chunk(b, banks, name):
                for t in range(NT):
                    for half in range(2):
                        u = b + half
                        pe.wait_ge(s_lo, u + 1)
                        pe.wait_ge(s_tlo, 4 * TURNS.index(name) + 2 * t + half + 1)
                        mm = rows4(u % RING, half, t, banks[t][:, :])
                        if t == NT - 1:
                            mm.then_inc(s_used, 1)
                        elif half == 0:
                            turn(name, 1)

            def last_chunk(b, banks, following):
                for t in range(NT):
                    for half in range(2):
                        u = b + half
                        pe.wait_ge(s_lo, u + 1)
                        mm = rows4(u % RING, half, t, banks[t][:, :])
                        if t == NT - 1:
                            mm.then_inc(s_used, 1)
                            if half == 0:
                                turn(following, 0)
                    if t == 0:
                        mm.then_inc(s_tile0, 1)

            def out_part(slot, t, k, last=False):
                h_hi, h_lo = (ghi_last, glo_last) if last else (ghi, glo)
                tok = slice(t * P, (t + 1) * P)
                for n in range(2):
                    col = slice(k * D + n * CW, k * D + (n + 1) * CW)
                    mm = three(acc[2 * t + n][:, :], h_hi[:, k, tok], h_lo[:, k, tok],
                               whi[slot][:, col], wlo[slot][:, col], False, last and k == 1)
                return mm

            def hidden_turn(need, tiles=range(NT)):
                pe.wait_ge(s_g, need)
                for k in range(2):
                    for t in tiles:
                        mm = pe.transpose(tb[0][:, k * SEQ + t * P:k * SEQ + (t + 1) * P],
                                          gg[:, t, k * P:(k + 1) * P], ident[:, :])
                mm.then_inc(s_gt, 1)

            def ffn(f, following=None):
                b, n0, h0 = U_FFN[f], NJ * f, (NJ + 1) * f
                first_chunk(b, inb, f"ffn{f}")
                for a in acc:
                    pe.matmul(a[:, :], zeros[:, :], zeros[:, :].unsqueeze(1).broadcast_to([32, 4, P]),
                              start=True, stop=False, skip_group_check=True)
                hidden_turn(2 * (n0 + 1))
                with pe.Fori(1, NJ - 1) as j:
                    for half in range(2):
                        u = b + 2 + half
                        unit_in(u % RING, half, inb, 3 * (j - 1) + u + 1)
                    pe.wait_ge(s_lo, 3 * (j - 1) + b + 5)
                    pe.wait_ge(s_glo, j + h0)
                    slot = (b + 4) % RING
                    out_part(slot, 0, 0)
                    out_part(slot, 0, 1)
                    out_part(slot, 1, 0)
                    hidden_turn(2 * j + 2 * n0 + 2)
                    out_part(slot, 1, 1).then_inc(s_used, 1)
                u = b + 3 * (NJ - 1) - 1
                for t in range(NT):
                    for half in range(2):
                        pe.wait_ge(s_lo, u + half + 1)
                        mm = rows4((u + half) % RING, half, t, inb[t][:, :])
                        if t == NT - 1:
                            mm.then_inc(s_used, 1)
                            if half == 0:
                                pe.wait_ge(s_glo, h0 + NJ - 1)
                                hidden_turn(2 * (n0 + NJ) - 1, [0])
                    if t == 0:
                        mm.then_inc(s_in0, 1)
                for t in range(NT):
                    pe.wait_ge(s_lo, u + 3)
                    out_part((u + 2) % RING, t, 0)
                    mm = out_part((u + 2) % RING, t, 1)
                    pe.wait_ge(s_lo, u + 4)
                    pe.wait_ge(s_glo, h0 + NJ + t)
                    if t == 0:
                        out_part((u + 3) % RING, t, 0, True)
                        out_part((u + 3) % RING, t, 1, True).then_inc(s_tile0, 1)
                        hidden_turn(2 * (n0 + NJ), [1])
                    else:
                        mm.then_inc(s_used, 1)
                        if following:
                            turn(following, 0)
                        out_part((u + 3) % RING, t, 0, True)
                        out_part((u + 3) % RING, t, 1, True).then_inc(s_used, 1)

            def tail(cols):
                for t in range(NT):
                    tok = slice(t * P, (t + 1) * P)
                    for k in range(KT):
                        mm = three(acc[2 + t][:, 0:cols], thi[:, k, tok], tlo[:, k, tok],
                                   gwhi[:, k * cols:(k + 1) * cols], gwlo[:, k * cols:(k + 1) * cols],
                                   k == 0, k == KT - 1)
                mm.then_inc(s_tail, 1)

            def round_(r, parts):
                if r % 12 >= 2:
                    pe.wait_ge(s_ra, r - 1)
                    pe.wait_ge(s_rd, r - 1)
                for k, src in enumerate(parts):
                    for t in range(NT):
                        mm = pe.transpose(tb[r % 2][:, k * SEQ + t * P:k * SEQ + (t + 1) * P],
                                          src(t), ident[:, :])
                mm.then_inc(s_rt, 1)

            def copied(n):
                pe.wait_ge(s_nat_a, n)
                pe.wait_ge(s_nat_d, n)

            def kv_round(r, kind, g0):
                round_(r, [lambda t, g=g: kd[:, t, kind, g].rearrange("p u d -> p (u d)")
                           for g in (g0, g0 + 1)])

            def pair_round(r, m, i):
                round_(r, [lambda t, p=p: m[:, t, p * P:(p + 1) * P] for p in (2 * i, 2 * i + 1)])

            def scores(n, kidx, p):
                s1, s0 = acc[2 * (n % 2)], acc[2 * (n % 2) + 1]
                pe.matmul(s1[:, :], qT[:, p, P:2 * P], kblk[:, :, kidx, :], start=True,
                          stop=True).then_inc(s_qk, 1)
                pe.matmul(s0[:, 0:2 * P], qT[:, p, 0:P], kblk[:, :, kidx, 0:P], start=True,
                          stop=True).then_inc(s_qk, 1)

            def turn_probs(n, n_first):
                pe.wait_ge(s_exp, 4 * n + 4)
                if n > n_first:
                    pe.wait_ge(s_pta, n)
                    pe.wait_ge(s_ptd, n)
                for h in range(2):
                    parts = [h * P, 2 * P + h * SEQ, 2 * P + h * SEQ + P]
                    for i, c in enumerate(parts):
                        mm = pe.transpose(tb[h][:, i * P:(i + 1) * P], probs[:, n % 2, c:c + P],
                                          ident[:, :])
                    mm.then_inc(s_pt, 1)

            def values(n, n_first, v):
                pe.wait_ge(s_pta, n + 1)
                pe.wait_ge(s_ptd, n + 1)
                if n > n_first:
                    pe.wait_ge(s_on, n)
                for h in range(2):
                    o = inb[0]
                    mm = pe.matmul(o[:, h * DH:(h + 1) * DH], pT[:, n % 2, h, 0:P], v(0, h),
                                   start=True, stop=True)
                    for k in range(2):
                        mm = pe.matmul(o[:, P + h * DH:P + (h + 1) * DH],
                                       pT[:, n % 2, h, (1 + k) * P:(2 + k) * P], v(k, h),
                                       start=k == 0, stop=k == 1)
                mm.then_inc(s_pv, 1)

            def items(n0, kidx, v, count, between):
                for i in range(count + 1):
                    if i + 1 < count:
                        scores(n0 + i + 1, kidx(i + 1), (i + 1) % 8)
                    if i < count:
                        turn_probs(n0 + i, n0)
                    if i >= 1:
                        values(n0 + i - 1, n0, v(i - 1))
                    if i in between:
                        between[i]()

            def turn_o(g, first):
                if g:
                    pe.wait_ge(s_olo, first + g)
                if first:
                    pe.wait_ge(s_on, 16 + 2 * g + 2)
                else:
                    pe.wait_ge(s_oadd, 2 * g + 2)
                for i in range(2):
                    for t in range(NT):
                        p = 2 * g + i
                        mm = pe.transpose(inb[1][:, i * SEQ + t * P:i * SEQ + (t + 1) * P],
                                          xn[:, t, p * P:(p + 1) * P], ident[:, :])
                mm.then_inc(s_ot, 1)

            def project_out(b, first, following):
                pe.wait_ge(s_lo, b + 1)
                pe.wait_ge(s_olo, first + 2)
                rows4(b % RING, 0, 0, acc[0][:, :])
                turn_o(3, first)
                rows4(b % RING, 0, 1, acc[1][:, :]).then_inc(s_used, 1)
                pe.wait_ge(s_olo, first + 4)
                unit(b, 0, 1, acc[0:2])
                last_chunk(b + 2, acc[2:4], following)

            pe.wait_ge(s_const, 1)
            for s in s_small:
                pe.wait_ge(s, 16)
            pe.transpose(inb[1][:, 0:56], work[0:56, 0:P], ident[0:56, 0:56])
            pe.transpose(inb[1][:, 64:96], work[0:32, P:2 * P], ident[0:32, 0:32])
            pe.transpose(inb[1][0:H, 96:128], rel_s[:, :], ident[0:NB, 0:NB]).then_inc(s_setup_t, 1)
            turn("ffn0", 0)
            pe.wait_ge(s_setup, 1)
            pe.wait_ge(s_const, 2)
            ffn(0, "nsa")

            first_chunk(U_NSA, inb, "nsa")
            unit(U_NSA, 1, 0, acc[0:2])
            copied(1)
            kv_round(0, 0, 0)
            kv_round(1, 0, 2)
            unit(U_NSA, 1, 1, acc[0:2])
            kv_round(2, 1, 0)
            kv_round(3, 1, 2)
            pe.wait_ge(s_tailw, 2)
            tail(NG)
            unit(U_NSA, 2, 0, inb)
            copied(2)
            kv_round(4, 2, 0)
            kv_round(5, 2, 2)
            unit(U_NSA, 2, 1, inb)
            unit(U_NSA, 3, 0, acc[0:2])
            copied(3)
            kv_round(6, 3, 0)
            kv_round(7, 3, 2)
            unit(U_NSA, 3, 1, acc[0:2])
            pe.wait_ge(s_gate, 1)
            unit(U_NSA, 4, 0, acc[2:4])
            copied(4)
            pair_round(8, xn, 0)
            pair_round(9, xn, 1)
            unit(U_NSA, 4, 1, acc[2:4])

            def compress(xk, i):
                if i == 0:
                    pe.wait_ge(s_flo, xk + 1)
                u = U_CMP + 2 * xk + i
                banks = inb if xk == 0 else acc[2:4]
                pe.wait_ge(s_lo, u + 1)
                for k in range(8):
                    c = 8 * i + k
                    for hh in range(2):
                        col = slice(k * CMP_HIDDEN + hh * P, k * CMP_HIDDEN + (hh + 1) * P)
                        win = slice(c * GN, (c + 1) * GN)
                        mm = three(banks[hh][:, 0:GN], whi[u % RING][:, col], wlo[u % RING][:, col],
                                   win_hi[xk][:, win], win_lo[xk][:, win], c == 0, c == 15)
                mm.then_inc(s_used, 1)

            compress(0, 0)
            copied(5)
            pair_round(10, xn, 2)
            pair_round(11, xn, 3)
            compress(0, 1)
            compress(1, 0)
            compress(1, 1)
            pe.wait_ge(s_ra, 12)
            pe.wait_ge(s_rd, 12)

            def cmp_layer2():
                for c in range(2):
                    pe.matmul(inb[1][:, 0:GN], w2k[:, c].rearrange("p u d -> p (u d)"), hidk[:, c, :],
                              start=c == 0, stop=c == 1)
                for e in range(2):
                    for c in range(2):
                        mm = pe.matmul(inb[1][0:HN, 64 + e * DH:64 + (e + 1) * DH],
                                       hidv2[:, c, e * HN:(e + 1) * HN], w2v[:, c, :],
                                       start=c == 0, stop=c == 1)
                mm.then_inc(s_cmp2, 1)

            def cmp_scores():
                pe.wait_ge(s_kcb, 1)
                for t in range(NT):
                    for p in range(H // 2):
                        c0 = t * H * NCMP + 2 * p * NCMP
                        mm = pe.matmul(inb[1][:, c0:c0 + 2 * NCMP], qT[:, p, t * P:(t + 1) * P],
                                       kcb[:, p // 2].rearrange("p u n -> p (u n)"), start=True, stop=True)
                mm.then_inc(s_sc, 1)

            def cmp_turn():
                pe.wait_ge(s_cp, 1)
                for t in range(NT):
                    for e in range(2):
                        c0 = (t * H + 8 * e) * NCMP
                        mm = pe.transpose(inb[1][0:HN, (2 * t + e) * P:(2 * t + e + 1) * P],
                                          pc[:, c0:c0 + HN], ident[:, :])
                mm.then_inc(s_cpt, 1)

            def cmp_values(c):
                t, e = CMP_PIECES[c]
                if c == 0:
                    pe.wait_ge(s_cpc, 1)
                else:
                    pe.wait_ge(s_cog, c)
                pe.matmul(inb[1][:, :], pcT[:, 2 * t + e, :], vblk[:, e].rearrange("p h d -> p (h d)"),
                          start=True, stop=True).then_inc(s_co, 1)

            scores(0, 0, 0)
            pe.wait_ge(s_hid, 4)
            cmp_layer2()
            items(0, lambda i: i // 2, lambda i: (lambda k, h: vd[:, k, i // 8, (i % 8 // 2) * DH:
                                                              (i % 8 // 2 + 1) * DH]), 16,
                  {1: cmp_scores, 4: cmp_turn, 6: lambda: cmp_values(0), 7: lambda: cmp_values(1),
                   8: lambda: cmp_values(2), 9: lambda: cmp_values(3), 12: lambda: turn_o(0, 0),
                   14: lambda: turn_o(1, 0), 16: lambda: turn_o(2, 0)})
            project_out(U_NSA_OUT, 0, "ffn1")
            ffn(1, "kv")

            first_chunk(U_KV, acc[0:2], "kv")
            pe.wait_ge(s_tailw, 4)
            tail(H)
            unit(U_KV, 1, 0, inb)
            pe.wait_ge(s_flc, 1)
            for t in range(NT):
                mm = pe.transpose(tb[0][0:H, t * P:(t + 1) * P], fl[:, t, :], ident[:, :])
            mm.then_inc(s_flt, 1)
            unit(U_KV, 1, 1, inb)
            copied(6)
            pe.wait_ge(s_fa, 1)
            pair_round(12, kf, 0)
            pair_round(13, kf, 1)
            unit(U_KV, 2, 0, acc[0:2])
            copied(7)
            pair_round(14, kf, 2)
            pair_round(15, kf, 3)
            unit(U_KV, 2, 1, acc[0:2])
            pe.wait_ge(s_neg, 1)
            for t in range(NT):
                mm = pe.transpose(acc[2][:, t * H:(t + 1) * H], rfl[:, t * P:(t + 1) * P],
                                  ident[0:H, 0:H])
            mm.then_inc(s_ct, 1)
            pe.wait_ge(s_ra, 16)
            pe.wait_ge(s_rd, 16)
            pe.wait_ge(s_cq, 1)
            last_chunk(U_KV + 6, inb, "ffn2")
            copied(9)
            ffn(2, "fox")

            first_chunk(U_FOXQ, acc[0:2], "fox")
            unit(U_FOXQ, 1, 0, inb)
            copied(10)
            pair_round(16, xn, 0)
            pair_round(17, xn, 1)
            unit(U_FOXQ, 1, 1, inb)
            pe.wait_ge(s_ra, 17)
            pe.wait_ge(s_rd, 17)
            scores(16, 0, 0)
            copied(11)
            pair_round(18, xn, 2)
            pair_round(19, xn, 3)
            pe.wait_ge(s_ra, 20)
            pe.wait_ge(s_rd, 20)
            items(16, lambda i: i, lambda i: (lambda k, h: vf[:, k, (2 * i + h) * DH:(2 * i + h + 1) * DH]), 8,
                  {3: lambda: turn_o(0, 4), 5: lambda: turn_o(1, 4), 7: lambda: turn_o(2, 4)})
            project_out(U_FOX_OUT, 4, "ffn3")
            ffn(3)

        @block.scalar
        def _(act):
            def hi(u):
                if u >= U_END:
                    return
                act.wait_ge(s_raw[u % RING], 32 * (u // RING + 1))
                if u >= RING:
                    act.wait_ge(s_used, u - RING + 1)
                act.copy(whi[u % RING][:, :], raw[u % RING][:, :]).then_inc(s_hi, 1)

            def hi_loop(u, j):
                act.wait_ge(s_raw[u % RING], 32 * (j - 1) + 32 * (u // RING + 1))
                act.wait_ge(s_used, 3 * (j - 1) + u - RING + 1)
                act.copy(whi[u % RING][:, :], raw[u % RING][:, :]).then_inc(s_hi, 1)

            def squares(name, t):
                if name == "ffn0":
                    act.wait_ge(s_x[t], 16)
                else:
                    act.wait_ge(s_xadd, max(added(name, t, 0), added(name, t, 1)))
                act.activation(xn[:, t, :], xs[:, t, :], ACT.Square,
                               accum_out=ss[:, t:t + 1]).then_inc(s_sumsq, 1)

            def rms(name, tiles=slice(0, NT)):
                act.wait_ge(s_sumsq, NT * NORMS.index(name) + tiles.stop)
                act.activation(ss[:, NT + tiles.start:NT + tiles.stop], ss[:, tiles], ACT.Sqrt,
                               bias=epst[:, :], scale=1.0 / D).then_inc(s_rms, 1)

            def normed(name):
                act.wait_ge(s_rstd, NORMS.index(name) + 1)

            def turned(name, t):
                tok = slice(t * P, (t + 1) * P)
                for e in range(2):
                    bank = tbanks[2 * t + e]
                    act.wait_ge(s_tt, 4 * TURNS.index(name) + 2 * t + e + 1)
                    for k in range(4):
                        g = GAIN[name] * KT + 4 * e + k
                        ins = act.mul(thi[:, 4 * e + k, tok], bank[:, k * P:(k + 1) * P], gains[:, g:g + 1])
                    ins.then_inc(s_thi, 1)

            def o_hi(g, first):
                act.wait_ge(s_ot, first + g + 1)
                act.copy(thi[:, 2 * g:2 * g + 2, :].rearrange("p k n -> p (k n)"),
                         inb[1][:, :]).then_inc(s_ohi, 1)

            def boundary(name, u):
                squares(name, 0)
                turned(name, 0)
                hi(u)
                squares(name, 1)
                turned(name, 1)
                hi(u + 1)
                rms(name)
                normed(name)

            def silu_tile(t):
                act.activation(sa[:, t, :], inb[t][:, 0:FC], ACT.Silu, scale=rstd[:, t:t + 1]).then_inc(s_silu, 1)

            def silu(used):
                act.wait_ge(s_used, used)
                for t in range(NT):
                    silu_tile(t)

            def hidden_hi(n):
                act.wait_ge(s_gt, n)
                act.copy(ghi[:, :, :].rearrange("p k n -> p (k n)"), tb[0][:, :]).then_inc(s_ghi, 1)

            def hidden_last_hi(n, t):
                act.wait_ge(s_gt, n)
                tok = slice(t * P, (t + 1) * P)
                act.copy(ghi_last[:, :, tok],
                         tb[0][:, :].rearrange("p (k n) -> p k n", k=2)[:, :, tok]).then_inc(s_ghi, 1)

            def ffn(f):
                b, h0 = U_FFN[f], (NJ + 1) * f
                hi(b + 3)
                silu(b + 2)
                hi(b + 4)
                with act.Fori(1, NJ - 1) as j:
                    act.wait_ge(s_used, 3 * (j - 1) + b + 2)
                    hidden_hi(j + h0)
                    hi_loop(b + 5, j)
                    silu(3 * (j - 1) + b + 4)
                    hi_loop(b + 6, j)
                    hi_loop(b + 7, j)
                act.wait_ge(s_used, 3 * (NJ - 2) + b + 2)
                hidden_hi(h0 + NJ - 1)
                act.wait_ge(s_in0, f + 1)
                silu_tile(0)
                hidden_last_hi(h0 + NJ, 0)
                hi(b + FFN_UNITS - 1)
                act.wait_ge(s_used, b + FFN_UNITS - 2)
                silu_tile(1)
                hi(b + FFN_UNITS)
                hidden_last_hi(h0 + NJ + 1, 1)

            def chunk_q(bank, c, used):
                act.wait_ge(s_used, used)
                act.mul(xn[:, 0, c * CW:(c + 1) * CW], bank[:, :], rstd_q[:, :]).then_inc(s_nat_a, 1)

            def lower(r, dst):
                act.wait_ge(s_rt, r + 1)
                act.copy(dst, tb[r % 2][0:DH, :]).then_inc(s_ra, 1)

            def q_half(r, i):
                act.wait_ge(s_rt, r + 1)
                act.copy(qT[:, 2 * i, :], tb[r % 2][:, 0:SEQ]).then_inc(s_ra, 1)

            def exps(n):
                act.wait_ge(s_nmax, n + 1)
                for i in range(4):
                    t, h = divmod(i, 2)
                    c0, w = (h * P, P) if t == 0 else (2 * P + h * SEQ, SEQ)
                    act.activation(probs[:, n % 2, c0:c0 + w], probs[:, n % 2, c0:c0 + w], ACT.Exp,
                                   bias=nmx[:, n % 4, i:i + 1],
                                   accum_out=lsum[:, n % 4, i:i + 1]).then_inc(s_exp, 1)

            def pt_copy(n):
                act.wait_ge(s_pt, 2 * n + 1)
                act.copy(pT[:, n % 2, 0, :], tb[0][:, 0:3 * P]).then_inc(s_pta, 1)

            def items(n0, count, between):
                exps(n0)
                for i in range(count):
                    pt_copy(n0 + i)
                    if i + 1 < count:
                        exps(n0 + i + 1)
                    if i in between:
                        between[i]()

            for i, (dst, src) in enumerate([
                    (work[0:48, 0:P], norm_g.rearrange("l n (k p) -> (l n k) p", p=P)),
                    (work[48:56, 0:P], kv_norm_g.rearrange("(k p) -> k p", p=P)),
                    (work[0:32, P:2 * P], nsa_cmp_pos.rearrange("l x (t c) d -> (l x t) (c d)", c=2)),
                    (rel_s[:, :], rel_bias)]):
                act.dma_start(dst, src).then_inc(s_small[i], 16)
            act.wait_ge(s_const, 1)
            hi(0)
            act.wait_ge(s_setup, 1)
            turned("ffn0", 0)
            hi(1)
            squares("ffn0", 0)
            squares("ffn0", 1)
            turned("ffn0", 1)
            hi(2)
            rms("ffn0")
            normed("ffn0")
            ffn(0)

            boundary("nsa", U_NSA + 1)
            act.wait_ge(s_small2, 16 * 6)
            act.copy(gwhi[:, 0:KT * NG], gate_w[:, :, :].rearrange("p k n -> p (k n)")).then_inc(s_tailw, 1)
            hi(U_NSA + 3)
            act.wait_ge(s_used, U_NSA + 2)
            act.mul(kd[:, 0, 0:2].rearrange("p k g u d -> p (k g) u d"),
                    inb[0][:, :].rearrange("p (g d) -> p g d", d=DH).unsqueeze(2)
                    .broadcast_to([P, 8, 2, DH]), rstd[:, 0:1]).then_inc(s_nat_a, 1)
            hi(U_NSA + 4)

            def kv_copy(bank, kind, a, used):
                act.wait_ge(s_used, used)
                act.mul(kd[:, 0, kind], bank[:, 0:KVD].rearrange("p (g d) -> p g d", d=DH).unsqueeze(2)
                        .broadcast_to([P, G, 2, DH]), rstd[:, 0:1])
                act.mul(vd[:, 0, a, :], bank[:, KVD:2 * KVD], rstd[:, 0:1]).then_inc(s_nat_a, 1)

            def even_tokens(r):
                act.wait_ge(s_rt, r + 1)
                act.copy(k2[0:DH, r // 2, 2 * (r % 2):2 * (r % 2) + 2, :],
                         tb[r % 2][0:DH, :].rearrange("p (g m s) -> p g m s", g=2, s=2)[:, :, :, 0]
                         ).then_inc(s_ra, 1)

            def window_hi(xk):
                act.wait_ge(s_fsum, xk + 1)
                act.copy(win_hi[xk], fsum[:, xk, :]).then_inc(s_fhi, 1)

            even_tokens(0)
            even_tokens(1)
            hi(U_NSA + 5)
            kv_copy(acc[0], 2, 0, U_NSA + 4)
            even_tokens(2)
            even_tokens(3)
            hi(U_NSA + 6)
            act.wait_ge(s_tail, 1)
            for t in range(NT):
                ins = act.activation(gate[:, t, :], acc[2 + t][:, 0:NG], ACT.Sigmoid,
                                     scale=rstd[:, t:t + 1])
            ins.then_inc(s_gate, 1)
            for r in range(2):
                lower(4 + r, kblk[0:DH, 0, 2 * r:2 * r + 2, :])
            hi(U_NSA + 7)
            window_hi(0)
            kv_copy(inb[0], 3, 1, U_NSA + 6)
            hi(U_NSA + 8)
            for r in range(2):
                lower(6 + r, kblk[0:DH, 0, 4 + 2 * r:6 + 2 * r, :])
            hi(U_NSA + 9)
            chunk_q(acc[0], 0, U_NSA + 8)
            hi(U_NSA + 10)
            q_half(8, 0)
            q_half(9, 1)
            hi(U_NSA + 11)
            chunk_q(acc[2], 1, U_NSA + 10)
            window_hi(1)
            hi(U_NSA + 12)
            q_half(10, 2)
            q_half(11, 3)
            hi(U_NSA + 13)
            act.wait_ge(s_flo, 2)
            act.wait_ge(s_used, U_CMP + 2)
            for c in range(2):
                act.activation(hidk[:, c, :], inb[c][:, 0:GN], ACT.Silu).then_inc(s_hid, 1)
            hi(U_NSA + 14)
            hi(U_NSA + 15)
            act.wait_ge(s_used, U_CMP + 4)
            for c in range(2):
                act.activation(hidv[:, c], acc[2 + c][:, 0:GN].rearrange("p (g n) -> p g n", g=G).unsqueeze(2)
                               .broadcast_to([P, G, 4, NCMP]), ACT.Silu).then_inc(s_hid, 1)

            def cmp_exp():
                act.wait_ge(s_csh, 1)
                act.activation(pc, pc, ACT.Exp).then_inc(s_cexp, 1)

            def cmp_copy():
                act.wait_ge(s_cpt, 1)
                act.copy(pcT.rearrange("p c n -> p (c n)"), inb[1][0:HN, :]).then_inc(s_cpc, 1)

            items(0, 16, {2: cmp_exp, 5: cmp_copy, 8: lambda: hi(U_NSA_OUT + 2), 12: lambda: o_hi(0, 0),
                          14: lambda: o_hi(1, 0)})
            o_hi(2, 0)
            o_hi(3, 0)
            hi(U_NSA_OUT + 3)
            hi(U_NSA_OUT + 4)
            boundary("ffn1", U_FFN1 + 1)
            ffn(1)

            boundary("kv", U_KV + 1)
            act.copy(gwhi[:, 0:KT * H], fl_w[:, :, :].rearrange("p k n -> p (k n)")).then_inc(s_tailw, 1)
            hi(U_KV + 3)
            act.wait_ge(s_used, U_KV + 2)
            act.mul(kf[:, 0, 0:CW], acc[0][:, :], rstd[:, 0:1]).then_inc(s_nat_a, 1)
            hi(U_KV + 4)
            hi(U_KV + 5)
            act.wait_ge(s_fa, 1)
            act.activation(fexp, raux, ACT.Exp).then_inc(s_fexp, 1)
            act.wait_ge(s_fexp, 1)
            act.activation(flog, fexp, ACT.Ln, bias=1.0).then_inc(s_flog, 1)
            act.wait_ge(s_used, U_KV + 4)
            act.mul(kf[:, 0, CW:2 * CW], inb[0][:, :], rstd[:, 0:1]).then_inc(s_nat_a, 1)
            for i in range(2):
                lower(12 + i, kblk[0:DH, 0, 2 * i:2 * i + 2, :])
            hi(U_KV + 6)
            for i in range(2, 4):
                lower(12 + i, kblk[0:DH, 0, 2 * i:2 * i + 2, :])
            hi(U_KV + 7)
            act.wait_ge(s_used, U_KV + 6)
            act.mul(vf[:, 0, 0:CW], acc[0][:, :], rstd[:, 0:1]).then_inc(s_nat_a, 1)
            hi(U_KV + 8)
            act.wait_ge(s_tile0, TILE0.index("kv") + 1)
            act.mul(vf[:, 0, CW:2 * CW], inb[0][:, :], rstd[:, 0:1]).then_inc(s_nat_a, 1)
            turned("ffn2", 0)
            hi(U_KV + 9)
            turned("ffn2", 1)
            hi(U_FFN2 + 2)
            ffn(2)

            boundary("fox", U_FOXQ + 1)
            hi(U_FOXQ + 3)
            chunk_q(acc[0], 0, U_FOXQ + 2)
            hi(U_FOXQ + 4)
            q_half(16, 0)
            q_half(17, 1)
            hi(U_FOXQ + 5)
            chunk_q(inb[0], 1, U_FOXQ + 4)
            q_half(18, 2)
            q_half(19, 3)
            items(16, 8, {2: lambda: hi(U_FOX_OUT + 2), 3: lambda: o_hi(0, 4), 5: lambda: o_hi(1, 4),
                          7: lambda: o_hi(2, 4)})
            o_hi(3, 4)
            hi(U_FOX_OUT + 3)
            hi(U_FOX_OUT + 4)
            boundary("ffn3", U_FFN3 + 1)
            ffn(3)
            for t in range(NT):
                squares("final", t)
                rms("final", slice(t, t + 1))

        @block.vector
        def _(dve):
            steps = [0]

            def step(ins):
                steps[0] += 1
                ins.then_inc(s_step, 1)
                dve.wait_ge(s_step, steps[0])

            def lo(u):
                if u >= U_END:
                    return
                dve.wait_ge(s_hi, u + 1)
                dve.tensor_tensor(wlo[u % RING][:, :], raw[u % RING][:, :],
                                  whi[u % RING][:, :].bitcast(F32), ALU.subtract).then_inc(s_lo, 1)

            def lo_loop(u, j):
                dve.wait_ge(s_hi, 3 * (j - 1) + u + 1)
                dve.tensor_tensor(wlo[u % RING][:, :], raw[u % RING][:, :],
                                  whi[u % RING][:, :].bitcast(F32), ALU.subtract).then_inc(s_lo, 1)

            def root(name, tiles=slice(0, NT)):
                i = NORMS.index(name)
                dve.wait_ge(s_rms, i + 1 + (tiles.start if name == "final" else 0))
                step(dve.reciprocal(rstd[:, tiles], ss[:, NT + tiles.start:NT + tiles.stop]))
                if name != "final":
                    dve.tensor_scalar(rstd_q[:, :], rstd[:, 0:1], SCALE, None, ALU.mult).then_inc(s_rstd, 1)

            def turned(name, t):
                tok = slice(t * P, (t + 1) * P)
                for e in range(2):
                    bank = tbanks[2 * t + e]
                    dve.wait_ge(s_thi, 4 * TURNS.index(name) + 2 * t + e + 1)
                    for k in range(4):
                        g = GAIN[name] * KT + 4 * e + k
                        ins = dve.scalar_tensor_tensor(
                            out=tlo[:, 4 * e + k, tok], in0=bank[:, k * P:(k + 1) * P], scalar=gains[:, g:g + 1],
                            in1=thi[:, 4 * e + k, tok].bitcast(F32), op0=ALU.mult, op1=ALU.subtract)
                    ins.then_inc(s_tlo, 1)

            def o_lo(g, first):
                dve.wait_ge(s_ohi, first + g + 1)
                ks = slice(2 * g, 2 * g + 2)
                dve.tensor_tensor(tlo[:, ks, :].rearrange("p k n -> p (k n)"), inb[1][:, :],
                                  thi[:, ks, :].rearrange("p k n -> p (k n)").bitcast(F32),
                                  ALU.subtract).then_inc(s_olo, 1)

            def boundary(name, u, add):
                turned(name, 0)
                add(1)
                lo(u)
                turned(name, 1)
                lo(u + 1)
                root(name)

            def hidden_tile(n, t):
                dve.wait_ge(s_silu, n + 1)
                dve.scalar_tensor_tensor(out=gg[:, t, :], in0=inb[t][:, FC:2 * FC], scalar=rstd[:, t:t + 1],
                                         in1=sa[:, t, :], op0=ALU.mult, op1=ALU.mult).then_inc(s_g, 1)

            def hidden(n):
                for t in range(NT):
                    hidden_tile(n + t, t)

            def hidden_lo(n):
                dve.wait_ge(s_ghi, n)
                dve.tensor_tensor(glo[:, :, :].rearrange("p k n -> p (k n)"), tb[0][:, :],
                                  ghi[:, :, :].rearrange("p k n -> p (k n)").bitcast(F32),
                                  ALU.subtract).then_inc(s_glo, 1)

            def hidden_last_lo(n, t):
                dve.wait_ge(s_ghi, n)
                tok = slice(t * P, (t + 1) * P)
                dve.tensor_tensor(glo_last[:, :, tok], tb[0][:, :].rearrange("p (k n) -> p k n", k=2)[:, :, tok],
                                  ghi_last[:, :, tok].bitcast(F32), ALU.subtract).then_inc(s_glo, 1)

            def ffn(f):
                b, n0, h0 = U_FFN[f], NJ * f, (NJ + 1) * f
                lo(b + 3)
                hidden(2 * n0)
                lo(b + 4)
                with dve.Fori(1, NJ - 1) as j:
                    hidden_lo(j + h0)
                    lo_loop(b + 5, j)
                    hidden(2 * j + 2 * n0)
                    lo_loop(b + 6, j)
                    lo_loop(b + 7, j)
                hidden_lo(h0 + NJ - 1)
                last = 2 * n0 + 2 * (NJ - 1)
                hidden_tile(last, 0)
                hidden_last_lo(h0 + NJ, 0)
                lo(b + FFN_UNITS - 1)
                hidden_tile(last + 1, 1)
                lo(b + FFN_UNITS)
                ffn_add(f, 0)
                hidden_last_lo(h0 + NJ + 1, 1)

            def ffn_add(f, t):
                if t == 0:
                    dve.wait_ge(s_tile0, TILE0.index(f"ffn{f}") + 1)
                else:
                    dve.wait_ge(s_used, U_FFN[f] + FFN_UNITS)
                for n in range(2):
                    xc = xs[:, t, n * CW:(n + 1) * CW]
                    dve.scalar_tensor_tensor(out=xc, in0=acc[2 * t + n][:, :], scalar=0.5, in1=xc,
                                             op0=ALU.mult, op1=ALU.add).then_inc(s_xadd, 1)

            def mixer_add(name, b, c, t):
                if c == 1 and t == 0:
                    dve.wait_ge(s_tile0, TILE0.index(name) + 1)
                else:
                    dve.wait_ge(s_used, b + 2 * c + 2)
                xc = xs[:, t, c * CW:(c + 1) * CW]
                dve.tensor_tensor(xc, acc[2 * c + t][:, :], xc, ALU.add).then_inc(s_xadd, 1)

            def chunk_q(bank, c, used):
                dve.wait_ge(s_used, used)
                dve.tensor_scalar(xn[:, 1, c * CW:(c + 1) * CW], bank[:, :], rstd[:, 1:2], SCALE,
                                  ALU.mult, ALU.mult).then_inc(s_nat_d, 1)

            def upper(r, dst):
                dve.wait_ge(s_rt, r + 1)
                dve.tensor_copy(dst, tb[r % 2][DH:P, :]).then_inc(s_rd, 1)

            def q_half(r, i):
                dve.wait_ge(s_rt, r + 1)
                dve.wait_ge(s_ra, r + 1)
                dve.tensor_copy(qT[:, 2 * i + 1, :], tb[r % 2][:, SEQ:2 * SEQ]).then_inc(s_rd, 1)

            def add_max(n, p, table0):
                for i in (2, 3, 0, 1):
                    t, h = divmod(i, 2)
                    if h == 0:
                        dve.wait_ge(s_qk, 2 * n + (1 if t else 2))
                    if t:
                        dst = probs[:, n % 2, 2 * P + h * SEQ:2 * P + (h + 1) * SEQ]
                        src = acc[2 * (n % 2)][:, h * SEQ:(h + 1) * SEQ]
                        tab = bias[:, 2 * p + h, :]
                    else:
                        dst = probs[:, n % 2, h * P:(h + 1) * P]
                        src = acc[2 * (n % 2) + 1][:, h * P:(h + 1) * P]
                        tab = table0(2 * p + h)
                    dve.tensor_tensor_reduce(dst, src, tab, 1.0, -3e38, ALU.add, ALU.max,
                                             mx[:, n % 4, i:i + 1]).then_inc(s_max, 1)
                dve.wait_ge(s_max, 4 * n + 4)
                dve.tensor_scalar(nmx[:, n % 4, :], mx[:, n % 4, :], -1.0, None, ALU.mult).then_inc(s_nmax, 1)

            def pt_copy(n):
                dve.wait_ge(s_pt, 2 * n + 2)
                dve.tensor_copy(pT[:, n % 2, 1, :], tb[1][:, 0:3 * P]).then_inc(s_ptd, 1)

            def output(n, p, branch, direct):
                if n:
                    dve.wait_ge(s_on, n)
                dve.wait_ge(s_pv, n + 1)
                step(dve.reciprocal(linv[:, :], lsum[:, n % 4, :]))
                o = inb[0][:, 0:2 * P].rearrange("p (t h d) -> p t h d", t=2, h=2)
                if branch is None:
                    w, dst = linv, onat[:, :, 2 * p:2 * p + 2, :]
                else:
                    g = gate[:, :, :].rearrange("p t (h c) -> p t h c", c=3)[:, :, 2 * p:2 * p + 2, branch]
                    step(dve.tensor_tensor(lw[:, :].rearrange("p (t h) -> p t h", t=2),
                                           linv[:, :].rearrange("p (t h) -> p t h", t=2), g, ALU.mult))
                    w, dst = lw, onat[:, :, 2 * p:2 * p + 2, :] if direct else otmp[:, n % 2]
                    if n >= 10:
                        dve.wait_ge(s_oadd, n - 9)
                dve.tensor_tensor(dst, o, w[:, :].rearrange("p (t h) -> p t h", t=2).unsqueeze(3)
                                  .broadcast_to([P, 2, 2, DH]), ALU.mult).then_inc(s_on, 1)

            def items(n0, count, pair, table0, branch, between):
                for i in range(count + 1):
                    if i + 1 < count:
                        add_max(n0 + i + 1, pair(i + 1), table0)
                    if i < count:
                        pt_copy(n0 + i)
                    if i >= 1:
                        output(n0 + i - 1, pair(i - 1), branch(i - 1), i <= 8)
                    if i in between:
                        between[i]()

            dve.wait_ge(s_setup_t, 1)
            dve.tensor_copy(gains[:, :], inb[1][:, 0:56])
            dve.tensor_copy(posT[:, :], inb[1][:, 64:96])
            dve.tensor_copy(tbT[:, :], inb[1][0:H, 96:128]).then_inc(s_setup, 1)
            dve.wait_ge(s_setup, 1)
            lo(0)
            turned("ffn0", 0)
            lo(1)
            turned("ffn0", 1)
            lo(2)
            root("ffn0")
            ffn(0)

            boundary("nsa", U_NSA + 1, lambda t: ffn_add(0, t))
            dve.wait_ge(s_tailw, 1)
            dve.tensor_tensor(gwlo[:, 0:KT * NG], gate_w[:, :, :].rearrange("p k n -> p (k n)"),
                              gwhi[:, 0:KT * NG].bitcast(F32), ALU.subtract).then_inc(s_tailw, 1)
            lo(U_NSA + 3)
            dve.wait_ge(s_used, U_NSA + 2)
            dve.tensor_scalar(kd[:, 1, 0:2].rearrange("p k g u d -> p (k g) u d"),
                              inb[1][:, :].rearrange("p (g d) -> p g d", d=DH).unsqueeze(2)
                              .broadcast_to([P, 8, 2, DH]), rstd[:, 1:2], None, ALU.mult).then_inc(s_nat_d, 1)
            lo(U_NSA + 4)

            def kv_copy(bank, kind, a, used):
                dve.wait_ge(s_used, used)
                dve.tensor_scalar(kd[:, 1, kind], bank[:, 0:KVD].rearrange("p (g d) -> p g d", d=DH)
                                  .unsqueeze(2).broadcast_to([P, G, 2, DH]), rstd[:, 1:2], None, ALU.mult)
                dve.tensor_scalar(vd[:, 1, a, :], bank[:, KVD:2 * KVD], rstd[:, 1:2], None, ALU.mult).then_inc(s_nat_d, 1)

            def odd_tokens(r):
                dve.wait_ge(s_rt, r + 1)
                dve.tensor_copy(k2[DH:P, r // 2, 2 * (r % 2):2 * (r % 2) + 2, :],
                                tb[r % 2][DH:P, :].rearrange("p (g m s) -> p g m s", g=2, s=2)[:, :, :, 1]
                                ).then_inc(s_rd, 1)

            def windows(xk):
                dve.wait_ge(s_ra, 2 * xk + 2)
                dve.wait_ge(s_rd, 2 * xk + 2)
                for th in range(2):
                    tok = k2[:, xk].rearrange("p g (n t) -> p t g n", t=8)[:, :, :, th:th + NCMP]
                    pos = posT[:, 16 * xk + 8 * th:16 * xk + 8 * th + 8].unsqueeze(2).unsqueeze(3)
                    ins = dve.tensor_tensor(
                        fsum[:, xk, th * 8 * GN:(th + 1) * 8 * GN].rearrange("p (t g n) -> p t g n", t=8, g=G),
                        tok, pos.broadcast_to([P, 8, G, NCMP]), ALU.add)
                ins.then_inc(s_fsum, 1)

            def window_lo(xk):
                dve.wait_ge(s_fhi, xk + 1)
                dve.wait_ge(s_fsum, xk + 1)
                dve.tensor_tensor(win_lo[xk], fsum[:, xk, :], win_hi[xk].bitcast(F32),
                                  ALU.subtract).then_inc(s_flo, 1)

            odd_tokens(0)
            odd_tokens(1)
            lo(U_NSA + 5)
            windows(0)
            kv_copy(acc[1], 2, 0, U_NSA + 4)
            odd_tokens(2)
            odd_tokens(3)
            lo(U_NSA + 6)
            for r in range(2):
                upper(4 + r, kblk[DH:P, 1, 2 * r:2 * r + 2, :])
            lo(U_NSA + 7)
            window_lo(0)
            kv_copy(inb[1], 3, 1, U_NSA + 6)
            lo(U_NSA + 8)
            windows(1)
            for r in range(2):
                upper(6 + r, kblk[DH:P, 1, 4 + 2 * r:6 + 2 * r, :])
            lo(U_NSA + 9)
            chunk_q(acc[1], 0, U_NSA + 8)
            lo(U_NSA + 10)
            q_half(8, 0)
            q_half(9, 1)
            lo(U_NSA + 11)
            chunk_q(acc[3], 1, U_NSA + 10)
            window_lo(1)
            lo(U_NSA + 12)
            q_half(10, 2)
            q_half(11, 3)
            lo(U_NSA + 13)
            lo(U_NSA + 14)
            lo(U_NSA + 15)

            def cmp_keys_values():
                dve.wait_ge(s_biasc, 1)
                dve.wait_ge(s_cmp2, 1)
                for u in range(2):
                    dve.tensor_copy(kcb[u * DH:(u + 1) * DH, :, u, :],
                                    inb[1][u * DH:(u + 1) * DH, 0:GN].rearrange("p (g n) -> p g n", g=G))
                for e in range(2):
                    v = inb[1][0:HN, 64 + e * DH:64 + (e + 1) * DH].unsqueeze(1).broadcast_to([HN, 8, DH])
                    ins = dve.tensor_tensor(vblk[:, e], v,
                                            blkmask[:, :].unsqueeze(2).broadcast_to([HN, 8, DH]), ALU.mult)
                ins.then_inc(s_kcb, 1)

            pcr = pc.rearrange("p (r n) -> p r n", n=NCMP)

            def cmp_shift():
                dve.wait_ge(s_sc, 1)
                step(dve.tensor_tensor(pc, inb[1][:, 0:NT * H * NCMP],
                                       biasc.rearrange("p t h n -> p (t h n)"), ALU.add))
                step(dve.tensor_reduce(cmx[:, :], pcr, AX.X, ALU.max))
                dve.tensor_tensor(pcr, pcr, cmx[:, :].unsqueeze(2).broadcast_to([P, NT * H, NCMP]),
                                  ALU.subtract).then_inc(s_csh, 1)

            def cmp_probs():
                dve.wait_ge(s_cexp, 1)
                step(dve.tensor_reduce(csum[:, :], pcr, AX.X, ALU.add))
                for t in range(NT):
                    ins = dve.tensor_tensor(pc4[:, t], pc4[:, t],
                                            cmask01[:, t, :].unsqueeze(1).broadcast_to([P, H, NCMP]), ALU.mult)
                ins.then_inc(s_cp, 1)
                step(dve.reciprocal(cw[:, :], csum[:, :]))
                dve.wait_ge(s_gate, 1)
                step(dve.tensor_tensor(cw[:, :].rearrange("p (t h) -> p t h", t=NT),
                                       cw[:, :].rearrange("p (t h) -> p t h", t=NT),
                                       gate[:, :, :].rearrange("p t (h c) -> p t h c", c=3)[:, :, :, 0],
                                       ALU.mult))

            def cmp_gated(c):
                t, e = CMP_PIECES[c]
                dve.wait_ge(s_co, c + 1)
                if c:
                    dve.wait_ge(s_cadd, c)
                w = cw[:, t * H + 8 * e:t * H + 8 * e + 8].unsqueeze(2).broadcast_to([P, 8, DH])
                dve.tensor_tensor(ctmp, inb[1][:, :].rearrange("p (h d) -> p h d", h=8), w,
                                  ALU.mult).then_inc(s_cog, 1)

            dve.wait_ge(s_bias, 16)
            add_max(0, 0, lambda h: bias[:, h, P:2 * P])
            cmp_keys_values()
            items(0, 16, lambda i: i % 8, lambda h: bias[:, h, P:2 * P], lambda i: 1 + i // 8,
                  {1: cmp_shift, 3: cmp_probs, 6: lambda: cmp_gated(0), 7: lambda: cmp_gated(1),
                   8: lambda: cmp_gated(2), 9: lambda: cmp_gated(3), 10: lambda: lo(U_NSA_OUT + 2),
                   12: lambda: o_lo(0, 0), 14: lambda: o_lo(1, 0)})
            o_lo(2, 0)
            o_lo(3, 0)
            lo(U_NSA_OUT + 3)
            for t in range(NT):
                mixer_add("nsa", U_NSA_OUT, 0, t)
            lo(U_NSA_OUT + 4)
            mixer_add("nsa", U_NSA_OUT, 1, 0)
            boundary("ffn1", U_FFN1 + 1, lambda t: mixer_add("nsa", U_NSA_OUT, 1, t))
            ffn(1)

            boundary("kv", U_KV + 1, lambda t: ffn_add(1, t))
            dve.wait_ge(s_tailw, 3)
            dve.tensor_tensor(gwlo[:, 0:KT * H], fl_w[:, :, :].rearrange("p k n -> p (k n)"),
                              gwhi[:, 0:KT * H].bitcast(F32), ALU.subtract).then_inc(s_tailw, 1)
            lo(U_KV + 3)
            dve.wait_ge(s_used, U_KV + 2)
            dve.tensor_scalar(kf[:, 1, 0:CW], acc[1][:, :], rstd[:, 1:2], None, ALU.mult).then_inc(s_nat_d, 1)
            dve.wait_ge(s_tail, 2)
            for t in range(NT):
                ins = dve.tensor_scalar(fl[:, t, :], acc[2 + t][:, 0:H], rstd[:, t:t + 1], None, ALU.mult)
            ins.then_inc(s_flc, 1)
            lo(U_KV + 4)
            dve.wait_ge(s_flt, 1)
            step(dve.tensor_scalar(rfl, tb[0][0:H, 0:SEQ], bf[:, :], None, ALU.add))
            dve.scalar_tensor_tensor(out=raux, in0=rfl, scalar=-1.0, in1=rfl, op0=ALU.mult,
                                     op1=ALU.min).then_inc(s_fa, 1)
            lo(U_KV + 5)
            dve.wait_ge(s_used, U_KV + 4)
            dve.tensor_scalar(kf[:, 1, CW:2 * CW], inb[1][:, :], rstd[:, 1:2], None, ALU.mult).then_inc(s_nat_d, 1)
            for i in range(2):
                upper(12 + i, kblk[DH:P, 1, 2 * i:2 * i + 2, :])
            lo(U_KV + 6)
            for i in range(2, 4):
                upper(12 + i, kblk[DH:P, 1, 2 * i:2 * i + 2, :])
            dve.wait_ge(s_flog, 1)
            step(dve.tensor_scalar(fcor, fexp, 1.0, None, ALU.add))
            step(dve.reciprocal(frec, fcor))
            step(dve.tensor_scalar(fcor, fcor, -1.0, None, ALU.add))
            step(dve.tensor_tensor(fcor, fexp, fcor, ALU.subtract))
            step(dve.tensor_tensor(fcor, fcor, frec, ALU.mult))
            step(dve.tensor_tensor(flog, flog, fcor, ALU.add))
            step(dve.tensor_scalar(rfl, rfl, 0.0, None, ALU.min))
            step(dve.tensor_tensor(flog, rfl, flog, ALU.subtract))
            step(dve.memset(fcor, 1.0))
            step(dve.tensor_tensor_scan(rfl, fcor, flog, 0.0, ALU.mult, ALU.add))
            dve.tensor_scalar(raux, rfl, -1.0, None, ALU.mult).then_inc(s_neg, 1)
            lo(U_KV + 7)
            dve.wait_ge(s_used, U_KV + 6)
            dve.tensor_scalar(vf[:, 1, 0:CW], acc[1][:, :], rstd[:, 1:2], None, ALU.mult).then_inc(s_nat_d, 1)
            dve.wait_ge(s_ct, 1)
            dve.tensor_copy(cq[:, :, :].rearrange("p t h -> p (t h)"), acc[2][:, 0:NT * H]).then_inc(s_cq, 1)
            lo(U_KV + 8)
            turned("ffn2", 0)
            lo(U_KV + 9)
            dve.wait_ge(s_used, U_KV + 8)
            dve.tensor_scalar(vf[:, 1, CW:2 * CW], inb[1][:, :], rstd[:, 1:2], None, ALU.mult).then_inc(s_nat_d, 1)
            turned("ffn2", 1)
            lo(U_FFN2 + 2)
            ffn(2)

            boundary("fox", U_FOXQ + 1, lambda t: ffn_add(2, t))
            lo(U_FOXQ + 3)
            chunk_q(acc[1], 0, U_FOXQ + 2)
            lo(U_FOXQ + 4)
            q_half(16, 0)
            q_half(17, 1)
            lo(U_FOXQ + 5)
            chunk_q(inb[1], 1, U_FOXQ + 4)
            dve.wait_ge(s_decay, H // 4)
            add_max(16, 0, lambda h: decay0[:, h, :])
            q_half(18, 2)
            q_half(19, 3)
            items(16, 8, lambda i: i, lambda h: decay0[:, h, :], lambda i: None,
                  {3: lambda: [lo(U_FOX_OUT + 2), o_lo(0, 4)], 5: lambda: o_lo(1, 4), 7: lambda: o_lo(2, 4)})
            o_lo(3, 4)
            lo(U_FOX_OUT + 3)
            for t in range(NT):
                mixer_add("fox", U_FOX_OUT, 0, t)
            lo(U_FOX_OUT + 4)
            mixer_add("fox", U_FOX_OUT, 1, 0)
            boundary("ffn3", U_FFN3 + 1, lambda t: mixer_add("fox", U_FOX_OUT, 1, t))
            ffn(3)
            dve.wait_ge(s_fg, 16)
            for t in range(NT):
                if t:
                    ffn_add(3, t)
                root("final", slice(t, t + 1))
                dve.scalar_tensor_tensor(out=xn[:, t, :], in0=xs[:, t, :], scalar=rstd[:, t:t + 1],
                                         in1=finalb, op0=ALU.mult, op1=ALU.mult).then_inc(s_y, 1)

        @block.gpsimd
        def _(pool):
            steps = [0]

            def step(ins):
                steps[0] += 1
                ins.then_inc(s_pstep, 1)
                pool.wait_ge(s_pstep, steps[0])

            pool.memset(epst[:, :], EPS)
            step(pool.memset(ident[:, :], 0.0))
            pool.affine_select(out=ident[:, :], in_=ident[:, :], compare_op=ALU.not_equal, fill=1.0, base=0,
                               pattern=[[-1, P]], channel_multiplier=1).then_inc(s_const, 1)
            pool.memset(zeros[:, :], 0.0)
            step(pool.memset(cmask[:, :], 0.0))
            pool.affine_select(out=cmask[:, :], in_=cmask[:, :], compare_op=ALU.is_ge, fill=NEG, base=0,
                               pattern=[[-1, P]], channel_multiplier=1)
            step(pool.memset(cmask01[:, :, :], 1.0))
            for t in range(NT):
                pool.affine_select(out=cmask01[:, t, :], in_=cmask01[:, t, :], compare_op=ALU.is_ge, fill=0.0,
                                   base=t * P - (CMP_BLOCK - 1), pattern=[[-CMP_STRIDE, NCMP]],
                                   channel_multiplier=1)
            step(pool.memset(blkmask[:, :], 1.0))
            step(pool.affine_select(out=blkmask[:, :], in_=blkmask[:, :], compare_op=ALU.is_ge, fill=0.0,
                                    base=0, pattern=[[-NCMP, 8]], channel_multiplier=1))
            pool.affine_select(out=blkmask[:, :], in_=blkmask[:, :], compare_op=ALU.is_ge, fill=0.0,
                               base=NCMP - 1, pattern=[[NCMP, 8]], channel_multiplier=-1)
            pool.memset(kcb[:, :, :, :], 0.0)
            pool.memset(kblk[:, :, :, :], 0.0).then_inc(s_const, 1)
            small = [(gate_w[:, :, :], nsa_w_in[0, :, D + 6 * KVD:].rearrange("(k p) n -> p k n", p=P)),
                     (fl_w[:, :, :], fox_w_kvf[:, 2 * D:].rearrange("(k p) n -> p k n", p=P)),
                     (w2k[:, :, 0, :], nsa_cmp_w2[0, 0].rearrange("(c p) d -> p c d", p=P)),
                     (w2k[:, :, 1, :], nsa_cmp_w2[0, 0].rearrange("(c p) d -> p c d", p=P)),
                     (w2v[:, :, :], nsa_cmp_w2[0, 1].rearrange("(c p) d -> p c d", p=P)),
                     (bf[:, :], fox_b_f.rearrange("(h a) -> h a", a=1))]
            for dst, src in small:
                pool.dma_start(dst, src).then_inc(s_small2, 16)
            pool.wait_ge(s_setup, 1)
            starts = bucket_starts()
            for b in range(NB):
                near, far = starts[b], starts[b + 1] - 1
                pool.tensor_copy(rows[:, SEQ - 1 - far:SEQ - near],
                                 tbT[:, b:b + 1].broadcast_to([H, far - near + 1]))
            pool.memset(rows[:, SEQ:2 * SEQ], NEG).then_inc(s_rows, 1)
            pool.wait_ge(s_rows, 1)
            pool.dma_start(scratch_b.rearrange("p h m -> h p m"),
                           rows.unsqueeze(1).broadcast_to([H, P, 512])).then_inc(s_rows_out, 16)
            pool.wait_ge(s_rows_out, 16)
            pool.dma_start(bias[:, :, :], bass.AP(tensor=scratch_b.tensor, offset=P - 1,
                                                  ap=[[H * 512 - 1, P], [512, H], [1, SEQ]])).then_inc(s_bias, 16)
            step(pool.memset(biasc, NEG))
            pool.wait_ge(s_bias, 16)
            end = CMP_BLOCK - 1
            pool.tensor_copy(biasc[:, 1], bias[:, :, end:end + (NCMP - 1) * CMP_STRIDE + 1:CMP_STRIDE])
            pool.tensor_copy(biasc[:, 0, :, 0:7],
                             bias[:, :, P + end:P + end + 6 * CMP_STRIDE + 1:CMP_STRIDE]).then_inc(s_biasc, 1)
            for c, (t, e) in enumerate(CMP_PIECES):
                pool.wait_ge(s_on, 4 * e + 4)
                pool.wait_ge(s_cog, c + 1)
                o = onat[:, t, 8 * e:8 * e + 8, :]
                pool.tensor_tensor(o, o, ctmp, ALU.add).then_inc(s_cadd, 1)
            pool.wait_ge(s_cadd, len(CMP_PIECES))
            for n in range(8, 16):
                pool.wait_ge(s_on, n + 1)
                o = onat[:, :, 2 * (n % 8):2 * (n % 8) + 2, :]
                pool.tensor_tensor(o, o, otmp[:, n % 2], ALU.add).then_inc(s_oadd, 1)
            pool.wait_ge(s_neg, 1)
            pool.dma_start(scratch_c, raux).then_inc(s_cst, 16)
            pool.wait_ge(s_cst, 16)
            pool.dma_start(bias[:, :, :].rearrange("p h n -> p (h n)"),
                           bass.AP(tensor=scratch_c.tensor, offset=0, ap=[[0, P], [1, H * SEQ]])
                           ).then_inc(s_cb, 16)
            pool.wait_ge(s_cb, 16)
            pool.wait_ge(s_cq, 1)
            cmask_h = cmask[:, :].unsqueeze(1).broadcast_to([P, 4, P])
            for h in range(0, H, 4):
                d0, d1 = decay0[:, h:h + 4, :], bias[:, h:h + 4, :]
                step(pool.tensor_tensor(d0, d1[:, :, 0:P], cmask_h, ALU.add))
                pool.tensor_tensor(d0, d0, cq[:, 0, h:h + 4].unsqueeze(2).broadcast_to([P, 4, P]), ALU.add)
                step(pool.tensor_tensor(d1, d1, cq[:, 1, h:h + 4].unsqueeze(2).broadcast_to([P, 4, SEQ]),
                                        ALU.add))
                pool.tensor_tensor(d1[:, :, P:SEQ], d1[:, :, P:SEQ], cmask_h, ALU.add).then_inc(s_decay, 1)
            pool.wait_ge(s_on, 24)
            pool.dma_start(finalb, final_g.partition_broadcast(P)).then_inc(s_fg, 16)


_INS = ["x", "norm_g", "ffn_w_in", "ffn_w_out", "nsa_w_in", "nsa_cmp_pos", "nsa_cmp_w1", "nsa_cmp_w2",
        "nsa_w_out", "rel_bias", "kv_norm_g", "fox_w_kvf", "fox_b_f", "fox_w_q", "fox_w_out", "final_g"]


def kernel(**inputs):
    import concourse.bacc as bacc
    from concourse.bass_utils import run_bass_kernel_spmd

    nc = bacc.Bacc("TRN2", target_bir_lowering=False, num_devices=1)
    arrays, args = {}, []
    for name in _INS:
        a = np.ascontiguousarray(inputs[name])
        arrays[f"in_{name}"] = a
        args.append(nc.dram_tensor(f"in_{name}", a.shape, mybir.dt.from_np(a.dtype), kind="ExternalInput").ap())
    out = nc.dram_tensor("out", (1, SEQ, D), F32, kind="ExternalOutput").ap()
    yoco_trunk(nc, *args, out)
    r = run_bass_kernel_spmd(nc, [arrays], core_ids=[0])
    return r.results[0]["out"]
```

```python
import math
from contextlib import ExitStack

import numpy as np
import concourse.bass as bass
from concourse import mybir

F32 = mybir.dt.float32
F32R = mybir.dt.float32r
BF16 = mybir.dt.bfloat16
ALU = mybir.AluOpType
ACT = mybir.ActivationFunctionType
AX = mybir.AxisListType

P = 128
SEQ, D = 256, 1024
NT = SEQ // P
KT = D // P
H, DH = 16, 64
G = 4
KVD = G * DH
DFF = 2816
FC = 256
NJ = DFF // FC
CMP_BLOCK, CMP_STRIDE, CMP_HIDDEN = 32, 16, 256
NCMP = (SEQ - CMP_BLOCK) // CMP_STRIDE + 1
GN = G * NCMP
HN = 8 * NCMP
NB, MAXD = 32, 128
NG = 3 * H
EPS = 1e-6
NEG = -1e30
SCALE = DH ** -0.5
CW = 512
UNIT = 4 * CW
RING = 3

FFN_UNITS = 3 * NJ
U_FFN0 = 0
U_NSA = U_FFN0 + FFN_UNITS
U_CMP = [U_NSA + 6, U_NSA + 10]
U_NSAQ = [U_NSA + 8, U_NSA + 12]
U_NSA_OUT = U_NSA + 14
U_FFN1 = U_NSA_OUT + 4
U_KV = U_FFN1 + FFN_UNITS
U_FFN2 = U_KV + 8
U_FOXQ = U_FFN2 + FFN_UNITS
U_FOX_OUT = U_FOXQ + 4
U_FFN3 = U_FOX_OUT + 4
U_END = U_FFN3 + FFN_UNITS
U_FFN = [U_FFN0, U_FFN1, U_FFN2, U_FFN3]

TURNS = ["ffn0", "nsa", "ffn1", "kv", "ffn2", "fox", "ffn3"]
GAIN = {"ffn0": 0, "nsa": 1, "ffn1": 2, "ffn2": 3, "fox": 4, "ffn3": 5, "kv": 6}
NORMS = ["ffn0", "nsa", "ffn1", "kv", "fox", "ffn3", "final"]
ADDS = ["ffn0", "nsa", "ffn1", "ffn2", "fox", "ffn3"]
TILE0 = ["nsa", "kv", "fox"]
ADD_BEFORE = {"nsa": "ffn0", "ffn1": "nsa", "kv": "ffn1", "fox": "ffn2", "ffn3": "fox", "final": "ffn3"}


def added(name, t, half):
    before = ADD_BEFORE[name]
    return 4 * ADDS.index(before) + (2 * t + half if before.startswith("ffn") else 2 * half + t) + 1


CMP_PIECES = [(0, 0), (1, 0), (0, 1), (1, 1)]


def bucket_starts():
    dist = np.arange(SEQ)
    exact = NB // 2
    scaled = np.log(np.maximum(dist, 1).astype(np.float32) / np.float32(exact)).astype(np.float32)
    scaled = scaled / np.float32(math.log(MAXD / exact))
    large = np.minimum(exact + (scaled * np.float32(NB - exact)).astype(np.int32), NB - 1)
    bucket = np.where(dist < exact, dist, large)
    return [int(np.argmax(bucket == b)) for b in range(NB)] + [SEQ]


def yoco_trunk(nc, x, norm_g, ffn_w_in, ffn_w_out, nsa_w_in, nsa_cmp_pos, nsa_cmp_w1, nsa_cmp_w2,
               nsa_w_out, rel_bias, kv_norm_g, fox_w_kvf, fox_b_f, fox_w_q, fox_w_out, final_g, out):
    ctx = ExitStack()
    with ctx:
        def sb(name, shape, dt=F32):
            return ctx.enter_context(nc.sbuf_tensor(name, shape, dt))

        def ps(name):
            return ctx.enter_context(nc.psum_tensor(name, [P, 512], F32))

        def sem(name):
            return ctx.enter_context(nc.semaphore(name))

        raw = [sb(f"raw{s}", [P, UNIT]) for s in range(RING)]
        whi = [sb(f"whi{s}", [P, UNIT], F32R) for s in range(RING)]
        wlo = [sb(f"wlo{s}", [P, UNIT], F32R) for s in range(RING)]
        xs = sb("xs", [P, NT, D])
        xn = sb("xn", [P, NT, D])
        thi = sb("thi", [P, KT, SEQ], F32R)
        tlo = sb("tlo", [P, KT, SEQ], F32R)
        ghi = sb("ghi", [P, 2, SEQ], F32R)
        glo = sb("glo", [P, 2, SEQ], F32R)
        sa = sb("sa", [P, NT, FC])
        gg = sb("gg", [P, NT, FC])
        qT = sb("qT", [P, H // 2, SEQ])
        nat = sb("nat", [P, 5120])
        kblk = sb("kblk", [P, 2, 8, SEQ])
        bias = sb("bias", [P, H, SEQ])
        work = sb("work", [P, 3072])
        fhi = sb("fhi", [P, 16, GN], F32R)
        flo = sb("flo", [P, 16, GN], F32R)
        low = sb("low", [P, 2048])
        gate_w = sb("gate_w", [P, KT, NG])
        fl_w = sb("fl_w", [P, KT, H])
        w2k = sb("w2k", [P, 2, 2, DH])
        w2v = sb("w2v", [P, 2, DH])
        ident = sb("ident", [P, P])
        cmask = sb("cmask", [P, P])
        gains = sb("gains", [P, 56])
        posT = sb("posT", [P, 32])
        tbT = sb("tbT", [H, NB])
        cmask01 = sb("cmask01", [P, NT, NCMP])
        blkmask = sb("blkmask", [HN, 8])
        kcb = sb("kcb", [P, G, 2, NCMP])
        zeros = sb("zeros", [32, P], BF16)
        epst = sb("epst", [P, 1])
        half_sq = sb("half_sq", [P, 2 * NT])
        junk = sb("junk", [P, 3])
        ss = sb("ss", [P, 2 * NT])
        rstd = sb("rstd", [P, NT])
        rstd_q = sb("rstd_q", [P, 1])
        mx = sb("mx", [P, 4, 4])
        nmx = sb("nmx", [P, 4, 4])
        lsum = sb("lsum", [P, 4, 4])
        linv = sb("linv", [P, 4])
        lw = sb("lw", [P, 4])
        gate = sb("gate", [P, NT, NG])
        cmx = sb("cmx", [P, NT * H])
        csum = sb("csum", [P, NT * H])
        cw = sb("cw", [P, NT * H])
        cq = sb("cq", [P, NT, H])
        rstd_h = sb("rstd_h", [P, NT, H])
        bf = sb("bf", [H, 1])
        rel_s = sb("rel_s", [NB, H])

        kd = nat[:, 0:4096].rearrange("p (t k g u d) -> p t k g u d", t=NT, k=4, g=G, u=2)
        vd = nat[:, 4096:5120].rearrange("p (t a n) -> p t a n", t=NT, a=2)
        kf = nat[:, 0:2048].rearrange("p (t n) -> p t n", t=NT)
        vf = nat[:, 2048:4096].rearrange("p (t n) -> p t n", t=NT)
        k2 = work[:, 0:1024].rearrange("p (x g m) -> p x g m", x=2, g=G)
        fsum = work[:, 1024:1024 + 2 * 16 * GN].rearrange("p (x c) -> p x c", x=2)
        hid = work[0:GN, 768:768 + 2 * CMP_HIDDEN].rearrange("p (x n) -> p x n", x=2)
        hidk = work[:, 2304:2304 + 2 * GN].rearrange("p (c n) -> p c n", c=2)
        hidv = work[:, 2432:2432 + 4 * HN].rearrange("p (c g r n) -> p c g r n", c=2, g=G, r=4)
        hidv_rows = work[:, 2432:2432 + 4 * HN].rearrange("p (c n) -> p c n", c=2)
        probs = work[:, 0:1536].rearrange("p (b n) -> p b n", b=2)
        pT = work[:, 1536:3072].rearrange("p (b h n) -> p b h n", b=2, h=2)
        vblk = low[0:HN, 0:1024].rearrange("p (e h d) -> p e h d", e=2, h=8)
        pcT = low[0:HN, 1024:1536].rearrange("p (c n) -> p c n", c=4)
        biasc = low[:, 1536:1536 + NT * H * NCMP].rearrange("p (t h n) -> p t h n", t=NT, h=H)
        decay0 = low[:, :].rearrange("p (h n) -> p h n", h=H)
        pc = sa[:, :, :].rearrange("p t n -> p (t n)")[:, 0:NT * H * NCMP]
        pc4 = pc.rearrange("p (t h n) -> p t h n", t=NT, h=H)
        ctmp = low[:, 1536:2048].rearrange("p (h d) -> p h d", h=8)
        win_hi = fhi[:, :, :].rearrange("p t n -> p (t n)")
        win_lo = flo[:, :, :].rearrange("p t n -> p (t n)")
        gateT = gg[0:NG, 0, :]
        otmp = gg[:, :, :].rearrange("p b (t h d) -> p b t h d", t=2, h=2)
        ghi_last = fhi[:, :, :].rearrange("p t n -> p (t n)")[:, 0:2 * SEQ].rearrange("p (k n) -> p k n", k=2)
        glo_last = flo[:, :, :].rearrange("p t n -> p (t n)")[:, 0:2 * SEQ].rearrange("p (k n) -> p k n", k=2)
        gwhi = ghi[:, :, :].rearrange("p a n -> p (a n)")
        gwlo = glo[:, :, :].rearrange("p a n -> p (a n)")
        onat = xn[:, :, :].rearrange("p t (h d) -> p t h d", h=H)
        rows = low[0:H, 0:512]
        rfl = rows[:, 0:SEQ]
        raux = rows[:, SEQ:2 * SEQ]
        finalb = work[:, 0:D]
        squares_out = work[:, D:2 * D]
        fexp = work[0:H, 0:SEQ]
        flog = work[0:H, SEQ:2 * SEQ]
        fcor = work[0:H, 2 * SEQ:3 * SEQ]
        frec = work[0:H, 3 * SEQ:4 * SEQ]

        acc = [ps(f"acc{i}") for i in range(4)]
        inb = [ps(f"inb{i}") for i in range(2)]
        tb = [ps(f"tb{i}") for i in range(2)]
        tbanks = [tb[0], tb[1], acc[2], acc[3]]

        s_raw = [sem(f"raw_loaded{s}") for s in range(RING)]
        s_hi = sem("unit_hi")
        s_lo = sem("unit_lo")
        s_used = sem("unit_used")
        s_x = [sem(f"x_loaded{t}") for t in range(NT)]
        s_small = [sem(f"small_loaded{i}") for i in range(4)]
        s_small2 = sem("small_loaded_later")
        s_const = sem("consts")
        s_setup_t = sem("setup_turned")
        s_setup = sem("setup_copied")
        s_rows = sem("bias_rows")
        s_rows_out = sem("bias_rows_stored")
        s_bias = sem("bias_loaded")
        s_biasc = sem("biasc_ready")
        s_sumsq = sem("sumsq")
        s_rms = sem("rms")
        s_rstd = sem("rstd_ready")
        s_rstd_h = sem("rstd_by_head")
        s_tt = sem("turned")
        s_thi = sem("turned_hi")
        s_tlo = sem("turned_lo")
        s_silu = sem("silu_done")
        s_g = sem("hidden_ready")
        s_gt = sem("hidden_turned")
        s_ghi = sem("hidden_hi")
        s_glo = sem("hidden_lo")
        s_in0 = sem("hidden_cols_tile0")
        s_out_bank = sem("ffn_out_bank")
        s_tile0 = sem("tile0_done")
        s_ot = sem("o_turned")
        s_ohi = sem("o_hi")
        s_olo = sem("o_lo")
        s_xadd = sem("x_added")
        s_nat_a = sem("chunk_copied_act")
        s_nat_d = sem("chunk_copied_dve")
        s_rt = sem("round_turned")
        s_ra = sem("round_copied_act")
        s_rd = sem("round_copied_dve")
        s_tailw = sem("small_split")
        s_tail = sem("tail_done")
        s_tailc = sem("gates_copied")
        s_tailt = sem("gates_turned")
        s_half0 = sem("first_half_hi")
        s_half1 = sem("first_half_lo")
        s_gate = sem("gate_ready")
        s_fsum = sem("windows_summed")
        s_fhi = sem("windows_hi")
        s_flo = sem("windows_lo")
        s_hid = sem("cmp_hidden")
        s_hidt = sem("cmp_hidden_turned")
        s_hidc = sem("cmp_hidden_copied")
        s_cmp2 = sem("cmp_out")
        s_kcb = sem("cmp_kv_ready")
        s_sc = sem("cmp_scores")
        s_csh = sem("cmp_shifted")
        s_cexp = sem("cmp_exp")
        s_cp = sem("cmp_probs")
        s_cpt = sem("cmp_probs_turned")
        s_cpc = sem("cmp_probs_copied")
        s_co = sem("cmp_values")
        s_cog = sem("cmp_gated")
        s_qk = sem("scores")
        s_max = sem("max_done")
        s_nmax = sem("negmax_ready")
        s_exp = sem("probs_ready")
        s_pt = sem("probs_turned")
        s_pta = sem("pT_act")
        s_ptd = sem("pT_dve")
        s_pv = sem("values_done")
        s_on = sem("o_gated")
        s_cadd = sem("cmp_added")
        s_oadd = sem("o_added")
        s_fa = sem("fl_abs_ready")
        s_fexp = sem("fl_exp_act")
        s_flog = sem("fl_log")
        s_neg = sem("neg_c_ready")
        s_cst = sem("neg_c_stored")
        s_cb = sem("neg_c_loaded")
        s_ct = sem("c_turned")
        s_cq = sem("c_by_query")
        s_decay = sem("decay_ready")
        s_fg = sem("final_gain")
        s_fin = sem("final_squares")
        s_rfin = sem("final_rstd")
        s_y = sem("y_ready")
        s_ya = sem("y_ready_act")
        s_out = sem("out_stored")
        s_step = sem("dve_step")
        s_pstep = sem("pool_step")

        scratch_b = nc.dram_tensor("bias_rows_dram", [P, H, 512], F32).ap()
        scratch_c = nc.dram_tensor("neg_c_dram", [H, SEQ], F32).ap()

        block = ctx.enter_context(nc.Block())

        @block.sync
        def _(sp):
            def load(u, halves, number=None):
                if number is not None or u >= RING:
                    sp.wait_ge(s_lo, (u if number is None else number) - RING + 1)
                for dst, src in halves:
                    sp.dma_start(dst, src).then_inc(s_raw[u % RING], 16)

            def ffn_in(f, j, half, u):
                w = ffn_w_in[f // 2, f % 2][half * 512:(half + 1) * 512, :]
                w = w.rearrange("(k p) n -> p k n", p=P)
                r = raw[u % RING][:, :].rearrange("p (k n) -> p k n", k=4)
                return [(r[:, :, 0:FC], w[:, :, bass.ds(j * FC, FC)]),
                        (r[:, :, FC:2 * FC], w[:, :, bass.ds(j * FC + DFF, FC)])]

            def ffn_out(f, j, u):
                w = ffn_w_out[f // 2, f % 2]
                r = raw[u % RING][:, :].rearrange("p (k n) -> p k n", k=2)
                return [(r[:, k, :], w[bass.ds(j * FC + k * P, P), :]) for k in range(2)]

            def ffn(f):
                b = U_FFN[f]
                for i in range(2):
                    load(b + i, ffn_in(f, 0, i, b + i))
                    if b + i == 0:
                        sp.dma_start(xs[:, 1, :], x[0, P:2 * P, :]).then_inc(s_x[1], 16)
                with sp.Fori(1, NJ) as j:
                    for i in range(3):
                        u = b + 2 + i
                        halves = ffn_in(f, j, i, u) if i < 2 else ffn_out(f, j - 1, u)
                        load(u, halves, 3 * (j - 1) + max(u, RING))
                u = b + FFN_UNITS - 1
                load(u, ffn_out(f, NJ - 1, u))

            def matrix(w, b, chunks):
                for c, col in enumerate(chunks):
                    for i in range(2):
                        u = b + 2 * c + i
                        wr = w[i * 512:(i + 1) * 512, col:col + CW].rearrange("(k p) n -> p k n", p=P)
                        r = raw[u % RING][:, :].rearrange("p (k n) -> p k n", k=4)
                        load(u, [(r[:, 0:2], wr[:, 0:2]), (r[:, 2:4], wr[:, 2:4])])

            sp.dma_start(xs[:, 0, :], x[0, 0:P, :]).then_inc(s_x[0], 16)
            ffn(0)
            matrix(nsa_w_in[0], U_NSA, [D, D + 2 * KVD, D + 4 * KVD])
            for xk in range(2):
                for i in range(2):
                    u = U_CMP[xk] + i
                    wr = nsa_cmp_w1[0, xk, i * 1024:(i + 1) * 1024, :].rearrange("(k p) n -> p k n", p=P)
                    r = raw[u % RING][:, :].rearrange("p (k n) -> p k n", k=8)
                    load(u, [(r[:, 0:4], wr[:, 0:4]), (r[:, 4:8], wr[:, 4:8])])
                matrix(nsa_w_in[0], U_NSAQ[xk], [xk * CW])
            matrix(nsa_w_out[0], U_NSA_OUT, [0, CW])
            ffn(1)
            matrix(fox_w_kvf, U_KV, [0, CW, 2 * CW, 3 * CW])
            ffn(2)
            matrix(fox_w_q[0], U_FOXQ, [0, CW])
            matrix(fox_w_out[0], U_FOX_OUT, [0, CW])
            ffn(3)
            for t in range(NT):
                for n, done in enumerate([s_y, s_ya]):
                    cols = slice(n * CW, (n + 1) * CW)
                    sp.wait_ge(done, t + 1)
                    sp.dma_start(out[0, t * P:(t + 1) * P, cols], xn[:, t, cols]).then_inc(s_out, 16)
            sp.wait_ge(s_out, 16 * 2 * NT)

        @block.tensor
        def _(pe):
            def turn(name, t):
                for e in range(2):
                    if name == "ffn0":
                        pe.wait_ge(s_x[t], 16)
                    elif name != "ffn2":
                        pe.wait_ge(s_xadd, added(name, t, e))
                    for k in range(4):
                        mm = pe.transpose(tbanks[2 * t + e][:, k * P:(k + 1) * P],
                                          xs[:, t, (4 * e + k) * P:(4 * e + k + 1) * P], ident[:, :])
                    mm.then_inc(s_tt, 1)

            def three(o, lh, ll, rh, rl, start, stop):
                pe.matmul(o, lh, rh, start=start, stop=False, skip_group_check=True)
                pe.matmul(o, lh, rl, start=False, stop=False, skip_group_check=True)
                return pe.matmul(o, ll, rh, start=False, stop=stop, skip_group_check=True)

            def rows4(slot, half, t, o, wait_third=None):
                tok = slice(t * P, (t + 1) * P)
                for k in range(4):
                    if k == 2 and wait_third:
                        pe.wait_ge(*wait_third)
                    kk = 4 * half + k
                    mm = three(o, thi[:, kk, tok], tlo[:, kk, tok], whi[slot][:, k * CW:(k + 1) * CW],
                               wlo[slot][:, k * CW:(k + 1) * CW], kk == 0, kk == KT - 1)
                return mm

            def unit_in(slot, half, banks, need):
                pe.wait_ge(s_lo, need)
                for t in range(NT):
                    mm = rows4(slot, half, t, banks[t][:, :])
                mm.then_inc(s_used, 1)

            def unit(b, c, half, banks):
                u = b + 2 * c + half
                unit_in(u % RING, half, banks, u + 1)

            def first_chunk(b, banks, name):
                for t in range(NT):
                    for half in range(2):
                        u = b + half
                        pe.wait_ge(s_tlo, 4 * TURNS.index(name) + 2 * t + half + 1)
                        if u == 0 and t == 0:
                            pe.wait_ge(s_half1, 1)
                            mm = rows4(u % RING, half, t, banks[t][:, :], (s_lo, 1))
                        else:
                            pe.wait_ge(s_lo, u + 1)
                            mm = rows4(u % RING, half, t, banks[t][:, :])
                        if t == NT - 1:
                            mm.then_inc(s_used, 1)
                        elif half == 0:
                            turn(name, 1)
                        elif name.startswith("ffn"):
                            mm.then_inc(s_in0, 1)

            def last_chunk(b, banks, following, banks_free=None):
                for t in range(NT):
                    for half in range(2):
                        u = b + half
                        pe.wait_ge(s_lo, u + 1)
                        mm = rows4(u % RING, half, t, banks[t][:, :])
                        if t == NT - 1:
                            mm.then_inc(s_used, 1)
                            if half == 0:
                                if banks_free:
                                    banks_free()
                                turn(following, 0)
                    if t == 0:
                        mm.then_inc(s_tile0, 1)

            def out_part(slot, t, k):
                for n in range(2):
                    mm = out_columns(slot, t, k, n)
                return mm

            def out_columns(slot, t, k, n, last=False):
                h_hi, h_lo = (ghi_last, glo_last) if last else (ghi, glo)
                tok = slice(t * P, (t + 1) * P)
                col = slice(k * D + n * CW, k * D + (n + 1) * CW)
                return three(acc[2 * t + n][:, :], h_hi[:, k, tok], h_lo[:, k, tok],
                             whi[slot][:, col], wlo[slot][:, col], False, last and k == 1)

            def out_last(slot, t):
                for n in range(2):
                    out_columns(slot, t, 0, n, True)
                    mm = out_columns(slot, t, 1, n, True)
                    mm.then_inc(s_used if (t, n) == (1, 1) else s_out_bank, 1)

            def copied(n):
                pe.wait_ge(s_nat_a, n)
                pe.wait_ge(s_nat_d, n)

            def hidden_turn(need, tiles=range(NT)):
                pe.wait_ge(s_g, need)
                for k in range(2):
                    for t in tiles:
                        mm = pe.transpose(tb[0][:, k * SEQ + t * P:k * SEQ + (t + 1) * P],
                                          gg[:, t, k * P:(k + 1) * P], ident[:, :])
                mm.then_inc(s_gt, 1)

            def ffn(f, following=None):
                b, n0, h0 = U_FFN[f], NJ * f, (NJ + 1) * f
                first_chunk(b, inb, f"ffn{f}")
                if f == 2:
                    copied(9)
                if f == 0:
                    pe.wait_ge(s_setup, 2)
                    pe.wait_ge(s_const, 2)
                for a in acc:
                    pe.matmul(a[:, :], zeros[:, :], zeros[:, :].unsqueeze(1).broadcast_to([32, 4, P]),
                              start=True, stop=False, skip_group_check=True)
                hidden_turn(2 * (n0 + 1))
                with pe.Fori(1, NJ - 1) as j:
                    for half in range(2):
                        u = b + 2 + half
                        unit_in(u % RING, half, inb, 3 * (j - 1) + u + 1)
                    pe.wait_ge(s_lo, 3 * (j - 1) + b + 5)
                    pe.wait_ge(s_glo, j + h0)
                    slot = (b + 4) % RING
                    out_part(slot, 0, 0)
                    out_part(slot, 0, 1)
                    out_part(slot, 1, 0)
                    hidden_turn(2 * j + 2 * n0 + 2)
                    out_part(slot, 1, 1).then_inc(s_used, 1)
                u = b + 3 * (NJ - 1) - 1
                for t in range(NT):
                    for half in range(2):
                        pe.wait_ge(s_lo, u + half + 1)
                        mm = rows4((u + half) % RING, half, t, inb[t][:, :])
                        if t == NT - 1:
                            mm.then_inc(s_used, 1)
                            if half == 0:
                                pe.wait_ge(s_glo, h0 + NJ - 1)
                                hidden_turn(2 * (n0 + NJ) - 1, [0])
                    if t == 0:
                        mm.then_inc(s_in0, 1)
                pe.wait_ge(s_lo, u + 3)
                out_part((u + 2) % RING, 0, 0)
                out_part((u + 2) % RING, 0, 1)
                pe.wait_ge(s_lo, u + 4)
                pe.wait_ge(s_glo, h0 + NJ)
                out_last((u + 3) % RING, 0)
                hidden_turn(2 * (n0 + NJ), [1])
                out_part((u + 2) % RING, 1, 0)
                pe.wait_ge(s_glo, h0 + NJ + 1)
                if following:
                    turn(following, 0)
                out_part((u + 2) % RING, 1, 1).then_inc(s_used, 1)
                out_last((u + 3) % RING, 1)

            def tail(cols):
                for k in range(KT):
                    col = slice(k * cols, (k + 1) * cols)
                    mm = three(acc[2][0:cols, 0:SEQ], gwhi[:, col], gwlo[:, col], thi[:, k, :], tlo[:, k, :],
                               k == 0, k == KT - 1)
                mm.then_inc(s_tail, 1)

            def round_(r, parts):
                if r % 12 >= 2:
                    pe.wait_ge(s_ra, r - 1)
                    pe.wait_ge(s_rd, r - 1)
                for k, src in enumerate(parts):
                    for t in range(NT):
                        mm = pe.transpose(tb[r % 2][:, k * SEQ + t * P:k * SEQ + (t + 1) * P],
                                          src(t), ident[:, :])
                mm.then_inc(s_rt, 1)

            def kv_round(r, kind, g0):
                round_(r, [lambda t, g=g: kd[:, t, kind, g].rearrange("p u d -> p (u d)")
                           for g in (g0, g0 + 1)])

            def pair_round(r, m, i):
                round_(r, [lambda t, p=p: m[:, t, p * P:(p + 1) * P] for p in (2 * i, 2 * i + 1)])

            def scores(n, kidx, p):
                s1, s0 = acc[2 * (n % 2)], acc[2 * (n % 2) + 1]
                pe.matmul(s1[:, :], qT[:, p, P:2 * P], kblk[:, :, kidx, :], start=True,
                          stop=True).then_inc(s_qk, 1)
                pe.matmul(s0[:, 0:2 * P], qT[:, p, 0:P], kblk[:, :, kidx, 0:P], start=True,
                          stop=True).then_inc(s_qk, 1)

            def turn_probs(n, n_first):
                pe.wait_ge(s_exp, 4 * n + 4)
                if n > n_first:
                    pe.wait_ge(s_pta, n)
                    pe.wait_ge(s_ptd, n)
                for h in range(2):
                    parts = [h * P, 2 * P + h * SEQ, 2 * P + h * SEQ + P]
                    for i, c in enumerate(parts):
                        mm = pe.transpose(tb[h][:, i * P:(i + 1) * P], probs[:, n % 2, c:c + P],
                                          ident[:, :])
                    mm.then_inc(s_pt, 1)

            def values(n, n_first, v):
                pe.wait_ge(s_pta, n + 1)
                pe.wait_ge(s_ptd, n + 1)
                if n > n_first:
                    pe.wait_ge(s_on, n)
                for h in range(2):
                    o = inb[0]
                    mm = pe.matmul(o[:, h * DH:(h + 1) * DH], pT[:, n % 2, h, 0:P], v(0, h),
                                   start=True, stop=True)
                    for k in range(2):
                        mm = pe.matmul(o[:, P + h * DH:P + (h + 1) * DH],
                                       pT[:, n % 2, h, (1 + k) * P:(2 + k) * P], v(k, h),
                                       start=k == 0, stop=k == 1)
                mm.then_inc(s_pv, 1)

            def items(n0, kidx, v, count, before, between):
                for i in range(count + 1):
                    if i + 1 < count:
                        scores(n0 + i + 1, kidx(i + 1), (i + 1) % 8)
                    if i in before:
                        before[i]()
                    if i < count:
                        turn_probs(n0 + i, n0)
                    if i >= 1:
                        values(n0 + i - 1, n0, v(i - 1))
                    if i in between:
                        between[i]()

            def turn_o(g, first):
                if g:
                    pe.wait_ge(s_olo, first + g)
                if first:
                    pe.wait_ge(s_on, 16 + 2 * g + 2)
                else:
                    pe.wait_ge(s_oadd, 2 * g + 2)
                for i in range(2):
                    for t in range(NT):
                        p = 2 * g + i
                        mm = pe.transpose(inb[1][:, i * SEQ + t * P:i * SEQ + (t + 1) * P],
                                          xn[:, t, p * P:(p + 1) * P], ident[:, :])
                mm.then_inc(s_ot, 1)

            def project_first(b, first):
                pe.wait_ge(s_lo, b + 1)
                pe.wait_ge(s_olo, first + 2)
                rows4(b % RING, 0, 0, acc[0][:, :])

            def project_out(b, first, following):
                rows4(b % RING, 0, 1, acc[1][:, :]).then_inc(s_used, 1)
                turn_o(3, first)
                pe.wait_ge(s_lo, b + 2)
                pe.wait_ge(s_olo, first + 3)
                rows4((b + 1) % RING, 1, 0, acc[0][:, :], (s_olo, first + 4))
                rows4((b + 1) % RING, 1, 1, acc[1][:, :]).then_inc(s_used, 1)
                last_chunk(b + 2, acc[2:4], following)

            def warm_up(n):
                for _ in range(n):
                    pe.transpose(acc[1][:, 0:P], ident[:, :], ident[:, :])

            pe.wait_ge(s_const, 1)
            warm_up(10)
            pe.wait_ge(s_small[0], 16)
            pe.wait_ge(s_small[1], 16)
            pe.transpose(inb[1][:, 0:56], work[0:56, 0:P], ident[0:56, 0:56]).then_inc(s_setup_t, 1)
            turn("ffn0", 0)
            pe.wait_ge(s_small[2], 16)
            pe.wait_ge(s_small[3], 16)
            pe.transpose(acc[0][:, 64:96], work[0:32, P:2 * P], ident[0:32, 0:32])
            pe.transpose(acc[0][0:H, 96:128], rel_s[:, :], ident[0:NB, 0:NB]).then_inc(s_setup_t, 1)
            warm_up(10)
            ffn(0, "nsa")

            first_chunk(U_NSA, inb, "nsa")
            unit(U_NSA, 1, 0, acc[0:2])
            copied(1)
            kv_round(0, 0, 0)
            kv_round(1, 0, 2)
            unit(U_NSA, 1, 1, acc[0:2])
            kv_round(2, 1, 0)
            kv_round(3, 1, 2)
            pe.wait_ge(s_tailw, 2)
            tail(NG)
            unit(U_NSA, 2, 0, inb)
            pe.wait_ge(s_tailc, 1)
            for t in range(NT):
                mm = pe.transpose(acc[3][:, t * NG:(t + 1) * NG], gateT[:, t * P:(t + 1) * P],
                                  ident[0:NG, 0:NG])
            mm.then_inc(s_tailt, 1)
            copied(2)
            kv_round(4, 2, 0)
            kv_round(5, 2, 2)
            unit(U_NSA, 2, 1, inb)

            def compress(xk, i):
                u = U_CMP[xk] + i
                pe.wait_ge(s_lo, u + 1)
                for k in range(8):
                    c = 8 * i + k
                    col = slice(k * CMP_HIDDEN, (k + 1) * CMP_HIDDEN)
                    win = slice(c * GN, (c + 1) * GN)
                    mm = three(acc[xk][0:GN, 0:CMP_HIDDEN], win_hi[:, win], win_lo[:, win],
                               whi[u % RING][:, col], wlo[u % RING][:, col], c == 0, c == 15)
                mm.then_inc(s_used, 1)

            def turn_hidden(xk):
                pe.wait_ge(s_hid, xk + 1)
                if xk:
                    pe.wait_ge(s_hidc, 1)
                for c in range(2):
                    mm = pe.transpose(inb[0][:, (2 * xk + c) * GN:(2 * xk + c + 1) * GN],
                                      hid[:, xk, c * P:(c + 1) * P], ident[0:GN, 0:GN])
                mm.then_inc(s_hidt, 1)

            pe.wait_ge(s_flo, 1)
            compress(0, 0)
            copied(3)
            kv_round(6, 3, 0)
            kv_round(7, 3, 2)
            compress(0, 1)
            pe.wait_ge(s_gate, 1)
            unit(U_NSAQ[0], 0, 0, acc[2:4])
            unit(U_NSAQ[0], 0, 1, acc[2:4])
            turn_hidden(0)
            pe.wait_ge(s_flo, 2)
            compress(1, 0)
            copied(4)
            pair_round(8, xn, 0)
            pair_round(9, xn, 1)
            compress(1, 1)
            unit(U_NSAQ[1], 0, 0, acc[2:4])
            turn_hidden(1)
            unit(U_NSAQ[1], 0, 1, acc[2:4])
            pe.wait_ge(s_ra, 10)
            pe.wait_ge(s_rd, 10)

            def cmp_layer2():
                for c in range(2):
                    pe.matmul(inb[1][:, 0:GN], w2k[:, c].rearrange("p u d -> p (u d)"), hidk[:, c, :],
                              start=c == 0, stop=c == 1)
                for e in range(2):
                    for c in range(2):
                        mm = pe.matmul(inb[1][0:HN, 64 + e * DH:64 + (e + 1) * DH],
                                       hidv_rows[:, c, e * HN:(e + 1) * HN], w2v[:, c, :],
                                       start=c == 0, stop=c == 1)
                mm.then_inc(s_cmp2, 1)

            def cmp_scores():
                pe.wait_ge(s_kcb, 1)
                for t in range(NT):
                    for p in range(H // 2):
                        c0 = t * H * NCMP + 2 * p * NCMP
                        mm = pe.matmul(inb[1][:, c0:c0 + 2 * NCMP], qT[:, p, t * P:(t + 1) * P],
                                       kcb[:, p // 2].rearrange("p u n -> p (u n)"), start=True, stop=True)
                mm.then_inc(s_sc, 1)

            def cmp_turn():
                pe.wait_ge(s_cp, 1)
                for t in range(NT):
                    for e in range(2):
                        c0 = (t * H + 8 * e) * NCMP
                        mm = pe.transpose(inb[1][0:HN, (2 * t + e) * P:(2 * t + e + 1) * P],
                                          pc[:, c0:c0 + HN], ident[:, :])
                mm.then_inc(s_cpt, 1)

            def cmp_values(c):
                t, e = CMP_PIECES[c]
                if c == 0:
                    pe.wait_ge(s_cpc, 1)
                else:
                    pe.wait_ge(s_cog, c)
                pe.matmul(inb[1][:, :], pcT[:, 2 * t + e, :], vblk[:, e].rearrange("p h d -> p (h d)"),
                          start=True, stop=True).then_inc(s_co, 1)

            scores(0, 0, 0)
            pe.wait_ge(s_hidc, 2)
            cmp_layer2()
            copied(5)
            pair_round(10, xn, 2)
            pair_round(11, xn, 3)

            def rounds_copied(n):
                pe.wait_ge(s_ra, n)
                pe.wait_ge(s_rd, n)

            items(0, lambda i: i // 2, lambda i: (lambda k, h: vd[:, k, i // 8, (i % 8 // 2) * DH:
                                                              (i % 8 // 2 + 1) * DH]), 16,
                  {0: lambda: rounds_copied(12), 15: lambda: project_first(U_NSA_OUT, 0)},
                  {1: cmp_scores, 4: cmp_turn, 6: lambda: cmp_values(0), 7: lambda: cmp_values(1),
                   8: lambda: cmp_values(2), 9: lambda: cmp_values(3), 11: lambda: turn_o(0, 0),
                   13: lambda: turn_o(1, 0), 15: lambda: turn_o(2, 0)})
            project_out(U_NSA_OUT, 0, "ffn1")
            ffn(1, "kv")

            first_chunk(U_KV, inb, "kv")
            pe.wait_ge(s_tailw, 4)
            pe.wait_ge(s_rstd_h, 1)
            for t in range(NT):
                pe.matmul(acc[3][0:H, t * P:(t + 1) * P], rstd_h[:, t, :], ident[:, :], start=True, stop=True)
            tail(H)
            unit(U_KV, 1, 0, acc[0:2])
            unit(U_KV, 1, 1, acc[0:2])
            copied(6)
            pair_round(12, kf, 0)
            pair_round(13, kf, 1)
            unit(U_KV, 2, 0, inb)
            copied(7)
            pair_round(14, kf, 2)
            pair_round(15, kf, 3)
            unit(U_KV, 2, 1, inb)
            pe.wait_ge(s_neg, 1)
            for t in range(NT):
                mm = pe.transpose(acc[2][:, t * H:(t + 1) * H], rfl[:, t * P:(t + 1) * P],
                                  ident[0:H, 0:H])
            mm.then_inc(s_ct, 1)

            def kv_banks_free():
                rounds_copied(16)
                pe.wait_ge(s_cq, 1)

            last_chunk(U_KV + 6, acc[0:2], "ffn2", kv_banks_free)
            ffn(2, "fox")

            first_chunk(U_FOXQ, acc[0:2], "fox")
            unit(U_FOXQ, 1, 0, inb)
            copied(10)
            pair_round(16, xn, 0)
            pair_round(17, xn, 1)
            unit(U_FOXQ, 1, 1, inb)
            pe.wait_ge(s_ra, 17)
            pe.wait_ge(s_rd, 17)
            scores(16, 0, 0)
            copied(11)
            pair_round(18, xn, 2)
            pair_round(19, xn, 3)
            items(16, lambda i: i, lambda i: (lambda k, h: vf[:, k, (2 * i + h) * DH:(2 * i + h + 1) * DH]), 8,
                  {0: lambda: rounds_copied(20), 7: lambda: project_first(U_FOX_OUT, 4)},
                  {3: lambda: turn_o(0, 4), 5: lambda: turn_o(1, 4), 7: lambda: turn_o(2, 4)})
            project_out(U_FOX_OUT, 4, "ffn3")
            ffn(3)

        @block.scalar
        def _(act):
            def hi(u):
                if u >= U_END:
                    return
                act.wait_ge(s_raw[u % RING], 32 * (u // RING + 1))
                if u >= RING:
                    act.wait_ge(s_used, u - RING + 1)
                act.copy(whi[u % RING][:, :], raw[u % RING][:, :]).then_inc(s_hi, 1)

            def hi_loop(u, j):
                act.wait_ge(s_raw[u % RING], 32 * (j - 1) + 32 * (u // RING + 1))
                act.wait_ge(s_used, 3 * (j - 1) + u - RING + 1)
                act.copy(whi[u % RING][:, :], raw[u % RING][:, :]).then_inc(s_hi, 1)

            def squares(name, t):
                if name == "ffn0":
                    act.wait_ge(s_x[t], 16)
                else:
                    act.wait_ge(s_xadd, max(added(name, t, 0), added(name, t, 1)))
                act.activation(xn[:, t, :], xs[:, t, :], ACT.Square,
                               accum_out=ss[:, t:t + 1]).then_inc(s_sumsq, 1)

            def rms(name):
                act.wait_ge(s_sumsq, NT * NORMS.index(name) + NT)
                act.activation(ss[:, NT:2 * NT], ss[:, 0:NT], ACT.Sqrt, bias=epst[:, :],
                               scale=1.0 / D).then_inc(s_rms, 1)

            def normed(name):
                act.wait_ge(s_rstd, NORMS.index(name) + 1)

            def turned_half(name, t, e):
                tok = slice(t * P, (t + 1) * P)
                bank = tbanks[2 * t + e]
                act.wait_ge(s_tt, 4 * TURNS.index(name) + 2 * t + e + 1)
                for k in range(4):
                    g = GAIN[name] * KT + 4 * e + k
                    ins = act.mul(thi[:, 4 * e + k, tok], bank[:, k * P:(k + 1) * P], gains[:, g:g + 1])
                ins.then_inc(s_thi, 1)

            def turned(name, t):
                for e in range(2):
                    turned_half(name, t, e)

            def o_hi(g, first):
                act.wait_ge(s_ot, first + g + 1)
                act.copy(thi[:, 2 * g:2 * g + 2, :].rearrange("p k n -> p (k n)"),
                         inb[1][:, :]).then_inc(s_ohi, 1)

            def boundary(name, u):
                squares(name, 0)
                turned(name, 0)
                hi(u)
                squares(name, 1)
                turned(name, 1)
                hi(u + 1)
                rms(name)
                normed(name)

            def silu_tile(t):
                act.activation(sa[:, t, :], inb[t][:, 0:FC], ACT.Silu, scale=rstd[:, t:t + 1]).then_inc(s_silu, 1)

            def silu(used):
                act.wait_ge(s_used, used)
                for t in range(NT):
                    silu_tile(t)

            def hidden_hi(n):
                act.wait_ge(s_gt, n)
                act.copy(ghi[:, :, :].rearrange("p k n -> p (k n)"), tb[0][:, :]).then_inc(s_ghi, 1)

            def hidden_last_hi(n, t):
                act.wait_ge(s_gt, n)
                tok = slice(t * P, (t + 1) * P)
                act.copy(ghi_last[:, :, tok],
                         tb[0][:, :].rearrange("p (k n) -> p k n", k=2)[:, :, tok]).then_inc(s_ghi, 1)

            def ffn(f):
                b, h0 = U_FFN[f], (NJ + 1) * f
                act.wait_ge(s_in0, 2 * f + 1)
                silu_tile(0)
                act.wait_ge(s_used, b + 2)
                silu_tile(1)
                hi(b + 3)
                hi(b + 4)
                with act.Fori(1, NJ - 1) as j:
                    act.wait_ge(s_used, 3 * (j - 1) + b + 2)
                    hidden_hi(j + h0)
                    hi_loop(b + 5, j)
                    silu(3 * (j - 1) + b + 4)
                    hi_loop(b + 6, j)
                    hi_loop(b + 7, j)
                act.wait_ge(s_used, 3 * (NJ - 2) + b + 2)
                hidden_hi(h0 + NJ - 1)
                act.wait_ge(s_in0, 2 * f + 2)
                silu_tile(0)
                hidden_last_hi(h0 + NJ, 0)
                hi(b + FFN_UNITS - 1)
                act.wait_ge(s_used, b + FFN_UNITS - 2)
                silu_tile(1)
                hi(b + FFN_UNITS)
                hidden_last_hi(h0 + NJ + 1, 1)

            def chunk_q(bank, c, used):
                act.wait_ge(s_used, used)
                act.mul(xn[:, 0, c * CW:(c + 1) * CW], bank[:, :], rstd_q[:, :]).then_inc(s_nat_a, 1)

            def lower(r, dst):
                act.wait_ge(s_rt, r + 1)
                act.copy(dst, tb[r % 2][0:DH, :]).then_inc(s_ra, 1)

            def q_half(r, i):
                act.wait_ge(s_rt, r + 1)
                act.copy(qT[:, 2 * i, :], tb[r % 2][:, 0:SEQ]).then_inc(s_ra, 1)

            def exps(n):
                act.wait_ge(s_nmax, n + 1)
                for i in range(4):
                    t, h = divmod(i, 2)
                    c0, w = (h * P, P) if t == 0 else (2 * P + h * SEQ, SEQ)
                    act.activation(probs[:, n % 2, c0:c0 + w], probs[:, n % 2, c0:c0 + w], ACT.Exp,
                                   bias=nmx[:, n % 4, i:i + 1],
                                   accum_out=lsum[:, n % 4, i:i + 1]).then_inc(s_exp, 1)

            def pt_copy(n):
                act.wait_ge(s_pt, 2 * n + 1)
                act.copy(pT[:, n % 2, 0, :], tb[0][:, 0:3 * P]).then_inc(s_pta, 1)

            def items(n0, count, between):
                exps(n0)
                for i in range(count):
                    pt_copy(n0 + i)
                    if i + 1 < count:
                        exps(n0 + i + 1)
                    if i in between:
                        between[i]()

            for i, (dst, src) in enumerate([
                    (work[0:48, 0:P], norm_g.rearrange("l n (k p) -> (l n k) p", p=P)),
                    (work[48:56, 0:P], kv_norm_g.rearrange("(k p) -> k p", p=P)),
                    (work[0:32, P:2 * P], nsa_cmp_pos.rearrange("l x (t c) d -> (l x t) (c d)", c=2)),
                    (rel_s[:, :], rel_bias)]):
                act.dma_start(dst, src).then_inc(s_small[i], 16)
            act.wait_ge(s_const, 1)
            act.mul(junk[:, 2:3], epst[:, :], 1.0)
            act.wait_ge(s_setup, 1)
            turned_half("ffn0", 0, 0)
            act.wait_ge(s_raw[0], 32)
            act.copy(whi[0][:, 0:UNIT // 2], raw[0][:, 0:UNIT // 2]).then_inc(s_half0, 1)
            act.copy(whi[0][:, UNIT // 2:UNIT], raw[0][:, UNIT // 2:UNIT]).then_inc(s_hi, 1)
            turned_half("ffn0", 0, 1)
            hi(1)
            squares("ffn0", 0)
            squares("ffn0", 1)
            turned("ffn0", 1)
            hi(2)
            rms("ffn0")
            normed("ffn0")
            ffn(0)

            boundary("nsa", U_NSA + 1)
            act.wait_ge(s_small2, 16 * 6)
            act.copy(gwhi[:, 0:KT * NG], gate_w[:, :, :].rearrange("p k n -> p (k n)")).then_inc(s_tailw, 1)
            hi(U_NSA + 3)
            act.wait_ge(s_used, U_NSA + 2)
            act.mul(kd[:, 0, 0:2].rearrange("p k g u d -> p (k g) u d"),
                    inb[0][:, :].rearrange("p (g d) -> p g d", d=DH).unsqueeze(2)
                    .broadcast_to([P, 8, 2, DH]), rstd[:, 0:1]).then_inc(s_nat_a, 1)
            hi(U_NSA + 4)

            def kv_copy(bank, kind, a, used):
                act.wait_ge(s_used, used)
                act.mul(kd[:, 0, kind], bank[:, 0:KVD].rearrange("p (g d) -> p g d", d=DH).unsqueeze(2)
                        .broadcast_to([P, G, 2, DH]), rstd[:, 0:1])
                act.mul(vd[:, 0, a, :], bank[:, KVD:2 * KVD], rstd[:, 0:1]).then_inc(s_nat_a, 1)

            def even_tokens(r):
                act.wait_ge(s_rt, r + 1)
                act.copy(k2[0:DH, r // 2, 2 * (r % 2):2 * (r % 2) + 2, :],
                         tb[r % 2][0:DH, :].rearrange("p (g m s) -> p g m s", g=2, s=2)[:, :, :, 0]
                         ).then_inc(s_ra, 1)

            def window_hi(xk):
                act.wait_ge(s_fsum, xk + 1)
                if xk:
                    act.wait_ge(s_used, U_CMP[0] + 2)
                act.copy(win_hi, fsum[:, xk, :]).then_inc(s_fhi, 1)

            def cmp_silu(xk):
                act.wait_ge(s_fsum, 2)
                act.wait_ge(s_flo, 1)
                act.wait_ge(s_used, U_CMP[xk] + 2)
                act.activation(hid[:, xk, :], acc[xk][0:GN, 0:CMP_HIDDEN], ACT.Silu).then_inc(s_hid, 1)

            def cmp_hidden_copy(xk):
                act.wait_ge(s_hidt, xk + 1)
                act.wait_ge(s_flo, 2)
                src = inb[0][:, 2 * xk * GN:(2 * xk + 2) * GN]
                if xk == 0:
                    act.copy(hidk.rearrange("p c n -> p (c n)"), src).then_inc(s_hidc, 1)
                    return
                for c in range(2):
                    ins = act.copy(hidv[:, c], src[:, c * GN:(c + 1) * GN].rearrange("p (g n) -> p g n", g=G)
                                   .unsqueeze(2).broadcast_to([P, G, 4, NCMP]))
                ins.then_inc(s_hidc, 1)

            even_tokens(0)
            even_tokens(1)
            hi(U_NSA + 5)
            kv_copy(acc[0], 2, 0, U_NSA + 4)
            even_tokens(2)
            even_tokens(3)
            act.wait_ge(s_tail, 1)
            act.copy(gateT, acc[2][0:NG, 0:SEQ]).then_inc(s_tailc, 1)
            hi(U_NSA + 6)
            window_hi(0)
            act.wait_ge(s_tailt, 1)
            for t in range(NT):
                ins = act.activation(gate[:, t, :], acc[3][:, t * NG:(t + 1) * NG], ACT.Sigmoid,
                                     scale=rstd[:, t:t + 1])
            ins.then_inc(s_gate, 1)
            for r in range(2):
                lower(4 + r, kblk[0:DH, 0, 2 * r:2 * r + 2, :])
            hi(U_NSA + 7)
            kv_copy(inb[0], 3, 1, U_NSA + 6)
            hi(U_NSA + 8)
            for r in range(2):
                lower(6 + r, kblk[0:DH, 0, 4 + 2 * r:6 + 2 * r, :])
            hi(U_NSA + 9)
            window_hi(1)
            hi(U_NSA + 10)
            cmp_silu(0)
            hi(U_NSA + 11)
            chunk_q(acc[2], 0, U_NSA + 10)
            cmp_hidden_copy(0)
            hi(U_NSA + 12)
            q_half(8, 0)
            q_half(9, 1)
            hi(U_NSA + 13)
            cmp_silu(1)
            hi(U_NSA + 14)
            cmp_hidden_copy(1)
            hi(U_NSA + 15)
            act.activation(junk[:, 0:1], epst[:, :], ACT.Exp)
            chunk_q(acc[2], 1, U_NSA + 14)
            q_half(10, 2)
            q_half(11, 3)

            def cmp_exp():
                act.wait_ge(s_csh, 1)
                act.activation(pc, pc, ACT.Exp).then_inc(s_cexp, 1)

            def cmp_copy():
                act.wait_ge(s_cpt, 1)
                act.copy(pcT.rearrange("p c n -> p (c n)"), inb[1][0:HN, :]).then_inc(s_cpc, 1)

            items(0, 16, {2: cmp_exp, 5: cmp_copy, 11: lambda: o_hi(0, 0), 13: lambda: o_hi(1, 0),
                          15: lambda: o_hi(2, 0)})
            o_hi(3, 0)
            act.wait_ge(s_hi, U_NSA_OUT + 3)
            hi(U_NSA_OUT + 3)
            hi(U_NSA_OUT + 4)
            boundary("ffn1", U_FFN1 + 1)
            ffn(1)

            boundary("kv", U_KV + 1)
            act.copy(gwhi[:, 0:KT * H], fl_w[:, :, :].rearrange("p k n -> p (k n)")).then_inc(s_tailw, 1)
            hi(U_KV + 3)
            act.wait_ge(s_used, U_KV + 2)
            act.mul(kf[:, 0, 0:CW], inb[0][:, :], rstd[:, 0:1]).then_inc(s_nat_a, 1)
            hi(U_KV + 4)
            act.wait_ge(s_fa, 1)
            act.activation(fexp, raux, ACT.Exp).then_inc(s_fexp, 1)
            act.wait_ge(s_fexp, 1)
            act.activation(flog, fexp, ACT.Ln, bias=1.0).then_inc(s_flog, 1)
            hi(U_KV + 5)
            act.wait_ge(s_used, U_KV + 4)
            act.mul(kf[:, 0, CW:2 * CW], acc[0][:, :], rstd[:, 0:1]).then_inc(s_nat_a, 1)
            for i in range(2):
                lower(12 + i, kblk[0:DH, 0, 2 * i:2 * i + 2, :])
            hi(U_KV + 6)
            for i in range(2, 4):
                lower(12 + i, kblk[0:DH, 0, 2 * i:2 * i + 2, :])
            hi(U_KV + 7)
            act.wait_ge(s_used, U_KV + 6)
            act.mul(vf[:, 0, 0:CW], inb[0][:, :], rstd[:, 0:1]).then_inc(s_nat_a, 1)
            hi(U_KV + 8)
            act.wait_ge(s_tile0, TILE0.index("kv") + 1)
            act.mul(vf[:, 0, CW:2 * CW], acc[0][:, :], rstd[:, 0:1]).then_inc(s_nat_a, 1)
            turned("ffn2", 0)
            hi(U_KV + 9)
            turned("ffn2", 1)
            hi(U_FFN2 + 2)
            ffn(2)

            boundary("fox", U_FOXQ + 1)
            hi(U_FOXQ + 3)
            chunk_q(acc[0], 0, U_FOXQ + 2)
            hi(U_FOXQ + 4)
            q_half(16, 0)
            q_half(17, 1)
            hi(U_FOXQ + 5)
            act.activation(junk[:, 1:2], epst[:, :], ACT.Exp)
            chunk_q(inb[0], 1, U_FOXQ + 4)
            q_half(18, 2)
            q_half(19, 3)
            items(16, 8, {3: lambda: o_hi(0, 4), 5: lambda: o_hi(1, 4),
                          7: lambda: o_hi(2, 4)})
            o_hi(3, 4)
            act.wait_ge(s_hi, U_FOX_OUT + 3)
            hi(U_FOX_OUT + 3)
            hi(U_FOX_OUT + 4)
            boundary("ffn3", U_FFN3 + 1)
            ffn(3)
            for t in range(NT):
                act.wait_ge(s_xadd, added("final", t, 0))
                act.activation(squares_out[:, 0:CW], xs[:, t, 0:CW], ACT.Square,
                               accum_out=half_sq[:, t:t + 1]).then_inc(s_fin, 1)
                act.wait_ge(s_fin, 3 * t + 1)
                act.activation(half_sq[:, NT + t:NT + t + 1], half_sq[:, t:t + 1], ACT.Identity,
                               bias=epst[:, :], scale=1.0 / D).then_inc(s_fin, 1)
                act.wait_ge(s_xadd, added("final", t, 1))
                act.activation(squares_out[:, CW:2 * CW], xs[:, t, CW:2 * CW], ACT.Square,
                               accum_out=ss[:, t:t + 1]).then_inc(s_fin, 1)
                act.wait_ge(s_fin, 3 * t + 3)
                act.activation(ss[:, NT + t:NT + t + 1], ss[:, t:t + 1], ACT.Sqrt,
                               bias=half_sq[:, NT + t:NT + t + 1], scale=1.0 / D).then_inc(s_rms, 1)
                act.wait_ge(s_rfin, t + 1)
                act.mul(xn[:, t, CW:2 * CW], xn[:, t, CW:2 * CW], rstd[:, t:t + 1]).then_inc(s_ya, 1)

        @block.vector
        def _(dve):
            steps = [0]

            def step(ins):
                steps[0] += 1
                ins.then_inc(s_step, 1)
                dve.wait_ge(s_step, steps[0])

            def lo(u):
                if u >= U_END:
                    return
                dve.wait_ge(s_hi, u + 1)
                dve.tensor_tensor(wlo[u % RING][:, :], raw[u % RING][:, :],
                                  whi[u % RING][:, :].bitcast(F32), ALU.subtract).then_inc(s_lo, 1)

            def lo_loop(u, j):
                dve.wait_ge(s_hi, 3 * (j - 1) + u + 1)
                dve.tensor_tensor(wlo[u % RING][:, :], raw[u % RING][:, :],
                                  whi[u % RING][:, :].bitcast(F32), ALU.subtract).then_inc(s_lo, 1)

            def root(name):
                dve.wait_ge(s_rms, NORMS.index(name) + 1)
                step(dve.reciprocal(rstd[:, :], ss[:, NT:2 * NT]))
                dve.tensor_scalar(rstd_q[:, :], rstd[:, 0:1], SCALE, None, ALU.mult).then_inc(s_rstd, 1)

            def turned_half(name, t, e):
                tok = slice(t * P, (t + 1) * P)
                bank = tbanks[2 * t + e]
                dve.wait_ge(s_thi, 4 * TURNS.index(name) + 2 * t + e + 1)
                for k in range(4):
                    g = GAIN[name] * KT + 4 * e + k
                    ins = dve.scalar_tensor_tensor(
                        out=tlo[:, 4 * e + k, tok], in0=bank[:, k * P:(k + 1) * P], scalar=gains[:, g:g + 1],
                        in1=thi[:, 4 * e + k, tok].bitcast(F32), op0=ALU.mult, op1=ALU.subtract)
                ins.then_inc(s_tlo, 1)

            def turned(name, t):
                for e in range(2):
                    turned_half(name, t, e)

            def o_lo(g, first):
                dve.wait_ge(s_ohi, first + g + 1)
                ks = slice(2 * g, 2 * g + 2)
                dve.tensor_tensor(tlo[:, ks, :].rearrange("p k n -> p (k n)"), inb[1][:, :],
                                  thi[:, ks, :].rearrange("p k n -> p (k n)").bitcast(F32),
                                  ALU.subtract).then_inc(s_olo, 1)

            def boundary(name, u, add):
                turned(name, 0)
                add(1)
                lo(u)
                turned(name, 1)
                lo(u + 1)
                root(name)

            def hidden_tile(n, t):
                dve.wait_ge(s_silu, n + 1)
                dve.scalar_tensor_tensor(out=gg[:, t, :], in0=inb[t][:, FC:2 * FC], scalar=rstd[:, t:t + 1],
                                         in1=sa[:, t, :], op0=ALU.mult, op1=ALU.mult).then_inc(s_g, 1)

            def hidden(n):
                for t in range(NT):
                    hidden_tile(n + t, t)

            def hidden_lo(n):
                dve.wait_ge(s_ghi, n)
                dve.tensor_tensor(glo[:, :, :].rearrange("p k n -> p (k n)"), tb[0][:, :],
                                  ghi[:, :, :].rearrange("p k n -> p (k n)").bitcast(F32),
                                  ALU.subtract).then_inc(s_glo, 1)

            def hidden_last_lo(n, t):
                dve.wait_ge(s_ghi, n)
                tok = slice(t * P, (t + 1) * P)
                dve.tensor_tensor(glo_last[:, :, tok], tb[0][:, :].rearrange("p (k n) -> p k n", k=2)[:, :, tok],
                                  ghi_last[:, :, tok].bitcast(F32), ALU.subtract).then_inc(s_glo, 1)

            def ffn(f):
                b, n0, h0 = U_FFN[f], NJ * f, (NJ + 1) * f
                hidden(2 * n0)
                lo(b + 3)
                lo(b + 4)
                with dve.Fori(1, NJ - 1) as j:
                    hidden_lo(j + h0)
                    lo_loop(b + 5, j)
                    hidden(2 * j + 2 * n0)
                    lo_loop(b + 6, j)
                    lo_loop(b + 7, j)
                hidden_lo(h0 + NJ - 1)
                last = 2 * n0 + 2 * (NJ - 1)
                hidden_tile(last, 0)
                hidden_last_lo(h0 + NJ, 0)
                lo(b + FFN_UNITS - 1)
                hidden_tile(last + 1, 1)
                lo(b + FFN_UNITS)
                ffn_add(f, 0)
                hidden_last_lo(h0 + NJ + 1, 1)

            def ffn_add(f, t):
                for n in range(2):
                    if (t, n) == (1, 1):
                        dve.wait_ge(s_used, U_FFN[f] + FFN_UNITS)
                    else:
                        dve.wait_ge(s_out_bank, 3 * f + 2 * t + n + 1)
                    xc = xs[:, t, n * CW:(n + 1) * CW]
                    dve.scalar_tensor_tensor(out=xc, in0=acc[2 * t + n][:, :], scalar=0.5, in1=xc,
                                             op0=ALU.mult, op1=ALU.add).then_inc(s_xadd, 1)

            def mixer_add(name, b, c, t):
                if c == 1 and t == 0:
                    dve.wait_ge(s_tile0, TILE0.index(name) + 1)
                else:
                    dve.wait_ge(s_used, b + 2 * c + 2)
                xc = xs[:, t, c * CW:(c + 1) * CW]
                dve.tensor_tensor(xc, acc[2 * c + t][:, :], xc, ALU.add).then_inc(s_xadd, 1)

            def chunk_q(bank, c, used):
                dve.wait_ge(s_used, used)
                dve.tensor_scalar(xn[:, 1, c * CW:(c + 1) * CW], bank[:, :], rstd[:, 1:2], SCALE,
                                  ALU.mult, ALU.mult).then_inc(s_nat_d, 1)

            def upper(r, dst):
                dve.wait_ge(s_rt, r + 1)
                dve.tensor_copy(dst, tb[r % 2][DH:P, :]).then_inc(s_rd, 1)

            def q_half(r, i):
                dve.wait_ge(s_rt, r + 1)
                dve.wait_ge(s_ra, r + 1)
                dve.tensor_copy(qT[:, 2 * i + 1, :], tb[r % 2][:, SEQ:2 * SEQ]).then_inc(s_rd, 1)

            def add_max(n, p, table0):
                for i in (2, 3, 0, 1):
                    t, h = divmod(i, 2)
                    if h == 0:
                        dve.wait_ge(s_qk, 2 * n + (1 if t else 2))
                    if t:
                        dst = probs[:, n % 2, 2 * P + h * SEQ:2 * P + (h + 1) * SEQ]
                        src = acc[2 * (n % 2)][:, h * SEQ:(h + 1) * SEQ]
                        tab = bias[:, 2 * p + h, :]
                    else:
                        dst = probs[:, n % 2, h * P:(h + 1) * P]
                        src = acc[2 * (n % 2) + 1][:, h * P:(h + 1) * P]
                        tab = table0(2 * p + h)
                    dve.tensor_tensor_reduce(dst, src, tab, 1.0, -3e38, ALU.add, ALU.max,
                                             mx[:, n % 4, i:i + 1]).then_inc(s_max, 1)
                dve.wait_ge(s_max, 4 * n + 4)
                dve.tensor_scalar(nmx[:, n % 4, :], mx[:, n % 4, :], -1.0, None, ALU.mult).then_inc(s_nmax, 1)

            def pt_copy(n):
                dve.wait_ge(s_pt, 2 * n + 2)
                dve.tensor_copy(pT[:, n % 2, 1, :], tb[1][:, 0:3 * P]).then_inc(s_ptd, 1)

            def output(n, p, branch, direct):
                if n:
                    dve.wait_ge(s_on, n)
                dve.wait_ge(s_pv, n + 1)
                step(dve.reciprocal(linv[:, :], lsum[:, n % 4, :]))
                o = inb[0][:, 0:2 * P].rearrange("p (t h d) -> p t h d", t=2, h=2)
                if branch is None:
                    w, dst = linv, onat[:, :, 2 * p:2 * p + 2, :]
                else:
                    g = gate[:, :, :].rearrange("p t (h c) -> p t h c", c=3)[:, :, 2 * p:2 * p + 2, branch]
                    step(dve.tensor_tensor(lw[:, :].rearrange("p (t h) -> p t h", t=2),
                                           linv[:, :].rearrange("p (t h) -> p t h", t=2), g, ALU.mult))
                    w, dst = lw, onat[:, :, 2 * p:2 * p + 2, :] if direct else otmp[:, n % 2]
                    if n >= 10:
                        dve.wait_ge(s_oadd, n - 9)
                dve.tensor_tensor(dst, o, w[:, :].rearrange("p (t h) -> p t h", t=2).unsqueeze(3)
                                  .broadcast_to([P, 2, 2, DH]), ALU.mult).then_inc(s_on, 1)

            def items(n0, count, pair, table0, branch, between):
                for i in range(count + 1):
                    if i + 1 < count:
                        add_max(n0 + i + 1, pair(i + 1), table0)
                    if i < count:
                        pt_copy(n0 + i)
                    if i >= 1:
                        output(n0 + i - 1, pair(i - 1), branch(i - 1), i <= 8)
                    if i in between:
                        between[i]()

            dve.wait_ge(s_setup_t, 1)
            dve.tensor_copy(gains[:, :], inb[1][:, 0:56]).then_inc(s_setup, 1)
            dve.wait_ge(s_setup, 1)
            turned_half("ffn0", 0, 0)
            dve.wait_ge(s_half0, 1)
            dve.tensor_tensor(wlo[0][:, 0:UNIT // 2], raw[0][:, 0:UNIT // 2],
                              whi[0][:, 0:UNIT // 2].bitcast(F32), ALU.subtract).then_inc(s_half1, 1)
            dve.wait_ge(s_hi, 1)
            dve.tensor_tensor(wlo[0][:, UNIT // 2:UNIT], raw[0][:, UNIT // 2:UNIT],
                              whi[0][:, UNIT // 2:UNIT].bitcast(F32), ALU.subtract).then_inc(s_lo, 1)
            turned_half("ffn0", 0, 1)
            dve.wait_ge(s_setup_t, 2)
            dve.tensor_copy(posT[:, :], acc[0][:, 64:96])
            dve.tensor_copy(tbT[:, :], acc[0][0:H, 96:128]).then_inc(s_setup, 1)
            lo(1)
            turned("ffn0", 1)
            lo(2)
            root("ffn0")
            ffn(0)

            boundary("nsa", U_NSA + 1, lambda t: ffn_add(0, t))
            dve.wait_ge(s_tailw, 1)
            dve.tensor_tensor(gwlo[:, 0:KT * NG], gate_w[:, :, :].rearrange("p k n -> p (k n)"),
                              gwhi[:, 0:KT * NG].bitcast(F32), ALU.subtract).then_inc(s_tailw, 1)
            lo(U_NSA + 3)
            dve.wait_ge(s_used, U_NSA + 2)
            dve.tensor_scalar(kd[:, 1, 0:2].rearrange("p k g u d -> p (k g) u d"),
                              inb[1][:, :].rearrange("p (g d) -> p g d", d=DH).unsqueeze(2)
                              .broadcast_to([P, 8, 2, DH]), rstd[:, 1:2], None, ALU.mult).then_inc(s_nat_d, 1)
            lo(U_NSA + 4)

            def kv_copy(bank, kind, a, used):
                dve.wait_ge(s_used, used)
                dve.tensor_scalar(kd[:, 1, kind], bank[:, 0:KVD].rearrange("p (g d) -> p g d", d=DH)
                                  .unsqueeze(2).broadcast_to([P, G, 2, DH]), rstd[:, 1:2], None, ALU.mult)
                dve.tensor_scalar(vd[:, 1, a, :], bank[:, KVD:2 * KVD], rstd[:, 1:2], None, ALU.mult).then_inc(s_nat_d, 1)

            def odd_tokens(r):
                dve.wait_ge(s_rt, r + 1)
                dve.tensor_copy(k2[DH:P, r // 2, 2 * (r % 2):2 * (r % 2) + 2, :],
                                tb[r % 2][DH:P, :].rearrange("p (g m s) -> p g m s", g=2, s=2)[:, :, :, 1]
                                ).then_inc(s_rd, 1)

            def windows(xk):
                dve.wait_ge(s_ra, 2 * xk + 2)
                dve.wait_ge(s_rd, 2 * xk + 2)
                for th in range(2):
                    tok = k2[:, xk].rearrange("p g (n t) -> p t g n", t=8)[:, :, :, th:th + NCMP]
                    pos = posT[:, 16 * xk + 8 * th:16 * xk + 8 * th + 8].unsqueeze(2).unsqueeze(3)
                    ins = dve.tensor_tensor(
                        fsum[:, xk, th * 8 * GN:(th + 1) * 8 * GN].rearrange("p (t g n) -> p t g n", t=8, g=G),
                        tok, pos.broadcast_to([P, 8, G, NCMP]), ALU.add)
                ins.then_inc(s_fsum, 1)

            def window_lo(xk):
                dve.wait_ge(s_fhi, xk + 1)
                dve.wait_ge(s_fsum, xk + 1)
                dve.tensor_tensor(win_lo, fsum[:, xk, :], win_hi.bitcast(F32),
                                  ALU.subtract).then_inc(s_flo, 1)

            odd_tokens(0)
            odd_tokens(1)
            lo(U_NSA + 5)
            windows(0)
            kv_copy(acc[1], 2, 0, U_NSA + 4)
            odd_tokens(2)
            odd_tokens(3)
            lo(U_NSA + 6)
            window_lo(0)
            for r in range(2):
                upper(4 + r, kblk[DH:P, 1, 2 * r:2 * r + 2, :])
            windows(1)
            lo(U_NSA + 7)
            kv_copy(inb[1], 3, 1, U_NSA + 6)
            lo(U_NSA + 8)
            for r in range(2):
                upper(6 + r, kblk[DH:P, 1, 4 + 2 * r:6 + 2 * r, :])
            lo(U_NSA + 9)
            window_lo(1)
            lo(U_NSA + 10)
            lo(U_NSA + 11)
            chunk_q(acc[3], 0, U_NSA + 10)
            lo(U_NSA + 12)
            q_half(8, 0)
            q_half(9, 1)
            lo(U_NSA + 13)
            lo(U_NSA + 14)
            lo(U_NSA + 15)
            chunk_q(acc[3], 1, U_NSA + 14)

            def cmp_keys_values():
                dve.wait_ge(s_biasc, 1)
                dve.wait_ge(s_cmp2, 1)
                for u in range(2):
                    dve.tensor_copy(kcb[u * DH:(u + 1) * DH, :, u, :],
                                    inb[1][u * DH:(u + 1) * DH, 0:GN].rearrange("p (g n) -> p g n", g=G))
                for e in range(2):
                    v = inb[1][0:HN, 64 + e * DH:64 + (e + 1) * DH].unsqueeze(1).broadcast_to([HN, 8, DH])
                    ins = dve.tensor_tensor(vblk[:, e], v,
                                            blkmask[:, :].unsqueeze(2).broadcast_to([HN, 8, DH]), ALU.mult)
                ins.then_inc(s_kcb, 1)

            pcr = pc.rearrange("p (r n) -> p r n", n=NCMP)

            def cmp_shift():
                dve.wait_ge(s_sc, 1)
                step(dve.tensor_tensor(pc, inb[1][:, 0:NT * H * NCMP],
                                       biasc.rearrange("p t h n -> p (t h n)"), ALU.add))
                step(dve.tensor_reduce(cmx[:, :], pcr, AX.X, ALU.max))
                dve.tensor_tensor(pcr, pcr, cmx[:, :].unsqueeze(2).broadcast_to([P, NT * H, NCMP]),
                                  ALU.subtract).then_inc(s_csh, 1)

            def cmp_probs():
                dve.wait_ge(s_cexp, 1)
                step(dve.tensor_reduce(csum[:, :], pcr, AX.X, ALU.add))
                for t in range(NT):
                    ins = dve.tensor_tensor(pc4[:, t], pc4[:, t],
                                            cmask01[:, t, :].unsqueeze(1).broadcast_to([P, H, NCMP]), ALU.mult)
                ins.then_inc(s_cp, 1)
                step(dve.reciprocal(cw[:, :], csum[:, :]))
                dve.wait_ge(s_gate, 1)
                step(dve.tensor_tensor(cw[:, :].rearrange("p (t h) -> p t h", t=NT),
                                       cw[:, :].rearrange("p (t h) -> p t h", t=NT),
                                       gate[:, :, :].rearrange("p t (h c) -> p t h c", c=3)[:, :, :, 0],
                                       ALU.mult))

            def cmp_gated(c):
                t, e = CMP_PIECES[c]
                dve.wait_ge(s_co, c + 1)
                if c:
                    dve.wait_ge(s_cadd, c)
                w = cw[:, t * H + 8 * e:t * H + 8 * e + 8].unsqueeze(2).broadcast_to([P, 8, DH])
                dve.tensor_tensor(ctmp, inb[1][:, :].rearrange("p (h d) -> p h d", h=8), w,
                                  ALU.mult).then_inc(s_cog, 1)

            dve.wait_ge(s_bias, 64)
            add_max(0, 0, lambda h: bias[:, h, P:2 * P])
            q_half(10, 2)
            q_half(11, 3)
            cmp_keys_values()
            items(0, 16, lambda i: i % 8, lambda h: bias[:, h, P:2 * P], lambda i: 1 + i // 8,
                  {1: cmp_shift, 3: cmp_probs, 6: lambda: cmp_gated(0), 7: lambda: cmp_gated(1),
                   8: lambda: cmp_gated(2), 9: lambda: cmp_gated(3), 11: lambda: o_lo(0, 0),
                   13: lambda: o_lo(1, 0), 15: lambda: o_lo(2, 0)})
            o_lo(3, 0)
            dve.wait_ge(s_lo, U_NSA_OUT + 3)
            lo(U_NSA_OUT + 3)
            for t in range(NT):
                mixer_add("nsa", U_NSA_OUT, 0, t)
            lo(U_NSA_OUT + 4)
            mixer_add("nsa", U_NSA_OUT, 1, 0)
            boundary("ffn1", U_FFN1 + 1, lambda t: mixer_add("nsa", U_NSA_OUT, 1, t))
            ffn(1)

            boundary("kv", U_KV + 1, lambda t: ffn_add(1, t))
            dve.wait_ge(s_tailw, 3)
            dve.tensor_tensor(gwlo[:, 0:KT * H], fl_w[:, :, :].rearrange("p k n -> p (k n)"),
                              gwhi[:, 0:KT * H].bitcast(F32), ALU.subtract).then_inc(s_tailw, 1)
            dve.tensor_copy(rstd_h[:, :, :], rstd[:, :].unsqueeze(2).broadcast_to([P, NT, H])).then_inc(s_rstd_h, 1)
            lo(U_KV + 3)
            dve.wait_ge(s_used, U_KV + 2)
            dve.tensor_scalar(kf[:, 1, 0:CW], inb[1][:, :], rstd[:, 1:2], None, ALU.mult).then_inc(s_nat_d, 1)
            dve.wait_ge(s_tail, 2)
            step(dve.tensor_copy(raux, acc[3][0:H, 0:SEQ]))
            step(dve.tensor_tensor(rfl, acc[2][0:H, 0:SEQ], raux, ALU.mult))
            step(dve.tensor_scalar(rfl, rfl, bf[:, :], None, ALU.add))
            dve.scalar_tensor_tensor(out=raux, in0=rfl, scalar=-1.0, in1=rfl, op0=ALU.mult,
                                     op1=ALU.min).then_inc(s_fa, 1)
            lo(U_KV + 4)
            lo(U_KV + 5)
            dve.wait_ge(s_used, U_KV + 4)
            dve.tensor_scalar(kf[:, 1, CW:2 * CW], acc[1][:, :], rstd[:, 1:2], None, ALU.mult).then_inc(s_nat_d, 1)
            dve.wait_ge(s_flog, 1)
            step(dve.tensor_scalar(fcor, fexp, 1.0, None, ALU.add))
            step(dve.reciprocal(frec, fcor))
            for i in range(2):
                upper(12 + i, kblk[DH:P, 1, 2 * i:2 * i + 2, :])
            step(dve.tensor_scalar(fcor, fcor, -1.0, None, ALU.add))
            step(dve.tensor_tensor(fcor, fexp, fcor, ALU.subtract))
            step(dve.tensor_tensor(fcor, fcor, frec, ALU.mult))
            step(dve.tensor_tensor(flog, flog, fcor, ALU.add))
            step(dve.tensor_scalar(rfl, rfl, 0.0, None, ALU.min))
            step(dve.tensor_tensor(flog, rfl, flog, ALU.subtract))
            step(dve.memset(fcor, 1.0))
            lo(U_KV + 6)
            step(dve.tensor_tensor_scan(rfl, fcor, flog, 0.0, ALU.mult, ALU.add))
            dve.tensor_scalar(raux, rfl, -1.0, None, ALU.mult).then_inc(s_neg, 1)
            for i in range(2, 4):
                upper(12 + i, kblk[DH:P, 1, 2 * i:2 * i + 2, :])
            lo(U_KV + 7)
            dve.wait_ge(s_used, U_KV + 6)
            dve.tensor_scalar(vf[:, 1, 0:CW], inb[1][:, :], rstd[:, 1:2], None, ALU.mult).then_inc(s_nat_d, 1)
            dve.wait_ge(s_ct, 1)
            dve.tensor_copy(cq[:, :, :].rearrange("p t h -> p (t h)"), acc[2][:, 0:NT * H]).then_inc(s_cq, 1)
            lo(U_KV + 8)
            turned("ffn2", 0)
            dve.wait_ge(s_used, U_KV + 8)
            dve.tensor_scalar(vf[:, 1, CW:2 * CW], acc[1][:, :], rstd[:, 1:2], None, ALU.mult).then_inc(s_nat_d, 1)
            lo(U_KV + 9)
            turned("ffn2", 1)
            lo(U_FFN2 + 2)
            ffn(2)

            boundary("fox", U_FOXQ + 1, lambda t: ffn_add(2, t))
            lo(U_FOXQ + 3)
            chunk_q(acc[1], 0, U_FOXQ + 2)
            lo(U_FOXQ + 4)
            q_half(16, 0)
            q_half(17, 1)
            lo(U_FOXQ + 5)
            chunk_q(inb[1], 1, U_FOXQ + 4)
            dve.wait_ge(s_decay, H // 4)
            add_max(16, 0, lambda h: decay0[:, h, :])
            q_half(18, 2)
            q_half(19, 3)
            items(16, 8, lambda i: i, lambda h: decay0[:, h, :], lambda i: None,
                  {3: lambda: o_lo(0, 4), 5: lambda: o_lo(1, 4), 7: lambda: o_lo(2, 4)})
            o_lo(3, 4)
            dve.wait_ge(s_lo, U_FOX_OUT + 3)
            lo(U_FOX_OUT + 3)
            for t in range(NT):
                mixer_add("fox", U_FOX_OUT, 0, t)
            lo(U_FOX_OUT + 4)
            mixer_add("fox", U_FOX_OUT, 1, 0)
            boundary("ffn3", U_FFN3 + 1, lambda t: mixer_add("fox", U_FOX_OUT, 1, t))
            ffn(3)
            dve.wait_ge(s_fg, 16)
            for t in range(NT):
                if t:
                    ffn_add(3, t)
                dve.wait_ge(s_xadd, added("final", t, 1))
                step(dve.tensor_tensor(xn[:, t, :], xs[:, t, :], finalb, ALU.mult))
                dve.wait_ge(s_rms, NORMS.index("final") + t + 1)
                dve.reciprocal(rstd[:, t:t + 1], ss[:, NT + t:NT + t + 1]).then_inc(s_rfin, 1)
                dve.wait_ge(s_rfin, t + 1)
                dve.tensor_scalar(xn[:, t, 0:CW], xn[:, t, 0:CW], rstd[:, t:t + 1], None,
                                  ALU.mult).then_inc(s_y, 1)

        @block.gpsimd
        def _(pool):
            steps = [0]

            def step(ins):
                steps[0] += 1
                ins.then_inc(s_pstep, 1)
                pool.wait_ge(s_pstep, steps[0])

            pool.memset(epst[:, :], EPS)
            step(pool.memset(ident[:, :], 0.0))
            pool.affine_select(out=ident[:, :], in_=ident[:, :], compare_op=ALU.not_equal, fill=1.0, base=0,
                               pattern=[[-1, P]], channel_multiplier=1).then_inc(s_const, 1)
            pool.memset(zeros[:, :], 0.0)
            step(pool.memset(cmask[:, :], 0.0))
            pool.affine_select(out=cmask[:, :], in_=cmask[:, :], compare_op=ALU.is_ge, fill=NEG, base=0,
                               pattern=[[-1, P]], channel_multiplier=1)
            step(pool.memset(cmask01[:, :, :], 1.0))
            for t in range(NT):
                pool.affine_select(out=cmask01[:, t, :], in_=cmask01[:, t, :], compare_op=ALU.is_ge, fill=0.0,
                                   base=t * P - (CMP_BLOCK - 1), pattern=[[-CMP_STRIDE, NCMP]],
                                   channel_multiplier=1)
            step(pool.memset(blkmask[:, :], 1.0))
            step(pool.affine_select(out=blkmask[:, :], in_=blkmask[:, :], compare_op=ALU.is_ge, fill=0.0,
                                    base=0, pattern=[[-NCMP, 8]], channel_multiplier=1))
            pool.affine_select(out=blkmask[:, :], in_=blkmask[:, :], compare_op=ALU.is_ge, fill=0.0,
                               base=NCMP - 1, pattern=[[NCMP, 8]], channel_multiplier=-1)
            pool.memset(kcb[:, :, :, :], 0.0)
            pool.memset(kblk[:, :, :, :], 0.0).then_inc(s_const, 1)
            small = [(gate_w[:, :, :], nsa_w_in[0, :, D + 6 * KVD:].rearrange("(k p) n -> p k n", p=P)),
                     (fl_w[:, :, :], fox_w_kvf[:, 2 * D:].rearrange("(k p) n -> p k n", p=P)),
                     (w2k[:, :, 0, :], nsa_cmp_w2[0, 0].rearrange("(c p) d -> p c d", p=P)),
                     (w2k[:, :, 1, :], nsa_cmp_w2[0, 0].rearrange("(c p) d -> p c d", p=P)),
                     (w2v[:, :, :], nsa_cmp_w2[0, 1].rearrange("(c p) d -> p c d", p=P)),
                     (bf[:, :], fox_b_f.rearrange("(h a) -> h a", a=1))]
            for dst, src in small:
                pool.dma_start(dst, src).then_inc(s_small2, 16)
            pool.wait_ge(s_setup, 2)
            starts = bucket_starts()
            for b in range(NB):
                near, far = starts[b], starts[b + 1] - 1
                pool.tensor_copy(rows[:, SEQ - 1 - far:SEQ - near],
                                 tbT[:, b:b + 1].broadcast_to([H, far - near + 1]))
            pool.memset(rows[:, SEQ:2 * SEQ], NEG).then_inc(s_rows, 1)
            pool.wait_ge(s_rows, 1)
            for i in range(4):
                hs = slice(4 * i, 4 * i + 4)
                pool.dma_start(scratch_b[:, hs, :].rearrange("p h m -> h p m"),
                               rows[hs].unsqueeze(1).broadcast_to([4, P, 512])).then_inc(s_rows_out, 16)
                pool.wait_ge(s_rows_out, 16 * (i + 1))
                pool.dma_start(bias[:, hs, :], bass.AP(tensor=scratch_b.tensor, offset=4 * i * 512 + P - 1,
                                                       ap=[[H * 512 - 1, P], [512, 4], [1, SEQ]])
                               ).then_inc(s_bias, 16)
                pool.wait_ge(s_bias, 16 * (i + 1))
            step(pool.memset(biasc, NEG))
            end = CMP_BLOCK - 1
            pool.tensor_copy(biasc[:, 1], bias[:, :, end:end + (NCMP - 1) * CMP_STRIDE + 1:CMP_STRIDE])
            pool.tensor_copy(biasc[:, 0, :, 0:7],
                             bias[:, :, P + end:P + end + 6 * CMP_STRIDE + 1:CMP_STRIDE]).then_inc(s_biasc, 1)
            def split(u):
                pool.wait_ge(s_raw[u % RING], 32 * (u // RING + 1))
                pool.wait_ge(s_used, u - RING + 1)
                pool.wait_ge(s_hi, u)
                pool.tensor_copy(whi[u % RING][:, :], raw[u % RING][:, :]).then_inc(s_hi, 1)
                pool.wait_ge(s_lo, u)
                pool.wait_ge(s_hi, u + 1)
                pool.tensor_tensor(wlo[u % RING][:, :], raw[u % RING][:, :],
                                   whi[u % RING][:, :].bitcast(F32), ALU.subtract).then_inc(s_lo, 1)

            split(U_NSA_OUT + 2)
            for c, (t, e) in enumerate(CMP_PIECES):
                pool.wait_ge(s_on, 4 * e + 4)
                pool.wait_ge(s_cog, c + 1)
                o = onat[:, t, 8 * e:8 * e + 8, :]
                pool.tensor_tensor(o, o, ctmp, ALU.add).then_inc(s_cadd, 1)
            pool.wait_ge(s_cadd, len(CMP_PIECES))
            for n in range(8, 16):
                pool.wait_ge(s_on, n + 1)
                o = onat[:, :, 2 * (n % 8):2 * (n % 8) + 2, :]
                pool.tensor_tensor(o, o, otmp[:, n % 2], ALU.add).then_inc(s_oadd, 1)
            pool.wait_ge(s_neg, 1)
            pool.dma_start(scratch_c, raux).then_inc(s_cst, 16)
            pool.wait_ge(s_cst, 16)
            pool.dma_start(bias[:, :, :].rearrange("p h n -> p (h n)"),
                           bass.AP(tensor=scratch_c.tensor, offset=0, ap=[[0, P], [1, H * SEQ]])
                           ).then_inc(s_cb, 16)
            pool.wait_ge(s_cb, 16)
            pool.wait_ge(s_cq, 1)
            cmask_h = cmask[:, :].unsqueeze(1).broadcast_to([P, 4, P])
            for h in range(0, H, 4):
                d0, d1 = decay0[:, h:h + 4, :], bias[:, h:h + 4, :]
                step(pool.tensor_tensor(d0, d1[:, :, 0:P], cmask_h, ALU.add))
                pool.tensor_tensor(d0, d0, cq[:, 0, h:h + 4].unsqueeze(2).broadcast_to([P, 4, P]), ALU.add)
                step(pool.tensor_tensor(d1, d1, cq[:, 1, h:h + 4].unsqueeze(2).broadcast_to([P, 4, SEQ]),
                                        ALU.add))
                pool.tensor_tensor(d1[:, :, P:SEQ], d1[:, :, P:SEQ], cmask_h, ALU.add).then_inc(s_decay, 1)
            split(U_FOX_OUT + 2)
            pool.wait_ge(s_on, 24)
            pool.dma_start(finalb, final_g.partition_broadcast(P)).then_inc(s_fg, 16)


_INS = ["x", "norm_g", "ffn_w_in", "ffn_w_out", "nsa_w_in", "nsa_cmp_pos", "nsa_cmp_w1", "nsa_cmp_w2",
        "nsa_w_out", "rel_bias", "kv_norm_g", "fox_w_kvf", "fox_b_f", "fox_w_q", "fox_w_out", "final_g"]


def kernel(**inputs):
    import concourse.bacc as bacc
    from concourse.bass_utils import run_bass_kernel_spmd

    nc = bacc.Bacc("TRN2", target_bir_lowering=False, num_devices=1)
    arrays, args = {}, []
    for name in _INS:
        a = np.ascontiguousarray(inputs[name])
        arrays[f"in_{name}"] = a
        args.append(nc.dram_tensor(f"in_{name}", a.shape, mybir.dt.from_np(a.dtype), kind="ExternalInput").ap())
    out = nc.dram_tensor("out", (1, SEQ, D), F32, kind="ExternalOutput").ap()
    yoco_trunk(nc, *args, out)
    r = run_bass_kernel_spmd(nc, [arrays], core_ids=[0])
    return r.results[0]["out"]
```
